# Optimizing a Trainium2 kernel written in Bass

```python
import math, functools
import jax, jax.numpy as jnp
from jax import lax
import numpy as np

D_MODEL = 1024
BATCH = 1
SEQ = 512
DEPTH = 1
DEC_BATCH = 8
DEC_SEQ = 4
PAST_LEN = 1024
PAGE_SIZE = 128

S5_WIDTH = D_MODEL // 2
S5_GROUP = 16
S5_GROUPS = S5_WIDTH // S5_GROUP
S5_STATE = 64
N_HEADS = 8
HEAD_DIM = 64
ATT_WIDTH = N_HEADS * HEAD_DIM
IDX_HEADS = 8
IDX_DIM = 32
TOPK_MAX = 256
Q_BLOCK = 128
N_BUCKETS = 32
MAX_DISTANCE = 128
D_FF = 2816
EPS = 1e-6
IN_SPLITS = (S5_WIDTH, ATT_WIDTH, ATT_WIDTH, ATT_WIDTH, IDX_HEADS * IDX_DIM, IDX_DIM, IDX_HEADS, D_MODEL, D_MODEL)
D_IN = sum(IN_SPLITS)

kernel_name = 'hybrid_s5_dsa_macaron_step'

def _rms_norm(x, g):
    xf = x.astype(jnp.float32)
    y = xf * lax.rsqrt(jnp.mean(xf * xf, axis=-1, keepdims=True) + EPS)
    return y.astype(x.dtype) * g

def _swiglu(x, w_in, w_out):
    gate, up = jnp.split(x @ w_in, 2, axis=-1)
    return (jax.nn.silu(gate) * up) @ w_out

def _t5_bucket(dist):
    max_exact = N_BUCKETS // 2
    nf = jnp.maximum(dist, 1).astype(jnp.float32)
    large = max_exact + (jnp.log(nf / max_exact) / math.log(MAX_DISTANCE / max_exact) * (N_BUCKETS - max_exact)).astype(jnp.int32)
    large = jnp.minimum(large, N_BUCKETS - 1)
    return jnp.where(dist < max_exact, dist, large)

def _gather_rows(a, idx):
    return jax.vmap(lambda ab, ib: ab[ib])(a, idx)

def _indexer_scores(qi, wi, kidx, qpos, kpos):
    logits = jnp.einsum('bqhd,bsd->bqhs', qi, kidx).astype(jnp.float32) * (IDX_DIM ** -0.5)
    score = jnp.einsum('bqhs,bqh->bqs', jax.nn.relu(logits), wi.astype(jnp.float32)) * (IDX_HEADS ** -0.5)
    causal = kpos[None, :] <= qpos[:, None]
    return jnp.where(causal[None], score, -jnp.inf)

def _sparse_attend(q, kg, vg, qpos, idx, rel_bias):
    valid = idx <= qpos[None, :, None]
    s = jnp.einsum('bqhd,bqkhd->bqhk', q, kg).astype(jnp.float32) * (HEAD_DIM ** -0.5)
    dist = jnp.maximum(qpos[None, :, None] - idx, 0)
    bias = rel_bias.astype(jnp.float32)[_t5_bucket(dist)]
    s = s + jnp.moveaxis(bias, -1, 2)
    s = jnp.where(valid[:, :, None, :], s, -jnp.inf)
    p = jax.nn.softmax(s, axis=-1).astype(vg.dtype)
    return jnp.einsum('bqhk,bqkhd->bqhd', p, vg)

def _prompt_attention(q, k, v, qi, ki, wi, rel_bias):
    b, L = q.shape[:2]
    topk = min(TOPK_MAX, L // 4)
    kpos = jnp.arange(L, dtype=jnp.int32)

    def block(i):
        start = i * Q_BLOCK
        sl = lambda a: lax.dynamic_slice_in_dim(a, start, Q_BLOCK, axis=1)
        qpos = start + jnp.arange(Q_BLOCK, dtype=jnp.int32)
        score = _indexer_scores(sl(qi), sl(wi), ki, qpos, kpos)
        _, idx = lax.top_k(score, topk)
        return _sparse_attend(sl(q), _gather_rows(k, idx), _gather_rows(v, idx), qpos, idx, rel_bias)

    out = lax.map(block, jnp.arange(L // Q_BLOCK, dtype=jnp.int32))
    return jnp.moveaxis(out, 0, 1).reshape(b, L, ATT_WIDTH)

def _sample_attention(q, k_new, v_new, qi, ki_new, wi, cache_k, cache_v, cache_kidx, page_table, rel_bias):
    db, ds = q.shape[:2]
    past = page_table.shape[1] * PAGE_SIZE
    L = past + ds
    topk = min(TOPK_MAX, L // 4)
    ki_past = cache_kidx[page_table].reshape(db, past, IDX_DIM).astype(ki_new.dtype)
    ki_all = jnp.concatenate([ki_past, ki_new], axis=1)
    qpos = past + jnp.arange(ds, dtype=jnp.int32)
    score = _indexer_scores(qi, wi, ki_all, qpos, jnp.arange(L, dtype=jnp.int32))
    _, idx = lax.top_k(score, topk)
    in_past = (idx < past)[..., None, None]
    pidx = jnp.minimum(idx, past - 1)
    phys = _gather_rows(page_table, pidx // PAGE_SIZE)
    off = pidx % PAGE_SIZE
    nidx = jnp.clip(idx - past, 0, ds - 1)
    kg = jnp.where(in_past, cache_k[phys, off].astype(k_new.dtype), _gather_rows(k_new, nidx))
    vg = jnp.where(in_past, cache_v[phys, off].astype(v_new.dtype), _gather_rows(v_new, nidx))
    return _sparse_attend(q, kg, vg, qpos, idx, rel_bias).reshape(db, ds, ATT_WIDTH)

def _s5_discretize(lam_re, lam_im, log_dt, b_re, b_im):
    f32 = jnp.float32
    lam_re, lam_im = lam_re.astype(f32), lam_im.astype(f32)
    dt = jnp.exp(log_dt.astype(f32))[:, None]
    mag = jnp.exp(lam_re * dt)
    a_re = mag * jnp.cos(lam_im * dt)
    a_im = mag * jnp.sin(lam_im * dt)
    den = lam_re * lam_re + lam_im * lam_im
    n_re = a_re - 1.0
    z_re = (n_re * lam_re + a_im * lam_im) / den
    z_im = (a_im * lam_re - n_re * lam_im) / den
    b_re, b_im = b_re.astype(f32), b_im.astype(f32)
    bb_re = z_re[..., None] * b_re - z_im[..., None] * b_im
    bb_im = z_re[..., None] * b_im + z_im[..., None] * b_re
    return a_re, a_im, bb_re, bb_im

def _s5_combine(e1, e2):
    a1r, a1i, b1r, b1i = e1
    a2r, a2i, b2r, b2i = e2
    return (a2r * a1r - a2i * a1i, a2r * a1i + a2i * a1r,
            a2r * b1r - a2i * b1i + b2r, a2r * b1i + a2i * b1r + b2i)

def _s5_branch(u, s0_re, s0_im, p):
    f32 = jnp.float32
    b, L = u.shape[:2]
    ug = u.astype(f32).reshape(b, L, S5_GROUPS, S5_GROUP)
    a_re, a_im, bb_re, bb_im = _s5_discretize(p['s5_lam_re'], p['s5_lam_im'], p['s5_log_dt'], p['s5_b_re'], p['s5_b_im'])
    bu_re = jnp.einsum('blgi,gpi->blgp', ug, bb_re)
    bu_im = jnp.einsum('blgi,gpi->blgp', ug, bb_im)
    s0_re, s0_im = s0_re.astype(f32), s0_im.astype(f32)
    bu_re = bu_re.at[:, 0].add(a_re * s0_re - a_im * s0_im)
    bu_im = bu_im.at[:, 0].add(a_re * s0_im + a_im * s0_re)
    ar = jnp.broadcast_to(a_re, bu_re.shape)
    ai = jnp.broadcast_to(a_im, bu_im.shape)
    _, _, s_re, s_im = lax.associative_scan(_s5_combine, (ar, ai, bu_re, bu_im), axis=1)
    c_re, c_im = p['s5_c_re'].astype(f32), p['s5_c_im'].astype(f32)
    y = (jnp.einsum('gip,blgp->blgi', c_re, s_re) - jnp.einsum('gip,blgp->blgi', c_im, s_im)
         + p['s5_d'].astype(f32).reshape(S5_GROUPS, S5_GROUP) * ug)
    g = jax.nn.gelu(y.reshape(b, L, S5_WIDTH)).astype(u.dtype)
    val, gate = jnp.split(g @ p['w_s5_glu'], 2, axis=-1)
    return val * jax.nn.sigmoid(gate), s_re[:, -1], s_im[:, -1]

def _mixer_proj(hn, w_in):
    b, L = hn.shape[:2]
    proj = hn @ w_in
    parts = []
    start = 0
    for n in IN_SPLITS:
        parts.append(proj[..., start:start + n])
        start += n
    u, q, k, v, qi, ki, wi, gs, ga = parts
    return (u, q.reshape(b, L, N_HEADS, HEAD_DIM), k.reshape(b, L, N_HEADS, HEAD_DIM),
            v.reshape(b, L, N_HEADS, HEAD_DIM), qi.reshape(b, L, IDX_HEADS, IDX_DIM), ki, wi, gs, ga)

def _layer(x, attn_fn, s0_re, s0_im, p):
    h = x + 0.5 * _swiglu(_rms_norm(x, p['g_ffn1']), p['w_ffn1_in'], p['w_ffn1_out'])
    hn = _rms_norm(h, p['g_mix'])
    u, q, k, v, qi, ki, wi, gs, ga = _mixer_proj(hn, p['w_in'])
    s5_y, s_re, s_im = _s5_branch(u, s0_re, s0_im, p)
    att = attn_fn(q, k, v, qi, ki, wi) @ p['w_att_proj']
    mixed = jax.nn.sigmoid(gs) * s5_y + jax.nn.sigmoid(ga) * att
    h = h + mixed @ p['w_out']
    h = h + 0.5 * _swiglu(_rms_norm(h, p['g_ffn2']), p['w_ffn2_in'], p['w_ffn2_out'])
    return h, k, v, ki, s_re, s_im

def setup_inputs(seed: int = 0) -> dict:
    key = jax.random.key(seed)
    k = jax.random.split(key, 32)
    f32 = jnp.float32
    nrm = lambda kk, shape, scale: scale * jax.random.normal(kk, shape, f32)
    n_pages = PAST_LEN // PAGE_SIZE
    n_used = DEC_BATCH * n_pages
    n_phys = n_used + max(1, n_used // 4)
    page_table = jax.random.permutation(k[0], n_phys)[:n_used].reshape(DEC_BATCH, n_pages).astype(jnp.int32)
    lam_im = math.pi * jnp.arange(S5_STATE, dtype=f32)[None, None, :] + nrm(k[10], (DEPTH, S5_GROUPS, S5_STATE), 0.01)
    return {
        'x_prompt': nrm(k[1], (BATCH, SEQ, D_MODEL), 1.0),
        'x_sample': nrm(k[2], (DEC_BATCH, DEC_SEQ, D_MODEL), 1.0),
        'cache_k': nrm(k[3], (DEPTH, n_phys, PAGE_SIZE, N_HEADS, HEAD_DIM), 1.0),
        'cache_v': nrm(k[4], (DEPTH, n_phys, PAGE_SIZE, N_HEADS, HEAD_DIM), 1.0),
        'cache_kidx': nrm(k[5], (DEPTH, n_phys, PAGE_SIZE, IDX_DIM), 1.0),
        'state_s5_re': nrm(k[6], (DEPTH, DEC_BATCH, S5_GROUPS, S5_STATE), 0.1),
        'state_s5_im': nrm(k[7], (DEPTH, DEC_BATCH, S5_GROUPS, S5_STATE), 0.1),
        'page_table': page_table,
        'g_ffn1': 1.0 + nrm(k[8], (DEPTH, D_MODEL), 0.05),
        'w_ffn1_in': nrm(k[11], (DEPTH, D_MODEL, 2 * D_FF), D_MODEL ** -0.5),
        'w_ffn1_out': nrm(k[12], (DEPTH, D_FF, D_MODEL), D_FF ** -0.5),
        'g_mix': 1.0 + nrm(k[13], (DEPTH, D_MODEL), 0.05),
        'w_in': nrm(k[14], (DEPTH, D_MODEL, D_IN), D_MODEL ** -0.5),
        's5_lam_re': -0.5 + nrm(k[9], (DEPTH, S5_GROUPS, S5_STATE), 0.01),
        's5_lam_im': lam_im,
        's5_log_dt': jax.random.uniform(k[15], (DEPTH, S5_GROUPS), f32, math.log(1e-3), math.log(1e-1)),
        's5_b_re': nrm(k[16], (DEPTH, S5_GROUPS, S5_STATE, S5_GROUP), S5_GROUP ** -0.5),
        's5_b_im': nrm(k[17], (DEPTH, S5_GROUPS, S5_STATE, S5_GROUP), S5_GROUP ** -0.5),
        's5_c_re': nrm(k[18], (DEPTH, S5_GROUPS, S5_GROUP, S5_STATE), S5_STATE ** -0.5),
        's5_c_im': nrm(k[19], (DEPTH, S5_GROUPS, S5_GROUP, S5_STATE), S5_STATE ** -0.5),
        's5_d': nrm(k[20], (DEPTH, S5_WIDTH), 1.0),
        'w_s5_glu': nrm(k[21], (DEPTH, S5_WIDTH, 2 * D_MODEL), S5_WIDTH ** -0.5),
        'w_att_proj': nrm(k[22], (DEPTH, ATT_WIDTH, D_MODEL), ATT_WIDTH ** -0.5),
        'rel_bias': nrm(k[23], (N_BUCKETS, N_HEADS), 0.5),
        'w_out': nrm(k[24], (DEPTH, D_MODEL, D_MODEL), D_MODEL ** -0.5),
        'g_ffn2': 1.0 + nrm(k[25], (DEPTH, D_MODEL), 0.05),
        'w_ffn2_in': nrm(k[26], (DEPTH, D_MODEL, 2 * D_FF), D_MODEL ** -0.5),
        'w_ffn2_out': nrm(k[27], (DEPTH, D_FF, D_MODEL), D_FF ** -0.5),
        'g_final': 1.0 + nrm(k[28], (D_MODEL,), 0.05),
    }

def reference(x_prompt, x_sample, cache_k, cache_v, cache_kidx, state_s5_re, state_s5_im, page_table,
              g_ffn1, w_ffn1_in, w_ffn1_out, g_mix, w_in, s5_lam_re, s5_lam_im, s5_log_dt,
              s5_b_re, s5_b_im, s5_c_re, s5_c_im, s5_d, w_s5_glu, w_att_proj, rel_bias, w_out,
              g_ffn2, w_ffn2_in, w_ffn2_out, g_final):
    hp, hs = x_prompt, x_sample
    new_p, new_s = [], []
    for l in range(DEPTH):
        p = dict(g_ffn1=g_ffn1[l], w_ffn1_in=w_ffn1_in[l], w_ffn1_out=w_ffn1_out[l], g_mix=g_mix[l],
                 w_in=w_in[l], s5_lam_re=s5_lam_re[l], s5_lam_im=s5_lam_im[l], s5_log_dt=s5_log_dt[l],
                 s5_b_re=s5_b_re[l], s5_b_im=s5_b_im[l], s5_c_re=s5_c_re[l], s5_c_im=s5_c_im[l],
                 s5_d=s5_d[l], w_s5_glu=w_s5_glu[l], w_att_proj=w_att_proj[l], w_out=w_out[l],
                 g_ffn2=g_ffn2[l], w_ffn2_in=w_ffn2_in[l], w_ffn2_out=w_ffn2_out[l])
        prompt_attn = functools.partial(_prompt_attention, rel_bias=rel_bias)
        sample_attn = functools.partial(_sample_attention, cache_k=cache_k[l], cache_v=cache_v[l],
                                        cache_kidx=cache_kidx[l], page_table=page_table, rel_bias=rel_bias)
        zeros = jnp.zeros((hp.shape[0], S5_GROUPS, S5_STATE), jnp.float32)
        hp, kp, vp, kip, srp, sip = _layer(hp, prompt_attn, zeros, zeros, p)
        hs, ks, vs, kis, srs, sis = _layer(hs, sample_attn, state_s5_re[l], state_s5_im[l], p)
        new_p.append((kp, vp, kip, srp, sip))
        new_s.append((ks, vs, kis, srs, sis))
    k_prompt, v_prompt, kidx_prompt, s5_re_prompt, s5_im_prompt = [jnp.stack(t) for t in zip(*new_p)]
    k_sample, v_sample, kidx_sample, s5_re_sample, s5_im_sample = [jnp.stack(t) for t in zip(*new_s)]
    y_prompt = _rms_norm(hp, g_final)
    y_sample = _rms_norm(hs, g_final)
    return (y_prompt, y_sample, k_prompt, v_prompt, kidx_prompt, s5_re_prompt, s5_im_prompt,
            k_sample, v_sample, kidx_sample, s5_re_sample, s5_im_sample)


_drawn_inputs = setup_inputs


def setup_inputs(seed=0):
    import zlib

    import numpy as np

    out = dict(_drawn_inputs(seed))
    spreads = {}
    factors = {'s5_lam_re': 4.047, 's5_c_re': 3.16, 's5_c_im': 3.264, 'g_ffn2': 2.886}
    for name, (base, spread) in spreads.items():
        noise = np.random.default_rng([zlib.crc32(name.encode()), seed]).standard_normal(out[name].shape)
        drawn = base * np.exp(spread * noise) if base else spread * noise
        out[name] = __import__('jax').numpy.asarray(drawn.astype(out[name].dtype))
    for name, factor in factors.items():
        out[name] = (out[name] * factor).astype(out[name].dtype)
    return out
```

```python
from contextlib import ExitStack
import math

import numpy as np
import concourse.bass as bass
from concourse import mybir

F32 = mybir.dt.float32
BF16 = mybir.dt.bfloat16
I32 = mybir.dt.int32
ALU = mybir.AluOpType
ACT = mybir.ActivationFunctionType
AX = mybir.AxisListType

P = 128
D = 1024
DK = D // P
SEQ, NB, NS = 512, 8, 4
NT = SEQ + NB * NS
HALF = NT // 2
FF = 2816
FK = FF // P
HEADS, HD = 8, 64
IH, ID = 8, 32
TOPK_P, TOPK_S = SEQ // 4, 256
PAST, PAGE = 1024, 128
NPAGE = PAST // PAGE
NKEY = PAST + NB * NS
G, GC, ST = 32, 16, 64
GP = G // 2
CH = 8
NC = SEQ // CH
UC = NC + NB
NBKT = 32
EPS = 1e-6
MASK = -1e30
TAKEN = -3e38
C_U, C_Q, C_K, C_V, C_QI = 0, 512, 1024, 1536, 2048
NQI = IH * ID + ID + IH
C_GS, C_GA = C_QI + NQI, C_QI + NQI + D


def bucket(dist):
    d = np.maximum(dist, 0)
    nf = np.maximum(d, 1).astype(np.float32)
    large = 16 + (np.log(nf / np.float32(16)) / np.float32(math.log(8.0)) * np.float32(16) + np.float32(1e-5)).astype(np.int32)
    return np.where(d < 16, d, np.minimum(large, NBKT - 1))


def shape_constants():
    c = {}
    c["ident"] = np.eye(P, dtype=np.float32)
    y = np.arange(640)
    c["oh_prompt"] = (bucket(511 - y)[None, :] == np.arange(NBKT)[:, None]).astype(np.float32)
    s = np.arange(PAST)
    oh = np.zeros((NS, NBKT, NKEY), np.float32)
    for q in range(NS):
        oh[q, bucket(PAST + q - s), s] = 1
        oh[q, bucket(q - np.arange(NB * NS) % NS), PAST + np.arange(NB * NS)] = 1
    c["oh_sample"] = oh.reshape(P, NKEY)
    q_of = np.arange(P) % NS
    c["same_step"] = (np.repeat(np.arange(NS), NBKT)[:, None] == q_of[None, :]).astype(np.float32)
    row_b, row_h = np.arange(P) // 32, np.arange(P) // NS % HEADS
    tok = np.arange(NB * NS)
    for g in range(2):
        c[f"row_tok{g}"] = ((row_b + 4 * g)[:, None] * NS + q_of[:, None] == tok[None, :]).astype(np.float32)
        c[f"tok_row{g}"] = np.ascontiguousarray(c[f"row_tok{g}"].T)
    c["row_head"] = (row_h[:, None] == np.arange(HEADS)[None, :]).astype(np.float32)
    c["head_row"] = np.ascontiguousarray(c["row_head"].T)
    c["causal"] = np.where(np.arange(P)[None, :] <= np.arange(P)[:, None], 0, MASK).astype(np.float32)
    ok = (tok[:, None] // NS == tok[None, :] // NS) & (tok[None, :] <= tok[:, None])
    c["new_mask"] = np.where(ok, 0, MASK).astype(np.float32)
    return c


def build(nc, t, out):
    ctx = ExitStack()
    with ctx:
        def sb(name, shape, dt=F32):
            return ctx.enter_context(nc.sbuf_tensor(name, shape, dt))

        def sem(name):
            return ctx.enter_context(nc.semaphore(name))

        def one(ap3, i):
            return ap3[:, bass.ds(i, 1), :].rearrange("p a n -> p (a n)")

        hT = sb("hT", [P, DK, NT])
        hn = sb("hn", [P, DK, NT])
        wslot = sb("wslot", [P, 2, FK * P])
        big = sb("big", [P, FK * NT])
        biasmem = sb("biasmem", [P, HEADS * SEQ + NKEY])
        kvtok = sb("kvtok", [P, 2, 5, 512])
        qkT = sb("qkT", [P, 2, 4, NT])
        qiT = sb("qiT", [P, 2, SEQ])
        kiT = sb("kiT", [P, NT])
        uv = sb("uv", [P, 2, G * UC])
        sg = sb("sg", [P, 2, NT])
        rstd = sb("rstd", [P, NT])
        ki4 = sb("ki4", [P, 5, 4, ID])
        qis = sb("qis", [P, NB, IH, NS])
        qbd = sb("qbd", [P, 4, NB, HEADS * NS])
        ident = sb("ident_sb", [P, P])
        identb = sb("identb", [P, P], BF16)
        causb = sb("causb", [P, P], BF16)
        caus = sb("caus", [P, P])
        ones = sb("ones", [P, P])
        gains = sb("gains", [P, 4, DK])
        epsc = sb("epsc", [P, 1])
        wtok = sb("wtok", [P, 4, IH])
        s0 = sb("s0", [P, 2, NB, GP])
        apow = sb("apow", [P, 9, 2, GP])
        cpow = sb("cpow", [P, 9, 2, GP])
        dch = sb("dch", [P, G])
        tiny = sb("tiny", [P, 64])
        pt_sb = sb("pt_sb", [1, NB * NPAGE], I32)
        ps = ctx.enter_context(nc.psum_tensor("ps", [P, 8, 512], F32))

        act = big[:, :].rearrange("p (f n) -> p f n", f=FK)
        tb = biasmem[:, 0:HEADS * SEQ].rearrange("p (h n) -> p h n", h=HEADS)
        bs = biasmem[:, HEADS * SEQ:]
        ktok, vtok = kvtok[:, 0], kvtok[:, 1]
        qT, kT = qkT[:, 0], qkT[:, 1]
        xtok = big[:, 0:5 * D].rearrange("p (t d) -> p t d", t=5)
        yre = biasmem[:, 0:2304].rearrange("p (g k i) -> p g k i", g=GP, k=9)
        yim = biasmem[:, 2304:4608].rearrange("p (g k i) -> p g k i", g=GP, k=9)
        wb = kvtok[:, :, :, :].rearrange("p a b c -> p (a b c)")[:, 0:4096].rearrange(
            "p (c g t j) -> p c g t j", c=2, g=GP, t=CH)
        toep = big[:, 0:4096].rearrange("p (g n) -> p g n", g=G)
        gb = big[:, 4096:8192].rearrange("p (c g n) -> p c g n", c=2, g=GP)
        ych = big[:, 4096:4096 + G * UC].rearrange("p (g c) -> p g c", g=G)
        kbuf = big[:, 8192:10240].rearrange("p (b g n) -> p b g n", b=2, g=8)
        udb = big[:, 8192:8192 + G * UC].rearrange("p (g c) -> p g c", g=G)
        uch = uv[:, 0].rearrange("p (g c) -> p g c", g=G)
        vst = uv[:, 1].rearrange("p (c g n) -> p c g n", c=2, g=GP)
        uT = uv[:, 1, 0:4 * NT].rearrange("p (t n) -> p t n", t=4)
        yT = uv[:, 1, 0:4 * NT].rearrange("p (t n) -> p t n", t=4)
        gT = uv[:, 0, 0:4 * NT].rearrange("p (t n) -> p t n", t=4)
        early = qkT[:, :, :, :].rearrange("p a b c -> p (a b c)")
        lam = early[:, 0:32].rearrange("p (c g) -> p c g", c=2)
        ldt = early[:, 32:48]
        s5v = early[:, 48:48 + 16 * 20].rearrange("p (k g) -> p k g", k=20)
        bmat = early[:, 512:1024].rearrange("p (c g j) -> p c g j", c=2, g=GP)
        bbar = early[:, 1024:1536].rearrange("p (c g j) -> p c g j", c=2, g=GP)
        craw = early[:, 1536:2560].rearrange("p (c t n) -> p c t n", c=2, t=4)
        cT = early[:, 2560:3072].rearrange("p (c g i) -> p c g i", c=2, g=GP)
        s0raw = early[:, 3072:3328].rearrange("p (c n) -> p c n", c=2)
        draw = early[0:G, 3328:3456].rearrange("p (t i) -> p t i", t=CH)
        pt1 = early[:, 3456:3712].rearrange("p (g j) -> p g j", g=GP)
        pt2 = early[:, 3712:3968].rearrange("p (g j) -> p g j", g=GP)
        pt3 = uv[:, 0, 0:256].rearrange("p (g j) -> p g j", g=GP)
        pt4 = uv[:, 0, 256:512].rearrange("p (g j) -> p g j", g=GP)
        fin_s = sg[:, 0, 0:256].rearrange("p (c b g) -> p c b g", c=2, b=NB)
        fin_p = sg[:, 0, 256:288].rearrange("p (c g) -> p c g", c=2)
        fin_t = rstd[:, 0:512]
        prod = sg[:, 1, 0:512]
        ohp = big[:, 5120:5760]
        relb = tiny[0:NBKT, 0:HEADS]
        relrep = big[:, 5760:6784].rearrange("p (h n) -> p h n", h=HEADS)
        shrow = big[:, 6784:6784 + 1280].rearrange("p (b n) -> p b n", b=2)
        nmx = tiny[:, 8:10]
        rsum = tiny[:, 16:32].rearrange("p (a h) -> p a h", a=2)
        rinv = tiny[:, 32:48].rearrange("p (a h) -> p a h", a=2)
        top8 = tiny[:, 48:56]
        topwait = tiny[:, 56:57]
        s5q = uv[:, 1, 0:256].rearrange("p (k m g) -> p k m g", k=4, m=4)
        prodmem = big[:, 4096:8192]

        def v(k):
            return s5v[:, k, :]

        mixed = big[:, 0:DK * NT].rearrange("p (m n) -> p m n", m=DK)
        base = DK * NT
        sc = big[:, base:base + 512]
        rl = big[:, base + 512:base + 1536].rearrange("p (b n) -> p b n", b=2)
        selb = big[:, base + 1536:base + 2560].bitcast(BF16).rearrange("p (q n) -> p q n", q=4)
        smx = big[:, base + 2560:base + 3584].rearrange("p (b n) -> p b n", b=2)
        pexp = big[:, base + 3584:base + 4608].rearrange("p (b n) -> p b n", b=2)
        pT = big[:, base + 4608:base + 5632].rearrange("p (b n) -> p b n", b=2)
        ao = big[:, base + 5632:base + 6656].rearrange("p (b n) -> p b n", b=2)
        attT = kvtok[:, 0, :, :].rearrange("p a b -> p (a b)")[:, 0:4 * NT].rearrange("p (j n) -> p j n", j=4)
        kring = big[:, base:base + 2048].rearrange("p (r n) -> p r n", r=4)
        kidx = big[:, base:base + 2048].rearrange("p (n d) -> p n d", d=ID)
        kxT = big[:, base + 2048:base + 2560].rearrange("p (b n) -> p b n", b=2)
        rls = big[:, base + 2560:base + 2560 + NKEY]
        scs = big[0:32, base + 3616:base + 3616 + NKEY]
        sels = big[0:32, base + 4672:base + 4672 + NKEY // 2].bitcast(BF16)
        ohs = big[:, base + 5200:base + 5200 + NKEY]
        sms = big[:, base + 2560:base + 2560 + NKEY]
        pes = big[:, base + 3616:base + 3616 + NKEY]
        ptS = big[:, base + 5200:base + 5200 + 9 * P].rearrange("p (k n) -> p k n", k=9)
        pgT = big[:, base + 6352:base + 7376].rearrange("p (b n) -> p b n", b=2)
        osel = sg[:, :, 0:512]
        qis4 = sg[0:32, :, :].rearrange("p a b -> p (a b)")[:, 0:IH * 4 * ID].rearrange("p (h r d) -> p h r d", h=IH, r=4)
        row_tok = rstd[:, 0:64].rearrange("p (g n) -> p g n", g=2)
        row_head = rstd[:, 64:72]
        head_row = rstd[0:8, 72:200]
        wT8 = rstd[0:8, 512:544]
        wsel = rstd[:, 232:296].rearrange("p (g n) -> p g n", g=2)
        new_mask = rstd[0:32, 296:328]
        tok_row = rstd[0:32, 328:456].bitcast(BF16).rearrange("p (g n) -> p g n", g=2)
        rb4 = rstd[:, 456:464]
        hmr = rstd[:, 464:480].rearrange("p (g h) -> p g h", g=2)
        same_step = sg[:, 0, 0:128]
        rbexp = sg[:, 0, 128:256]
        tok_row_f = sg[0:32, 1, 0:256].rearrange("p (g n) -> p g n", g=2)
        ytok = big[:, 0:5 * D].rearrange("p (t d) -> p t d", t=5)

        scr_shift = nc.dram_tensor("scr_shift", [HEADS, P, 640], F32, kind="Internal").ap()
        scr_u = nc.dram_tensor("scr_u", [CH, GC, 4, 8, NC], F32, kind="Internal").ap()
        scr_us = nc.dram_tensor("scr_us", [NS, GC, 4, 8, NB], F32, kind="Internal").ap()
        scr_y = nc.dram_tensor("scr_y", [G, GC, CH, NC], F32, kind="Internal").ap()
        scr_ys = nc.dram_tensor("scr_ys", [G, GC, NS, NB], F32, kind="Internal").ap()

        s = {n: sem(n) for n in (
            "x_in", "const_in", "par_in", "x_turned", "oh_in", "shift_mm",  "relrep",
            "pool_const", "early_pe", "early_act", "dt_done", "ang_done", "trig_done", "pow_done", "mm_done", "evac",
            "gate_done", "sq_done", "ssum_done", "sqrt_done", "norm_done", "dve_step", "pool_step", "bf_done",
            "prep_done", "gbt", "gb_ev", "km", "k_ev", "tz_zero", "u_zero", "u_out", "u_in", "ud_done", "kt_t", "kt_ev",
            "vmm", "v_ev", "scan_done", "ymm", "y_ev", "y_out", "y_in", "fin_ready", "fin_mm", "fin_ev", "gelu_done",
            "bias_in", "res_out", "ix_mm", "ix_relu", "ix_acc", "topk", "sel_done", "at_s", "at_sm", "at_exp", "at_t",
            "at_tc", "at_pv", "at_o", "at_ot", "at_otc", "sc_in", "sm_prep", "sm_pe", "sm_b", "kidx_in", "sx_t", "sx_tc",
            "sx_mm", "sx_relu", "sx_w", "sx_sel", "kv_used", "kp_t", "kp_tc", "kp_s", "ss_mm", "ss_sm", "ss_exp", "sp_t",
            "sp_tc", "sv_mm", "sv_o", "so_mm", "so_ev", "att_gated", "yt_t", "yt_ev")}
        s["shift_out"] = [sem(f"shift_out{i}") for i in range(2)]
        s["toep_in"] = [sem(f"toep_in{i}") for i in range(2)]
        w_ready = [sem(f"w_ready{i}") for i in range(2)]
        kv_in = [sem(f"kv_in{i}") for i in range(4)]

        LAYERS = [("ffn1_in", 22, 2), ("ffn1_out", 8, 1), ("uq", 8, 1), ("kv", 4, 1), ("idx", 1, 1),
                  ("glu", 8, 2), ("gs", 8, 1), ("ga_att", 8, 2), ("out", 8, 1), ("ffn2_in", 22, 2), ("ffn2_out", 8, 1)]
        first_tile, slot_base, n_, sl_ = {}, {}, 0, [0, 0]
        for name, cnt, d_ in LAYERS:
            first_tile[name], slot_base[name] = n_, list(sl_)
            for k_ in range(cnt):
                sl_[(n_ + k_) % 2] += 16 * d_
            n_ += cnt
        EV0 = DK

        def tiles(eng, name, body):
            n0, (_, cnt, d) = first_tile[name], next(l for l in LAYERS if l[0] == name)
            def step(i2, j, i):
                slot = (n0 + j) % 2
                body(i, slot, i + n0, slot_base[name][slot] + (i2 + 1) * (16 * d))
            if cnt > 2:
                with eng.Fori(0, cnt // 2) as r:
                    for j in range(2):
                        step(r, j, r * 2 + j)
            else:
                for i in range(cnt):
                    step(i // 2, i % 2, i)

        def slot_half(layer, slot):
            return slot

        ctx.enter_context(nc.allow_non_contiguous_dma(reason="small parameters"))
        block = ctx.enter_context(nc.Block())


        MM0 = DK
        ALLT = n_

        @block.sync
        def _(sp):
            sp.dma_start(xtok[:, 0:4, :], t["x_prompt"][0].rearrange("(t p) d -> p t d", p=P)).then_inc(s["x_in"], 16)
            sp.dma_start(xtok[0:32, 4, :], t["x_sample"].rearrange("b s d -> (b s) d")).then_inc(s["x_in"], 16)
            sp.dma_start(ident[:], t["ident"]).then_inc(s["const_in"], 16)
            sp.dma_start(caus[:], t["causal"]).then_inc(s["const_in"], 16)
            for k, n in enumerate(("g_ffn1", "g_mix", "g_ffn2", "g_final")):
                src = t[n] if n == "g_final" else t[n][0]
                sp.dma_start(gains[:, k, :], src.rearrange("(k p) -> p k", p=P)).then_inc(s["const_in"], 16)
            sp.dma_start(pt_sb[:], t["page_table"].rearrange("b (o n) -> o (b n)", o=1)).then_inc(s["const_in"], 16)
            for c, n in enumerate(("s5_lam_re", "s5_lam_im")):
                sp.dma_start(lam[:, c, :], t[n][0].rearrange("(g s) p -> (s p) g", s=2)).then_inc(s["par_in"], 16)
            for h in range(2):
                sp.dma_start(ldt[64 * h:64 * h + 64, :], t["s5_log_dt"][0].rearrange("(g s) -> s g", s=2)[h:h + 1, :]
                             .broadcast_to([64, GP])).then_inc(s["par_in"], 16)
            for c, n in enumerate(("s5_b_re", "s5_b_im")):
                sp.dma_start(bmat[:, c, :, :], t[n][0].rearrange("(g s) p j -> (s p) g j", s=2)).then_inc(s["par_in"], 16)
            for c, n in enumerate(("s5_c_re", "s5_c_im")):
                for h in range(2):
                    sp.dma_start(craw[:, c, :, 64 * h:64 * h + 64],
                                 t[n][0].rearrange("g i p -> (g i) p").rearrange("(t q) p -> q t p", q=P)).then_inc(s["par_in"], 16)
            for c, n in enumerate(("state_s5_re", "state_s5_im")):
                sp.dma_start(s0raw[:, c, :], t[n][0].rearrange("b (g s) p -> (b g) (s p)", s=2)).then_inc(s["par_in"], 16)
            for k in range(CH):
                sp.dma_start(draw[:, k, :], t["s5_d"][0].rearrange("(g i) -> g i", i=GC)).then_inc(s["par_in"], 16)

            def load(layer, *parts):
                def body(i, slot, n, ready):
                    sp.wait_ge(s["mm_done"], n + (MM0 - 1))
                    for at, w, c0, width in parts:
                        kb = w.shape[1]
                        dst = wslot[:, slot, at * P:at * P + kb * width].rearrange("p (k n) -> p k n", k=kb)
                        sp.dma_start(dst, w[:, :, bass.ds(i * width + c0, width)]).then_inc(w_ready[slot], 16)
                tiles(sp, layer, body)

            rows = lambda n: t[n][0].rearrange("(k p) n -> p k n", p=P)
            sp.wait_ge(s["x_turned"], 1)
            sp.dma_start(ohp[0:NBKT, :], t["oh_prompt"]).then_inc(s["oh_in"], 16)
            sp.dma_start(relb, t["rel_bias"]).then_inc(s["oh_in"], 16)
            for h in range(HEADS):
                sp.wait_ge(s["early_act"], 4 + h)
                sp.dma_start(scr_shift[h], shrow[:, h % 2, :]).then_inc(s["shift_out"][h % 2], 16)
            load("ffn1_in", (0, rows("w_ffn1_in"), 0, P), (DK, rows("w_ffn1_in"), FF, P))
            load("ffn1_out", (0, rows("w_ffn1_out"), 0, P))
            sp.wait_ge(s["tz_zero"], 1)
            for r in range(4):
                sp.wait_ge(s["k_ev"], r + 1)
                for k in range(CH):
                    sp.dma_start(toep[16 * k:16 * k + 16, 8 * r:8 * r + 8, 16 * k:P],
                                 kbuf[0:16, r % 2, :, 0:P - 16 * k]).then_inc(s["toep_in"][r % 2], 16)
            load("uq", (0, rows("w_in"), C_U, P))
            load("kv", (0, rows("w_in"), C_K, 256))
            load("idx", (0, rows("w_in"), C_QI, NQI))
            sp.wait_ge(s["evac"], EV0 + first_tile["uq"] + 4)
            for k in range(4):
                for gl in range(8):
                    sl = slice(16 * gl, 16 * gl + 16)
                    sp.dma_start(scr_u[:, :, k, gl, :].rearrange("t c n -> c t n"),
                                 uT[sl, k, 0:SEQ].rearrange("c (t n) -> c t n", t=CH)).then_inc(s["u_out"], 16)
                    sp.dma_start(scr_us[:, :, k, gl, :].rearrange("t c n -> c t n"),
                                 uT[sl, k, SEQ:NT].rearrange("c (t n) -> c t n", t=NS)).then_inc(s["u_out"], 16)
            sp.wait_ge(s["u_out"], 16 * 64)
            sp.wait_ge(s["u_zero"], 1)
            sp.dma_start(uch[:, :, 0:NC], scr_u.rearrange("t c k g n -> (t c) (k g) n")).then_inc(s["u_in"], 16)
            sp.dma_start(uch[64:128, :, NC:UC], scr_us.rearrange("t c k g n -> (t c) (k g) n")).then_inc(s["u_in"], 16)
            sp.wait_ge(s["evac"], EV0 + first_tile["idx"] + 1)
            for a, n in ((ktok, "k"), (vtok, "v")):
                sp.dma_start(out[n + "_prompt"][0, 0].rearrange("(t p) h d -> p t (h d)", p=P), a[:, 0:4, :]).then_inc(s["res_out"], 16)
                sp.dma_start(out[n + "_sample"][0].rearrange("b s h d -> (b s) (h d)"), a[0:32, 4, :]).then_inc(s["res_out"], 16)
            sp.dma_start(out["kidx_prompt"][0, 0].rearrange("(t p) d -> p t d", p=P), ki4[:, 0:4, 0, :]).then_inc(s["res_out"], 16)
            sp.dma_start(out["kidx_sample"][0].rearrange("b s d -> (b s) d"), ki4[0:32, 4, 0, :]).then_inc(s["res_out"], 16)
            sp.wait_ge(s["y_ev"], 8)
            for k in range(CH):
                sp.dma_start(scr_y[:, :, k, :].rearrange("g i n -> i g n"), ych[16 * k:16 * k + 16, :, 0:NC]).then_inc(s["y_out"], 16)
            for k in range(NS):
                sp.dma_start(scr_ys[:, :, k, :].rearrange("g i n -> i g n"), ych[64 + 16 * k:80 + 16 * k, :, NC:UC]).then_inc(s["y_out"], 16)
            sp.wait_ge(s["y_out"], 16 * 12)
            sp.dma_start(yT[:, :, 0:SEQ], scr_y.rearrange("g i k n -> (g i) (k n)").rearrange("(t q) n -> q t n", q=P)).then_inc(s["y_in"], 16)
            sp.dma_start(yT[:, :, SEQ:NT], scr_ys.rearrange("g i k n -> (g i) (k n)").rearrange("(t q) n -> q t n", q=P)).then_inc(s["y_in"], 16)
            sp.wait_ge(s["fin_ev"], 1)
            for c, n in enumerate(("s5_re", "s5_im")):
                sp.dma_start(out[n + "_sample"][0].rearrange("b (g s) p -> (b g) (s p)", s=2), fin_t[:, P * c:P * c + P]).then_inc(s["res_out"], 16)
                sp.dma_start(out[n + "_prompt"][0, 0].rearrange("(g s) p -> g (s p)", s=2),
                             fin_t[0:GP, 256 + P * c:384 + P * c]).then_inc(s["res_out"], 16)
            for k in range(2):
                sp.wait_ge(s["shift_out"][k], 16 * HEADS // 2)
            for h in range(HEADS):
                row = scr_shift[h].rearrange("p n -> (p n)")[127:127 + 639 * P].rearrange("(p n) -> p n", n=639)[:, 0:SEQ]
                sp.dma_start(tb[:, h, :], row).then_inc(s["bias_in"], 16)
            sp.wait_ge(s["res_out"], 16 * 10)
            for g in range(2):
                sp.dma_start(row_tok[:, g, :], t[f"row_tok{g}"]).then_inc(s["sc_in"], 16)
                sp.dma_start(tok_row_f[:, g, :], t[f"tok_row{g}"]).then_inc(s["sc_in"], 16)
            sp.dma_start(row_head, t["row_head"]).then_inc(s["sc_in"], 16)
            sp.dma_start(head_row, t["head_row"]).then_inc(s["sc_in"], 16)
            sp.dma_start(new_mask, t["new_mask"]).then_inc(s["sc_in"], 16)
            sp.dma_start(same_step, t["same_step"]).then_inc(s["sc_in"], 16)
            for q in range(NS):
                sp.dma_start(rb4[32 * q:32 * q + 32, :], t["rel_bias"]).then_inc(s["sc_in"], 16)
            sp.wait_ge(s["at_otc"], 4)
            sp.dma_start(ohs, t["oh_sample"]).then_inc(s["oh_in"], 16)
            sp.wait_ge(s["const_in"], 16 * 7)
            with sp.Fori(0, NB * NPAGE) as i:
                pg = sp.value_load(pt_sb[0:1, bass.ds(i, 1)], min_val=0, max_val=t["cache_kidx"].shape[1] - 1)
                sp.dma_start(one(kidx, i), t["cache_kidx"][0][bass.ds(pg, 1), :, :].rearrange("a p d -> p (a d)")).then_inc(s["kidx_in"], 16)
            for g in range(2):
                for c, n in enumerate(("cache_k", "cache_v")):
                    src = t[n][0].rearrange("n p h d -> n p (h d)")
                    with sp.Fori(0, 8) as i:
                        for r in range(4):
                            sp.wait_ge(s["kv_used"], i * 4 + (64 * g + 32 * c + r + 1))
                            pg = sp.value_load(pt_sb[0:1, bass.ds(i * 4 + (32 * g + r), 1)], min_val=0, max_val=src.shape[0] - 1)
                            sp.dma_start(kring[:, r, :], src[bass.ds(pg, 1), :, :].rearrange("a p d -> p (a d)")).then_inc(kv_in[r], 16)
            load("glu", (0, rows("w_s5_glu"), 0, P), (4, rows("w_s5_glu"), D, P))
            load("gs", (0, rows("w_in"), C_GS, P))
            load("ga_att", (0, rows("w_in"), C_GA, P), (DK, rows("w_att_proj"), 0, P))
            load("out", (0, rows("w_out"), 0, P))
            load("ffn2_in", (0, rows("w_ffn2_in"), 0, P), (DK, rows("w_ffn2_in"), FF, P))
            load("ffn2_out", (0, rows("w_ffn2_out"), 0, P))
            for k in range(5):
                sp.wait_ge(s["yt_ev"], k + 1)
                if k < 4:
                    sp.dma_start(out["y_prompt"][0, P * k:P * k + P, :], ytok[:, k, :]).then_inc(s["res_out"], 16)
                else:
                    sp.dma_start(out["y_sample"].rearrange("b s d -> (b s) d"), ytok[0:32, 4, :]).then_inc(s["res_out"], 16)
            sp.wait_ge(s["res_out"], 16 * (6 + 4 + 5))

        @block.tensor
        def _(pe):
            def acc(dst, pairs, last_sem=None, **kw):
                for k, (a, b) in enumerate(pairs):
                    ins = pe.matmul(dst, a, b, start=(k == 0), stop=(k == len(pairs) - 1), **kw)
                return ins

            def slot_block(slot, k, m=P):
                return wslot[:, slot, k * P:k * P + m]

            def norm_sum(k):
                pe.wait_ge(s["evac"], EV0 + {0: 0, 1: first_tile["uq"], 2: first_tile["ffn2_in"], 3: ALLT}[k])
                for j in range(DK):
                    pe.wait_ge(s["sq_done"], DK * k + j + 1)
                    for h in range(2):
                        ins = pe.matmul(ps[:, h, 0:HALF], ones[:], hn[:, j, h * HALF:(h + 1) * HALF],
                                        start=(j == 0), stop=(j == DK - 1), skip_group_check=True)
                ins.then_inc(s["ssum_done"], 1)

            def linear(layer, outs):
                def body(i, slot, n, ready):
                    half = slot_half(layer, slot)
                    pe.wait_ge(w_ready[slot], ready)
                    pe.wait_ge(s["evac"], n + (EV0 - 1))
                    for o, (k0, kb, x) in enumerate(outs):
                        for h in range(2):
                            ins = acc(ps[:, half * 4 + 2 * o + h, 0:HALF],
                                      [(slot_block(slot, k0 + k), x[:, k, h * HALF:(h + 1) * HALF]) for k in range(kb)])
                    ins.then_inc(s["mm_done"], 1)
                tiles(pe, layer, body)

            pe.wait_ge(s["x_in"], 32)
            pe.wait_ge(s["const_in"], 16 * 7)
            for k in range(DK):
                if k >= 2:
                    pe.wait_ge(s["evac"], k - 1)
                b = 4 * (k % 2)
                for j in range(4):
                    pe.transpose(ps[:, b, P * j:P * j + P], xtok[:, j, P * k:P * k + P], ident[:])
                pe.transpose(ps[:, b + 1, 0:32], xtok[0:32, 4, P * k:P * k + P], ident[0:32, 0:32]).then_inc(s["mm_done"], 1)
            pe.wait_ge(s["pool_const"], 1)
            norm_sum(0)
            pe.wait_ge(s["par_in"], 16 * 20)
            for c in range(2):
                for k in range(4):
                    pe.transpose(ps[:, 2 + c, P * k:P * k + P], craw[:, c, k, :], ident[:])
            for c in range(2):
                pe.transpose(ps[:, 4, P * c:P * c + P], s0raw[:, c, :], ident[:])
            pe.transpose(ps[:, 4, 256:288], draw.rearrange("g t i -> g (t i)"), ident[0:G, 0:G]).then_inc(s["early_pe"], 1)
            pe.wait_ge(s["relrep"], 1)
            pe.wait_ge(s["oh_in"], 32)
            for h in range(HEADS):
                pe.wait_ge(s["early_act"], 3 + h)
                for k in range(2):
                    ins = pe.matmul(ps[:, 6 + k, 0:320], relrep[0:NBKT, h, :], ohp[0:NBKT, 320 * k:320 * k + 320], start=True, stop=True)
                ins.then_inc(s["shift_mm"], 1)
            pe.wait_ge(s["early_act"], 3 + HEADS)
            pe.wait_ge(s["norm_done"], DK)
            linear("ffn1_in", [(0, DK, hn), (DK, DK, hn)])
            pe.wait_ge(s["evac"], EV0 + 22)
            linear("ffn1_out", [(0, FK, act)])
            pe.wait_ge(s["evac"], EV0 + 30)
            pe.wait_ge(s["prep_done"], 1)
            for r in range(8):
                c, g4 = r // 4, r % 4
                for q in range(4):
                    ins = pe.transpose(ps[:, r, P * q:P * q + P], wb[:, c, 4 * g4 + q, :, :].rearrange("p t j -> p (t j)"), ident[:])
                ins.then_inc(s["gbt"], 1)
            for r in range(4):
                pe.wait_ge(s["gb_ev"], 2 * (r % 2) + 2)
                if r >= 2:
                    pe.wait_ge(s["k_ev"], r - 1)
                for q in range(4):
                    gp = 4 * r + q
                    for h in range(2):
                        sl = slice(64 * h, 64 * h + 64)
                        ins = acc(ps[0:16, 2 * (r % 2) + h, P * q:P * q + P],
                                  [(bbar[sl, 0, gp, :], yre[sl, gp, 0:CH, :]), (bbar[sl, 1, gp, :], yim[sl, gp, 0:CH, :])])
                ins.then_inc(s["km"], 1)
            pe.wait_ge(s["gb_ev"], 8)
            pe.wait_ge(s["k_ev"], 4)
            norm_sum(1)
            pe.wait_ge(s["norm_done"], 2 * DK)
            linear("uq", [(0, DK, hn)])

            def tok_out(tt):
                return slice(P * tt, P * tt + (P if tt < 4 else 32))

            def kv_body(i, slot, n, ready):
                half = slot_half("kv", slot)
                pe.wait_ge(w_ready[slot], ready)
                pe.wait_ge(s["evac"], n + (EV0 - 1))
                w = wslot[:, slot, 0:2048].rearrange("p (k n) -> p k n", k=DK)
                for tt in range(5):
                    m = P if tt < 4 else 32
                    ins = acc(ps[0:m, 4 * half + tt // 2, 256 * (tt % 2):256 * (tt % 2) + 256],
                              [(hn[:, k, tok_out(tt)], w[:, k, :]) for k in range(DK)])
                ins.then_inc(s["mm_done"], 1)
            tiles(pe, "kv", kv_body)

            def idx_body(i, slot, n, ready):
                half = slot_half("idx", slot)
                pe.wait_ge(w_ready[slot], ready)
                pe.wait_ge(s["evac"], n + (EV0 - 1))
                w = wslot[:, slot, 0:DK * NQI].rearrange("p (k n) -> p k n", k=DK)
                for m in range(2):
                    acc(ps[:, 4 * half + m, :], [(w[:, k, P * m:P * m + P], hn[:, k, 0:SEQ]) for k in range(DK)])
                for tt in range(5):
                    m = P if tt < 4 else 32
                    acc(ps[0:m, 4 * half + 2, 40 * tt:40 * tt + 40], [(hn[:, k, tok_out(tt)], w[:, k, 256:296]) for k in range(DK)])
                acc(ps[0:32, 4 * half + 3, 0:256], [(hn[:, k, SEQ:NT], w[:, k, 0:256]) for k in range(DK)])
                acc(ps[0:8, 4 * half + 3, 256:288], [(w[:, k, 288:296], hn[:, k, SEQ:NT]) for k in range(DK)]).then_inc(s["mm_done"], 1)
            tiles(pe, "idx", idx_body)
            pe.wait_ge(s["evac"], EV0 + first_tile["idx"] + 1)

            def turn_tok(b, src):
                for tt in range(5):
                    m = P if tt < 4 else 32
                    dst = ps[:, b, P * tt:P * tt + P] if tt < 4 else ps[:, b + 1, 0:32]
                    ins = pe.transpose(dst, src(tt, m), ident[0:m, 0:m])
                return ins
            for j in range(4):
                if j >= 2:
                    pe.wait_ge(s["kt_ev"], j - 1)
                turn_tok(2 * (j % 2), lambda tt, m: ktok[0:m, tt, P * j:P * j + P]).then_inc(s["kt_t"], 1)
            turn_tok(4, lambda tt, m: ki4[0:m, tt, :, :].rearrange("p r d -> p (r d)")).then_inc(s["kt_t"], 1)
            for h in range(IH):
                ins = pe.transpose(ps[:, 6, 32 * h:32 * h + 32], qis4[:, h, :, :].rearrange("p r d -> p (r d)"), ident[0:32, 0:32])
            ins.then_inc(s["kt_t"], 1)

            pe.wait_ge(s["u_in"], 32)
            pe.wait_ge(s["kt_ev"], 6)
            for q in range(4):
                for g4 in range(4):
                    gp = 4 * q + g4
                    for h in range(2):
                        for c in range(2):
                            ins = pe.matmul(ps[64 * h:64 * h + 64, 2 * q + c, UC * g4:UC * g4 + UC], gb[:, c, gp, 64 * h:64 * h + 64],
                                            uch[:, 2 * gp + h, :], start=True, stop=True)
                ins.then_inc(s["vmm"], 1)
            pe.wait_ge(s["toep_in"][0], 16 * 16)
            pe.wait_ge(s["toep_in"][1], 16 * 16)
            pe.wait_ge(s["v_ev"], 4)
            pe.wait_ge(s["scan_done"], 1)
            for q4 in range(4):
                for g8 in range(8):
                    g = 8 * q4 + g8
                    q, gp, sl, c0 = q4 + 4 * (g % 2), g // 2, slice(64 * (g % 2), 64 * (g % 2) + 64), UC * (g8 // 2)
                    pe.matmul(ps[:, q, c0:c0 + UC], toep[:, g, :], uch[:, g, :], start=True, stop=False, skip_group_check=True)
                    for c, y in enumerate((yre, yim)):
                        pe.matmul(ps[:, q, c0 + 1:c0 + NC], y[sl, gp, 1:9, :].rearrange("p k i -> p (k i)"), vst[sl, c, gp, 0:NC - 1],
                                  start=False, stop=False, skip_group_check=True)
                    for c, y in enumerate((yre, yim)):
                        ins = pe.matmul(ps[64:128, q, c0 + NC:c0 + UC], y[sl, gp, 1:5, :].rearrange("p k i -> p (k i)"), s0[sl, c, :, gp],
                                        start=False, stop=(c == 1), skip_group_check=True)
                ins.then_inc(s["ymm"], 1)
            pe.wait_ge(s["y_ev"], 2)
            pe.wait_ge(s["fin_ready"], 1)
            for c in range(2):
                pe.transpose(ps[:, 0, P * c:P * c + P], fin_s[:, c, :, :].rearrange("p b g -> p (b g)"), ident[:])
                ins = pe.transpose(ps[0:GP, 0, 256 + P * c:384 + P * c], fin_p[:, c, :], ident[:])
            ins.then_inc(s["fin_mm"], 1)

            pe.wait_ge(s["fin_ev"], 1)
            pe.wait_ge(s["y_ev"], 8)
            for x in range(24):
                qb, h = 1 + x // 8, x % 8
                w = P * (qb + 1)
                r = slice(32 * (h % 4), 32 * (h % 4) + 32)
                if x >= 4:
                    pe.wait_ge(s["ix_relu"], x - 3)
                pe.matmul(ps[:, h % 4, 0:w], qiT[r, h // 4, P * qb:P * qb + P], kiT[r, 0:w], start=True, stop=True).then_inc(s["ix_mm"], 1)
            pe.wait_ge(s["bf_done"], 2)
            pe.wait_ge(s["ix_relu"], 24)
            pe.wait_ge(s["kt_ev"], 4)

            def p_scores(x):
                qb, h = x // 8, x % 8
                w = P * (qb + 1)
                r = slice(64 * (h % 2), 64 * (h % 2) + 64)
                if x >= 2:
                    pe.wait_ge(s["at_sm"], x - 1)
                if h == 0 and qb:
                    pe.wait_ge(s["sel_done"], qb)
                pe.matmul(ps[:, x % 2, 0:w], identb[:], causb[:] if qb == 0 else selb[:, qb, 0:w], start=True, stop=False)
                pe.matmul(ps[:, x % 2, 0:w], qT[r, h // 2, P * qb:P * qb + P], kT[r, h // 2, 0:w], start=False, stop=True).then_inc(s["at_s"], 1)

            def p_turn(x):
                qb = x // 8
                pe.wait_ge(s["at_exp"], x + 1)
                if x >= 2:
                    pe.wait_ge(s["at_tc"], x - 1)
                for k in range(qb + 1):
                    ins = pe.transpose(ps[:, 2 + x % 2, P * k:P * k + P], pexp[:, x % 2, P * k:P * k + P], ident[:])
                ins.then_inc(s["at_t"], 1)

            def p_values(x):
                qb, h = x // 8, x % 8
                pe.wait_ge(s["at_tc"], x + 1)
                if h == 0 and qb >= 2:
                    pe.wait_ge(s["at_o"], qb - 1)
                acc(ps[:, 4 + qb % 2, HD * h:HD * h + HD],
                    [(pT[:, x % 2, P * k:P * k + P], vtok[:, k, HD * h:HD * h + HD]) for k in range(qb + 1)]).then_inc(s["at_pv"], 1)

            def p_turn_out(qb):
                pe.wait_ge(s["at_o"], qb + 1)
                if qb >= 2:
                    pe.wait_ge(s["at_otc"], qb - 1)
                for j in range(4):
                    ins = pe.transpose(ps[:, 6 + qb % 2, P * j:P * j + P], ao[:, qb % 2, P * j:P * j + P], ident[:])
                ins.then_inc(s["at_ot"], 1)

            for x in range(34):
                if x < 32:
                    p_scores(x)
                if 1 <= x < 33:
                    p_turn(x - 1)
                if x >= 2:
                    p_values(x - 2)
                if x >= 2 and (x - 2) % 8 == 7:
                    p_turn_out((x - 2) // 8)

            pe.wait_ge(s["at_otc"], 4)
            pe.wait_ge(s["oh_in"], 48)
            pe.wait_ge(s["sm_prep"], 1)
            cols = [(0, 512), (512, 1024), (1024, NKEY)]
            for b, (c0, c1) in enumerate(cols):
                pe.matmul(ps[:, b, 0:c1 - c0], rbexp, ohs[:, c0:c1], start=True, stop=True)
            pe.matmul(ps[:, 3, 0:32], head_row, wT8, start=True, stop=True).then_inc(s["sm_pe"], 1)
            pe.wait_ge(s["sm_b"], 1)
            pe.wait_ge(s["kidx_in"], 16 * NB * NPAGE)
            for b in range(NB):
                if b:
                    pe.wait_ge(s["sx_tc"], b)
                for k in range(2):
                    ins = pe.transpose(ps[:, 4, P * k:P * k + P], kidx[:, 8 * b + 4 * k:8 * b + 4 * k + 4, :].rearrange("p n d -> p (n d)"), ident[:])
                ins.then_inc(s["sx_t"], 1)
                pe.wait_ge(s["sx_tc"], b + 1)
                if b == 4:
                    pe.wait_ge(s["sx_relu"], 1)
                q = slice(32 * (b % 4), 32 * (b % 4) + 32)
                for k in range(NPAGE):
                    r = slice(32 * (k % 4), 32 * (k % 4) + 32)
                    ins = pe.matmul(ps[q, k % 4, P * (k // 4):P * (k // 4) + P], qis[r, b, :, :].rearrange("p h q -> p (h q)"),
                              kxT[r, b % 2, P * (k // 4):P * (k // 4) + P], start=True, stop=True, tile_position=(32 * (k % 4), 32 * (b % 4)))
                if b >= 4:
                    ins.then_inc(s["kv_used"], 1)
                pe.matmul(ps[q, 0, 256:288], qis[0:32, b, :, :].rearrange("p h q -> p (h q)"), kiT[0:32, SEQ:NT],
                          start=True, stop=True, tile_position=(0, 32 * (b % 4))).then_inc(s["sx_mm"], 1)
                if b % 4 == 3:
                    g = b // 4
                    pe.wait_ge(s["sx_relu"], g + 1)
                    for k, (c0, c1) in enumerate(cols):
                        ins = pe.matmul(ps[0:32, 5 + k, 0:c1 - c0], wsel[:, g, :], rls[:, c0:c1], start=(g == 0), stop=(g == 1))
                    ins.then_inc(s["sx_w"], 1)
            pe.wait_ge(s["sx_sel"], 1)
            for g in range(2):
                if g:
                    pe.wait_ge(s["ss_sm"], g)
                for k, (c0, c1) in enumerate(cols):
                    pe.matmul(ps[:, k, 0:c1 - c0], tok_row[:, g, :], sels[:, c0:c1], start=True, stop=False, skip_group_check=True)
                for bl in range(4):
                    b = 4 * g + bl
                    q = slice(32 * bl, 32 * bl + 32)

                    for k in range(NPAGE):
                        n = 32 * g + 8 * bl + k
                        r = k % 4
                        pe.wait_ge(kv_in[r], 16 * (16 * g + (8 * bl + k) // 4 + 1))
                        if n >= 2:
                            pe.wait_ge(s["kp_tc"], n - 1)
                        for j in range(4):
                            ins = pe.transpose(ps[:, 3 + k % 2, P * j:P * j + P], kring[:, r, P * j:P * j + P], ident[:])
                        ins.then_inc(s["kp_t"], 1)
                        pe.wait_ge(s["kp_tc"], n + 1)
                        for j in range(4):
                            ins = pe.matmul(ps[q, k // 4, P * (k % 4):P * (k % 4) + P], qbd[:, j, b, :], pgT[:, k % 2, P * j:P * j + P],
                                            start=False, stop=False, skip_group_check=True)
                        ins.then_inc(s["kv_used"], 1)
                    for j in range(4):
                        ins = pe.matmul(ps[q, 2, 0:32], qbd[:, j, b, :], kT[:, j, SEQ:NT], start=False, stop=(j == 3), skip_group_check=True)
                    if bl == 3:
                        ins.then_inc(s["ss_mm"], 1)
                pe.wait_ge(s["ss_exp"], g + 1)
                if g:
                    pe.wait_ge(s["sp_tc"], g)
                    pe.wait_ge(s["sv_o"], g)
                for k in range(NPAGE):
                    pe.transpose(ps[:, 6 + k // 4, P * (k % 4):P * (k % 4) + P], pes[:, P * k:P * k + P], ident[:])
                pe.transpose(ps[0:32, 5, 0:P], pes[:, PAST:NKEY], ident[:]).then_inc(s["sp_t"], 1)
                pe.wait_ge(s["sp_tc"], g + 1)
                for bl in range(4):
                    q = slice(32 * bl, 32 * bl + 32)
                    for k in range(NPAGE):
                        r = k % 4
                        pe.wait_ge(kv_in[r], 16 * (16 * g + 8 + (8 * bl + k) // 4 + 1))
                        pe.matmul(ps[q, 5, :], ptS[:, k, q], kring[:, r, :], start=(k == 0), stop=False, skip_group_check=True).then_inc(s["kv_used"], 1)
                    ins = pe.matmul(ps[q, 5, :], ptS[0:32, 8, q], vtok[0:32, 4, :], start=False, stop=True, skip_group_check=True)
                ins.then_inc(s["sv_mm"], 1)
            pe.wait_ge(s["sv_o"], 2)
            for j in range(4):
                ins = acc(ps[:, 6, 32 * j:32 * j + 32], [(osel[:, g, P * j:P * j + P], row_tok[:, g, :]) for g in range(2)])
            ins.then_inc(s["so_mm"], 1)
            pe.wait_ge(s["so_ev"], 1)

            pe.wait_ge(s["gelu_done"], 2)
            linear("glu", [(0, 4, gT), (4, 4, gT)])
            linear("gs", [(0, DK, hn)])
            linear("ga_att", [(0, DK, hn), (DK, 4, attT)])
            pe.wait_ge(s["evac"], EV0 + first_tile["out"])
            linear("out", [(0, DK, mixed)])
            norm_sum(2)
            pe.wait_ge(s["norm_done"], 3 * DK)
            linear("ffn2_in", [(0, DK, hn), (DK, DK, hn)])
            pe.wait_ge(s["evac"], EV0 + first_tile["ffn2_out"])
            linear("ffn2_out", [(0, FK, act)])
            norm_sum(3)
            pe.wait_ge(s["norm_done"], 4 * DK)
            for k in range(5):
                m = P if k < 4 else 32
                if k >= 2:
                    pe.wait_ge(s["yt_ev"], k - 1)
                for j in range(DK):
                    ins = pe.transpose(ps[0:m, 2 + 2 * (k % 2) + j // 4, P * (j % 4):P * (j % 4) + P], hn[:, j, P * k:P * k + m], ident[:])
                ins.then_inc(s["yt_t"], 1)

        @block.scalar
        def _(act_e):
            def squares(k):
                for j in range(DK):
                    if k == 0:
                        act_e.wait_ge(s["evac"], j + 1)
                    else:
                        act_e.wait_ge(s["evac"], EV0 + {1: first_tile["uq"], 2: first_tile["ffn2_in"], 3: ALLT}[k])
                    act_e.activation(hn[:, j, :], hT[:, j, :], ACT.Square).then_inc(s["sq_done"], 1)

            def root(k):
                act_e.wait_ge(s["ssum_done"], k + 1)
                act_e.activation(rstd[:].rearrange("p (h n) -> p h n", h=2), ps[:, 0:2, 0:HALF], ACT.Sqrt, bias=epsc[:, 0:1],
                                 scale=1.0 / D).then_inc(s["sqrt_done"], 1)

            def gate(layer, func, done0, o):
                def body(i, slot, n, ready):
                    half = slot_half(layer, slot)
                    act_e.wait_ge(s["mm_done"], n + (MM0 + 1))
                    act_e.wait_ge(s["evac"], n + (EV0 - 1))
                    act_e.activation(sg[:, half, :].rearrange("p (h n) -> p h n", h=2), ps[:, 4 * half + 2 * o:4 * half + 2 * o + 2, 0:HALF],
                                     func).then_inc(s["gate_done"], 1)
                tiles(act_e, layer, body)

            act_e.wait_ge(s["pool_const"], 1)
            squares(0)
            act_e.wait_ge(s["par_in"], 16 * 20)
            act_e.activation(ldt, ldt, ACT.Exp).then_inc(s["dt_done"], 1)
            root(0)
            act_e.wait_ge(s["early_pe"], 1)
            for c in range(2):
                for h in range(2):
                    src = ps[64 * h:64 * h + 64, 2 + c, :].rearrange("p (g s i) -> p g s i", s=2, i=GC)[:, :, h, :]
                    ins = act_e.activation(cT[64 * h:64 * h + 64, c, :, :], src, ACT.Copy, scale=1.0 if c == 0 else -1.0)
            ins.then_inc(s["early_act"], 1)
            act_e.activation(s0[:].rearrange("p c b g -> p (c b g)"), ps[:, 4, 0:256], ACT.Copy).then_inc(s["early_act"], 1)
            act_e.activation(dch[:], ps[:, 4, 256:288], ACT.Copy).then_inc(s["early_act"], 1)
            for h in range(HEADS):
                act_e.wait_ge(s["shift_mm"], h + 1)
                if h >= 2:
                    act_e.wait_ge(s["shift_out"][h % 2], 16 * (h // 2))
                act_e.activation(shrow[:, h % 2, :].rearrange("p (b n) -> p b n", b=2), ps[:, 6:8, 0:320], ACT.Copy).then_inc(s["early_act"], 1)
            act_e.wait_ge(s["ang_done"], 1)
            act_e.activation(v(7), v(2), ACT.Sin).then_inc(s["trig_done"], 1)
            act_e.activation(v(8), v(2), ACT.Sin, scale=0.5).then_inc(s["trig_done"], 1)
            act_e.activation(v(4), v(1), ACT.Exp).then_inc(s["trig_done"], 1)
            gate("ffn1_in", ACT.Silu, 0, 0)
            for r in range(8):
                act_e.wait_ge(s["gbt"], r + 1)
                if r == 0:
                    act_e.wait_ge(s["mm_done"], MM0 + 30)
                act_e.activation(gb[:, r // 4, 4 * (r % 4):4 * (r % 4) + 4, :].rearrange("p g n -> p (g n)"), ps[:, r, :], ACT.Copy).then_inc(s["gb_ev"], 1)
            squares(1)
            root(1)
            for q in range(4):
                act_e.wait_ge(s["vmm"], q + 1)
                for c in range(2):
                    ins = act_e.activation(vst[:, c, 4 * q:4 * q + 4, :].rearrange("p g n -> p (g n)"), ps[:, 2 * q + c, 0:4 * UC], ACT.Copy)
                ins.then_inc(s["v_ev"], 1)
            act_e.wait_ge(s["y_in"], 32)
            act_e.activation(gT[:, :, 0:SEQ].rearrange("p k (n t) -> p k n t", t=CH),
                             yT[:, :, 0:SEQ].rearrange("p k (t n) -> p k n t", t=CH), ACT.Gelu_apprx_tanh).then_inc(s["gelu_done"], 1)
            act_e.activation(gT[:, :, SEQ:NT].rearrange("p k (n t) -> p k n t", t=NS),
                             yT[:, :, SEQ:NT].rearrange("p k (t n) -> p k n t", t=NS), ACT.Gelu_apprx_tanh).then_inc(s["gelu_done"], 1)
            for x in range(24):
                w = P * (2 + x // 8)
                act_e.wait_ge(s["ix_mm"], x + 1)
                if x >= 2:
                    act_e.wait_ge(s["ix_acc"], x - 1)
                act_e.activation(rl[:, x % 2, 0:w], ps[:, x % 4, 0:w], ACT.Relu).then_inc(s["ix_relu"], 1)
            for x in range(33):
                if x < 32:
                    w = P * (1 + x // 8)
                    act_e.wait_ge(s["at_sm"], x + 1)
                    if x >= 2:
                        act_e.wait_ge(s["at_t"], x - 1)
                    if x % 8 == 0 and x >= 16:
                        act_e.wait_ge(s["at_o"], x // 8 - 1)
                    act_e.activation(pexp[:, x % 2, 0:w], smx[:, x % 2, 0:w], ACT.Exp, scale=-1.0, bias=nmx[:, x % 2:x % 2 + 1],
                                     accum_out=rsum[:, x // 8 % 2, x % 8:x % 8 + 1]).then_inc(s["at_exp"], 1)
                if x >= 1:
                    w = P * (1 + (x - 1) // 8)
                    act_e.wait_ge(s["at_t"], x)
                    if x >= 3:
                        act_e.wait_ge(s["at_pv"], x - 2)
                    act_e.activation(pT[:, (x - 1) % 2, 0:w], ps[:, 2 + (x - 1) % 2, 0:w], ACT.Copy).then_inc(s["at_tc"], 1)
            for g in range(2):
                act_e.wait_ge(s["sx_mm"], 4 * g + 4)
                if g:
                    act_e.wait_ge(s["sx_w"], g)
                for k in range(4):
                    act_e.activation(rls[:, 0:PAST].rearrange("p (j r n) -> p r j n", j=2, r=4)[:, k],
                                     ps[:, k, 0:256].rearrange("p (j n) -> p j n", j=2), ACT.Relu)
                act_e.activation(rls[:, PAST:NKEY], ps[:, 0, 256:288], ACT.Relu).then_inc(s["sx_relu"], 1)
            for g in range(2):
                with act_e.Fori(0, 16) as i:
                    for k in range(2):
                        act_e.wait_ge(s["kp_t"], i * 2 + (32 * g + k + 1))
                        act_e.wait_ge(s["kv_used"], i * 2 + (64 * g + k + 3))
                        act_e.activation(pgT[:, k, :], ps[:, 3 + k, :], ACT.Copy).then_inc(s["kp_tc"], 1)
                act_e.wait_ge(s["ss_sm"], g + 1)
                act_e.activation(pes, sms, ACT.Exp, scale=-1.0, bias=nmx[:, g:g + 1], accum_out=rsum[:, 0, g:g + 1]).then_inc(s["ss_exp"], 1)
                act_e.wait_ge(s["sp_t"], g + 1)
                if g:
                    act_e.wait_ge(s["sv_mm"], g)
                act_e.activation(ptS[:, 0:8, :].rearrange("p (b k) n -> p b (k n)", b=2), ps[:, 6:8, :], ACT.Copy)
                act_e.activation(ptS[0:32, 8, :], ps[0:32, 5, 0:P], ACT.Copy).then_inc(s["sp_tc"], 1)
            act_e.wait_ge(s["so_mm"], 1)
            gate("glu", ACT.Sigmoid, 0, 1)
            gate("gs", ACT.Sigmoid, 0, 0)
            gate("ga_att", ACT.Sigmoid, 0, 0)
            squares(2)
            root(2)
            gate("ffn2_in", ACT.Silu, 0, 0)
            squares(3)
            root(3)

        @block.gpsimd
        def _(pool):
            pool.memset(ones[:], 1.0)
            pool.memset(epsc[:], EPS).then_inc(s["pool_const"], 1)
            pool.wait_ge(s["oh_in"], 32)
            for h in range(HEADS):
                ins = pool.tensor_copy(relrep[0:NBKT, h, :], relb[:, h:h + 1].broadcast_to([NBKT, P]))
            ins.then_inc(s["relrep"], 1)
            pool.wait_ge(s["pow_done"], 1)
            pool.wait_ge(s["early_act"], 1)

            def product(n0, i, ar, ai, xr, xi, o_re, o_im, sub_re, sub_im):
                for o, a, b in ((pt1, xr, ar), (pt2, xi, ai), (pt3, xi, ar), (pt4, xr, ai)):
                    ins = pool.tensor_tensor(o, a, b, ALU.mult)
                    ins.then_inc(s["pool_step"], 1)
                pool.wait_ge(s["pool_step"], i * 6 + (n0 + 4))
                pool.tensor_tensor(o_re, pt1, pt2, sub_re).then_inc(s["pool_step"], 1)
                pool.tensor_tensor(o_im, pt3, pt4, sub_im).then_inc(s["pool_step"], 1)
                pool.wait_ge(s["pool_step"], i * 6 + (n0 + 6))

            def power(k, c):
                return apow[:, bass.ds(k, 1), c, :].rearrange("p a g -> p (a g)").unsqueeze(2).broadcast_to([P, GP, GC])

            def at_lag(a, k):
                return a[:, :, bass.ds(k, 1), :].rearrange("p g a i -> p g (a i)")
            with pool.Fori(0, 9) as k:
                product(0, k, power(k, 0), power(k, 1), cT[:, 0], cT[:, 1], at_lag(yre, k), at_lag(yim, k), ALU.add, ALU.subtract)
            with pool.Fori(0, CH) as k:
                product(54, k, power(k * -1 + 7, 0), power(k * -1 + 7, 1), bbar[:, 0], bbar[:, 1],
                        at_lag(wb[:, 0], k), at_lag(wb[:, 1], k), ALU.subtract, ALU.add)
            pool.sem_inc(s["prep_done"], 1)
            pool.wait_ge(s["mm_done"], MM0 + 30)
            pool.memset(toep[:].rearrange("p g n -> p (g n)"), 0.0).then_inc(s["tz_zero"], 1)
            pool.memset(uch[0:64, :, NC:UC], 0.0).then_inc(s["u_zero"], 1)
            pool.wait_ge(s["u_in"], 32)
            pool.wait_ge(s["u_zero"], 1)
            pool.wait_ge(s["toep_in"][0], 256)
            pool.wait_ge(s["toep_in"][1], 256)
            pool.tensor_tensor(udb, uch, dch[:].unsqueeze(2).broadcast_to([P, G, UC]), ALU.mult).then_inc(s["ud_done"], 1)

        @block.vector
        def _(dve):
            count = [0]

            def link(*steps):
                for ins in steps:
                    count[0] += 1
                    ins.then_inc(s["dve_step"], 1)
                dve.wait_ge(s["dve_step"], count[0])

            def tt(o, a, b, op):
                return dve.tensor_tensor(o, a, b, op)

            def norm(k):
                dve.wait_ge(s["sqrt_done"], k + 1)
                link(dve.reciprocal(rstd[:], rstd[:]))
                for j in range(DK):
                    dve.scalar_tensor_tensor(out=hn[:, j, :], in0=hT[:, j, :], scalar=gains[:, k, j:j + 1], in1=rstd[:],
                                             op0=ALU.mult, op1=ALU.mult).then_inc(s["norm_done"], 1)

            def evac(layer, fn, wait_gate=None):
                def body(i, slot, n, ready):
                    dve.wait_ge(s["mm_done"], n + (MM0 + 1))
                    if wait_gate is not None:
                        dve.wait_ge(s["gate_done"], i + (wait_gate + 1))
                    fn(i, slot_half(layer, slot)).then_inc(s["evac"], 1)
                tiles(dve, layer, body)

            def pair(half, o):
                return ps[:, 4 * half + 2 * o:4 * half + 2 * o + 2, 0:HALF]

            def two(ap):
                return ap.rearrange("p (h n) -> p h n", h=2)

            for k in range(DK):
                dve.wait_ge(s["mm_done"], k + 1)
                dve.tensor_copy(hT[:, k, 0:SEQ], ps[:, 4 * (k % 2), :])
                dve.tensor_copy(hT[:, k, SEQ:NT], ps[:, 4 * (k % 2) + 1, 0:32]).then_inc(s["evac"], 1)
                if k == DK - 1:
                    dve.wait_ge(s["evac"], DK)
                    dve.sem_inc(s["x_turned"], 1)
            dve.tensor_copy(identb[:], ident[:]).then_inc(s["bf_done"], 1)
            dve.tensor_copy(causb[:], caus[:]).then_inc(s["bf_done"], 1)
            norm(0)
            dve.wait_ge(s["dt_done"], 1)
            dve.wait_ge(s["par_in"], 16 * 20)
            lr, li = lam[:, 0, :], lam[:, 1, :]
            TWO_PI_HI = 6.28125
            TWO_PI_LO = 2 * math.pi - TWO_PI_HI
            ROUND = 12582912.0
            link(tt(v(1), lr, ldt, ALU.mult), tt(v(2), li, ldt, ALU.mult))
            link(dve.tensor_scalar(v(5), v(2), 1 / (2 * math.pi), ROUND, ALU.mult, ALU.add))
            link(dve.tensor_scalar(v(5), v(5), -ROUND, None, ALU.add))
            link(dve.scalar_tensor_tensor(out=v(2), in0=v(5), scalar=-TWO_PI_HI, in1=v(2), op0=ALU.mult, op1=ALU.add))
            link(dve.scalar_tensor_tensor(out=v(2), in0=v(5), scalar=-TWO_PI_LO, in1=v(2), op0=ALU.mult, op1=ALU.add))
            link(dve.tensor_scalar(v(2), v(2), 3.1415925, -3.1415925, ALU.min, ALU.max))
            dve.sem_inc(s["ang_done"], 1)
            link(tt(v(9), lr, lr, ALU.mult), tt(v(10), li, li, ALU.mult))
            link(tt(v(9), v(9), v(10), ALU.add))
            link(dve.reciprocal(v(9), v(9)))
            dve.wait_ge(s["trig_done"], 3)
            link(tt(v(8), v(8), v(8), ALU.mult))
            link(dve.tensor_scalar(v(8), v(8), -2.0, 1.0, ALU.mult, ALU.add))
            link(dve.memset(apow[:, 0, 0, :], 1.0), dve.memset(apow[:, 0, 1, :], 0.0),
                 tt(apow[:, 1, 0, :], v(4), v(8), ALU.mult), tt(apow[:, 1, 1, :], v(4), v(7), ALU.mult))
            ar, ai = apow[:, 1, 0, :], apow[:, 1, 1, :]
            link(dve.tensor_scalar(v(10), ar, -1.0, None, ALU.add))
            link(tt(v(11), v(10), lr, ALU.mult), tt(v(12), ai, li, ALU.mult), tt(v(13), ai, lr, ALU.mult), tt(v(14), v(10), li, ALU.mult))
            link(tt(v(11), v(11), v(12), ALU.add), tt(v(13), v(13), v(14), ALU.subtract))
            link(tt(v(11), v(11), v(9), ALU.mult), tt(v(13), v(13), v(9), ALU.mult))

            def powers(arr):
                for m in (1, 2, 4):
                    def bc(c):
                        return arr[:, m, c, :].unsqueeze(1).broadcast_to([P, m, GP])
                    lo = [arr[:, 1:m + 1, c, :] for c in range(2)]
                    hi = [arr[:, m + 1:2 * m + 1, c, :] for c in range(2)]
                    p4 = [s5q[:, k, 0:m, :] for k in range(4)]
                    link(tt(p4[0], lo[0], bc(0), ALU.mult), tt(p4[1], lo[1], bc(1), ALU.mult),
                         tt(p4[2], lo[0], bc(1), ALU.mult), tt(p4[3], lo[1], bc(0), ALU.mult))
                    link(tt(hi[0], p4[0], p4[1], ALU.subtract), tt(hi[1], p4[2], p4[3], ALU.add))
            powers(apow)
            link(dve.tensor_copy(cpow[:, 1], apow[:, 8]))
            powers(cpow)

            def zb(k):
                return v(k).unsqueeze(2).broadcast_to([P, GP, GC])
            link(tt(pt1, bmat[:, 0], zb(11), ALU.mult), tt(pt2, bmat[:, 1], zb(13), ALU.mult),
                 tt(pt3, bmat[:, 1], zb(11), ALU.mult), tt(pt4, bmat[:, 0], zb(13), ALU.mult))
            link(tt(bbar[:, 0], pt1, pt2, ALU.subtract), tt(bbar[:, 1], pt3, pt4, ALU.add))
            dve.sem_inc(s["pow_done"], 1)

            def glu_out(i, half):
                return tt(two(one(act, i)), two(sg[:, half, :]), pair(half, 1), ALU.mult)
            evac("ffn1_in", glu_out, 0)

            def add_half(i, half):
                return dve.scalar_tensor_tensor(out=two(one(hT, i)), in0=pair(half, 0), scalar=0.5, in1=two(one(hT, i)), op0=ALU.mult, op1=ALU.add)
            evac("ffn1_out", add_half)
            for r in range(4):
                dve.wait_ge(s["km"], r + 1)
                if r == 0:
                    dve.wait_ge(s["mm_done"], MM0 + 30)
                if r >= 2:
                    dve.wait_ge(s["toep_in"][r % 2], 16 * 8)
                for h in range(2):
                    ins = dve.tensor_copy(kbuf[0:16, r % 2, :, :].rearrange("p (g s) n -> p g s n", s=2)[:, :, h, :],
                                          ps[0:16, 2 * (r % 2) + h, :].rearrange("p (g n) -> p g n", g=4))
                ins.then_inc(s["k_ev"], 1)
            norm(1)
            for i in range(4):
                n = first_tile["uq"] + i
                half = n % 2
                dve.wait_ge(s["mm_done"], MM0 + n + 1)
                o = uT[:, i, 0:SEQ].rearrange("p (t n) -> p n t", t=CH)
                c = HALF // CH
                dve.tensor_copy(o[:, 0:c, :], ps[:, 4 * half, 0:HALF].rearrange("p (n t) -> p n t", t=CH))
                dve.tensor_copy(o[:, c:NC, :], ps[:, 4 * half + 1, 0:SEQ - HALF].rearrange("p (n t) -> p n t", t=CH))
                dve.tensor_copy(uT[:, i, SEQ:NT].rearrange("p (t n) -> p n t", t=NS),
                                ps[:, 4 * half + 1, SEQ - HALF:HALF].rearrange("p (n t) -> p n t", t=NS)).then_inc(s["evac"], 1)
            for i in range(4):
                n = first_tile["uq"] + 4 + i
                dve.wait_ge(s["mm_done"], MM0 + n + 1)
                dve.tensor_scalar(two(qT[:, i, :]), pair(n % 2, 0), HD ** -0.5, None, ALU.mult).then_inc(s["evac"], 1)
            for i in range(4):
                n = first_tile["kv"] + i
                half, c0 = n % 2, 256 * (i % 2)
                dst = (ktok, vtok)[i // 2]
                dve.wait_ge(s["mm_done"], MM0 + n + 1)
                dve.tensor_copy(dst[:, 0:4, c0:c0 + 256].rearrange("p (a b) n -> p a b n", a=2),
                                ps[:, 4 * half:4 * half + 2, :].rearrange("p a (b n) -> p a b n", b=2))
                dve.tensor_copy(dst[0:32, 4, c0:c0 + 256], ps[0:32, 4 * half + 2, 0:256]).then_inc(s["evac"], 1)
            n = first_tile["idx"]
            b = 4 * (n % 2)
            dve.wait_ge(s["mm_done"], MM0 + n + 1)
            dve.tensor_copy(qiT[:, 0:2, :], ps[:, b:b + 2, :])
            W_SCALE = ID ** -0.5 * IH ** -0.5
            for tt_ in range(5):
                m = P if tt_ < 4 else 32
                c0 = 40 * tt_
                dve.tensor_copy(ki4[0:m, tt_, :, :], ps[0:m, b + 2, c0:c0 + ID].unsqueeze(1).broadcast_to([m, 4, ID]))
                if tt_ < 4:
                    dve.tensor_scalar(wtok[:, tt_, :], ps[:, b + 2, c0 + ID:c0 + ID + IH], W_SCALE, None, ALU.mult)
            dve.tensor_copy(qis4, ps[0:32, b + 3, 0:256].rearrange("p (h d) -> p h d", h=IH).unsqueeze(2).broadcast_to([32, IH, 4, ID]))
            dve.tensor_scalar(wT8, ps[0:8, b + 3, 256:288], W_SCALE, None, ALU.mult).then_inc(s["evac"], 1)
            for j in range(6):
                dve.wait_ge(s["kt_t"], j + 1)
                if j < 5:
                    bk = 2 * (j % 2) if j < 4 else 4
                    o = kT[:, j, :] if j < 4 else kiT[:]
                    dve.tensor_copy(o[:, 0:SEQ], ps[:, bk, :])
                    dve.tensor_copy(o[:, SEQ:NT], ps[:, bk + 1, 0:32]).then_inc(s["kt_ev"], 1)
                else:
                    dve.tensor_copy(qis[:].rearrange("p b h q -> p h b q"), ps[:, 6, 0:256].rearrange("p (h b q) -> p h b q", h=IH, b=NB)).then_inc(s["kt_ev"], 1)
            link(dve.memset(qbd[:].rearrange("p j b r -> p (j b r)"), 0.0))
            for j in range(4):
                for h in range(2):
                    sl = slice(64 * h, 64 * h + 64)
                    hh = 2 * j + h
                    ins = dve.tensor_copy(qbd[sl, j, :, NS * hh:NS * hh + NS], qT[sl, j, SEQ:NT].rearrange("p (b q) -> p b q", b=NB))
            link(ins)

            dve.wait_ge(s["v_ev"], 4)
            vb = vst[:, :, :, 0:NC].rearrange("p c g (b j) -> p c g b j", j=8)

            def advance(dst, src, a, shape):
                w = int(np.prod(shape))
                tm = [prodmem[:, w * k:w * (k + 1)] for k in range(4)]
                if len(shape) == 2:
                    tm = [x.rearrange("p (a b) -> p a b", a=shape[0]) for x in tm]
                if len(shape) == 3:
                    tm = [x.rearrange("p (a b c) -> p a b c", a=shape[0], b=shape[1]) for x in tm]
                link(tt(tm[0], src[0], a[0], ALU.mult), tt(tm[1], src[1], a[1], ALU.mult),
                     tt(tm[2], src[0], a[1], ALU.mult), tt(tm[3], src[1], a[0], ALU.mult))
                link(tt(tm[0], tm[0], tm[1], ALU.subtract), tt(tm[2], tm[2], tm[3], ALU.add))
                link(tt(dst[0], dst[0], tm[0], ALU.add), tt(dst[1], dst[1], tm[2], ALU.add))
            for j in range(1, 8):
                advance([vb[:, c, :, :, j] for c in range(2)], [vb[:, c, :, :, j - 1] for c in range(2)],
                        [cpow[:, 1, c, :].unsqueeze(2).broadcast_to([P, GP, 8]) for c in range(2)], (GP, 8))
            for b_ in range(1, 8):
                advance([vb[:, c, :, b_, 7] for c in range(2)], [vb[:, c, :, b_ - 1, 7] for c in range(2)],
                        [cpow[:, 8, c, :] for c in range(2)], (GP,))
            for j in range(7):
                advance([vb[:, c, :, 1:8, j] for c in range(2)], [vb[:, c, :, 0:7, 7] for c in range(2)],
                        [cpow[:, j + 1, c, :].unsqueeze(2).broadcast_to([P, GP, 7]) for c in range(2)], (GP, 7))
            link(*[dve.tensor_copy(fin_s[:, c, :, :], vst[:, c, :, NC:UC].rearrange("p g b -> p b g")) for c in range(2)],
                 *[dve.tensor_copy(fin_p[:, c, :], vst[:, c, :, NC - 1]) for c in range(2)])
            advance([fin_s[:, c] for c in range(2)], [s0[:, c] for c in range(2)],
                    [apow[:, 4, c, :].unsqueeze(1).broadcast_to([P, NB, GP]) for c in range(2)], (NB, GP))
            dve.sem_inc(s["scan_done"], 1)
            dve.sem_inc(s["fin_ready"], 1)
            dve.wait_ge(s["ud_done"], 1)
            for q in range(8):
                dve.wait_ge(s["ymm"], q // 2 + 1)
                gr = slice(8 * (q // 2) + q % 2, 8 * (q // 2) + 8, 2)
                tt(ych[:, gr, :], ps[:, q // 2 + 4 * (q % 2), 0:4 * UC].rearrange("p (g n) -> p g n", g=4), udb[:, gr, :], ALU.add).then_inc(s["y_ev"], 1)
            dve.wait_ge(s["fin_mm"], 1)
            dve.tensor_copy(fin_t[:, 0:256], ps[:, 0, 0:256])
            dve.tensor_copy(fin_t[0:GP, 256:512], ps[0:GP, 0, 256:512]).then_inc(s["fin_ev"], 1)

            dve.wait_ge(s["y_out"], 16 * 12)
            topk_n = [0]

            def top(scores, rounds):
                n0 = topk_n[0]
                with dve.Fori(0, rounds) as i:
                    dve.max(out=top8[0:scores.shape[0], :], in_=scores).then_inc(s["topk"], 1)
                    dve.wait_ge(s["topk"], i * 2 + (n0 + 1))
                    dve.tensor_copy(topwait, top8[:, 0:1])
                    dve.match_replace(out=scores, in_to_replace=top8[0:scores.shape[0], :], in_values=scores, imm_value=TAKEN).then_inc(s["topk"], 1)
                    dve.wait_ge(s["topk"], i * 2 + (n0 + 2))
                topk_n[0] += 2 * rounds
            for x in range(24):
                qb, h = 1 + x // 8, x % 8
                w = P * (qb + 1)
                dve.wait_ge(s["ix_relu"], x + 1)
                if h == 0:
                    dve.tensor_scalar(sc[:, 0:w], rl[:, x % 2, 0:w], wtok[:, qb, 0:1], None, ALU.mult).then_inc(s["ix_acc"], 1)
                else:
                    dve.wait_ge(s["ix_acc"], x)
                    dve.scalar_tensor_tensor(out=sc[:, 0:w], in0=rl[:, x % 2, 0:w], scalar=wtok[:, qb, h:h + 1], in1=sc[:, 0:w],
                                             op0=ALU.mult, op1=ALU.add).then_inc(s["ix_acc"], 1)
                if h == 7:
                    dve.wait_ge(s["ix_acc"], x + 1)
                    link(tt(sc[:, w - P:w], sc[:, w - P:w], caus[:], ALU.add))
                    top(sc[:, 0:w], TOPK_P // 8)
                    dve.tensor_scalar(selb[:, qb, 0:w], sc[:, 0:w], 0.5 * TAKEN, MASK, ALU.is_ge, ALU.mult).then_inc(s["sel_done"], 1)
                    dve.wait_ge(s["sel_done"], qb)

            dve.wait_ge(s["bias_in"], 16 * HEADS)
            for x in range(34):
                if x < 32:
                    qb, h = x // 8, x % 8
                    w = P * (qb + 1)
                    dve.wait_ge(s["at_s"], x + 1)
                    if x >= 2:
                        dve.wait_ge(s["at_exp"], x - 1)
                    dve.tensor_tensor_reduce(smx[:, x % 2, 0:w], ps[:, x % 2, 0:w], tb[:, h, SEQ - w:SEQ], -1.0, 3e38,
                                             ALU.add, ALU.min, nmx[:, x % 2:x % 2 + 1]).then_inc(s["at_sm"], 1)
                if x >= 2 and (x - 2) % 8 == 7:
                    qb = (x - 2) // 8
                    dve.wait_ge(s["at_pv"], x - 1)
                    dve.wait_ge(s["at_exp"], 8 * qb + 8)
                    link(dve.reciprocal(rinv[:, qb % 2, :], rsum[:, qb % 2, :]))
                    if qb >= 2:
                        dve.wait_ge(s["at_ot"], qb - 1)
                    tt(ao[:, qb % 2, :].rearrange("p (h d) -> p h d", h=HEADS), ps[:, 4 + qb % 2, :].rearrange("p (h d) -> p h d", h=HEADS),
                       rinv[:, qb % 2, :].unsqueeze(2).broadcast_to([P, HEADS, HD]), ALU.mult).then_inc(s["at_o"], 1)
                    dve.wait_ge(s["at_ot"], qb + 1)
                    if qb == 0:
                        dve.wait_ge(s["res_out"], 16 * 10)
                    dve.tensor_copy(attT[:, :, P * qb:P * qb + P], ps[:, 6 + qb % 2, :].rearrange("p (j n) -> p j n", j=4)).then_inc(s["at_otc"], 1)

            dve.wait_ge(s["sc_in"], 16 * 12)
            tt(rbexp.rearrange("p (b h q) -> p b h q", b=4, h=HEADS), same_step.rearrange("p (b h q) -> p b h q", b=4, h=HEADS),
               rb4.unsqueeze(1).unsqueeze(3).broadcast_to([P, 4, HEADS, NS]), ALU.mult)
            link(dve.tensor_copy(tok_row, tok_row_f))
            dve.sem_inc(s["sm_prep"], 1)
            dve.wait_ge(s["sm_pe"], 1)
            dve.tensor_copy(bs[:, 0:PAST].rearrange("p (b n) -> p b n", b=2), ps[:, 0:2, :])
            dve.tensor_copy(bs[:, PAST:NKEY], ps[:, 2, 0:32])
            for g in range(2):
                ins = tt(wsel[:, g, :], ps[:, 3, 0:32], row_tok[:, g, :], ALU.mult)
            link(ins)
            dve.sem_inc(s["sm_b"], 1)
            for b_ in range(NB):
                dve.wait_ge(s["sx_t"], b_ + 1)
                if b_ >= 2:
                    dve.wait_ge(s["sx_mm"], b_ - 1)
                dve.tensor_copy(kxT[:, b_ % 2, :], ps[:, 4, 0:256]).then_inc(s["sx_tc"], 1)
            dve.wait_ge(s["sx_w"], 2)
            link(dve.tensor_copy(scs[:, 0:PAST].rearrange("p (b n) -> p b n", b=2), ps[0:32, 5:7, :]),
                 tt(scs[:, PAST:NKEY], ps[0:32, 7, 0:32], new_mask, ALU.add))
            top(scs, TOPK_S // 8)
            dve.tensor_scalar(sels, scs, 0.5 * TAKEN, MASK, ALU.is_ge, ALU.mult).then_inc(s["sx_sel"], 1)
            dve.wait_ge(s["sx_sel"], 1)
            for g in range(2):
                dve.wait_ge(s["ss_mm"], g + 1)
                if g:
                    dve.wait_ge(s["ss_exp"], g)
                dve.tensor_tensor_reduce(sms, ps[:, 0:3, :].rearrange("p b n -> p (b n)")[:, 0:NKEY], bs, -1.0, 3e38,
                                         ALU.add, ALU.min, nmx[:, g:g + 1]).then_inc(s["ss_sm"], 1)
                dve.wait_ge(s["ss_exp"], g + 1)
                link(dve.reciprocal(rinv[:, 0, g:g + 1], rsum[:, 0, g:g + 1]))
                link(dve.tensor_scalar(hmr[:, g, :], row_head, rinv[:, 0, g:g + 1], None, ALU.mult))
                dve.wait_ge(s["sv_mm"], g + 1)
                tt(osel[:, g, :].rearrange("p (h d) -> p h d", h=HEADS), ps[:, 5, :].rearrange("p (h d) -> p h d", h=HEADS),
                   hmr[:, g, :].unsqueeze(2).broadcast_to([P, HEADS, HD]), ALU.mult).then_inc(s["sv_o"], 1)
            dve.wait_ge(s["so_mm"], 1)
            dve.tensor_copy(attT[:, :, SEQ:NT], ps[:, 6, 0:128].rearrange("p (j n) -> p j n", j=4)).then_inc(s["so_ev"], 1)

            evac("glu", lambda i, half: tt(two(one(mixed, i)), pair(half, 0), two(sg[:, half, :]), ALU.mult), 22)
            dve.wait_ge(s["evac"], EV0 + first_tile["gs"])
            evac("gs", lambda i, half: tt(two(one(mixed, i)), two(one(mixed, i)), two(sg[:, half, :]), ALU.mult), 30)
            dve.wait_ge(s["evac"], EV0 + first_tile["ga_att"])

            def add_att(i, half):
                tt(two(sg[:, half, :]), pair(half, 1), two(sg[:, half, :]), ALU.mult).then_inc(s["att_gated"], 1)
                dve.wait_ge(s["att_gated"], i + 1)
                return tt(one(mixed, i), one(mixed, i), sg[:, half, :], ALU.add)
            evac("ga_att", add_att, 38)
            evac("out", lambda i, half: tt(two(one(hT, i)), pair(half, 0), two(one(hT, i)), ALU.add))
            norm(2)
            evac("ffn2_in", glu_out, 46)
            evac("ffn2_out", add_half)
            norm(3)
            for k in range(5):
                m = P if k < 4 else 32
                bk = 2 + 2 * (k % 2)
                dve.wait_ge(s["yt_t"], k + 1)
                dve.tensor_copy(ytok[0:m, k, :].rearrange("p (b n) -> p b n", b=2), ps[0:m, bk:bk + 2, :]).then_inc(s["yt_ev"], 1)


INPUTS = ["x_prompt", "x_sample", "cache_k", "cache_v", "cache_kidx", "state_s5_re", "state_s5_im", "page_table",
          "g_ffn1", "w_ffn1_in", "w_ffn1_out", "g_mix", "w_in", "s5_lam_re", "s5_lam_im", "s5_log_dt",
          "s5_b_re", "s5_b_im", "s5_c_re", "s5_c_im", "s5_d", "w_s5_glu", "w_att_proj", "rel_bias", "w_out",
          "g_ffn2", "w_ffn2_in", "w_ffn2_out", "g_final"]
OUTPUTS = [("y_prompt", (1, SEQ, D)), ("y_sample", (NB, NS, D)),
           ("k_prompt", (1, 1, SEQ, HEADS, HD)), ("v_prompt", (1, 1, SEQ, HEADS, HD)), ("kidx_prompt", (1, 1, SEQ, ID)),
           ("s5_re_prompt", (1, 1, G, ST)), ("s5_im_prompt", (1, 1, G, ST)),
           ("k_sample", (1, NB, NS, HEADS, HD)), ("v_sample", (1, NB, NS, HEADS, HD)), ("kidx_sample", (1, NB, NS, ID)),
           ("s5_re_sample", (1, NB, G, ST)), ("s5_im_sample", (1, NB, G, ST))]


def kernel(**inputs):
    import concourse.bacc as _bacc
    from concourse.bass_utils import run_bass_kernel_spmd as _run

    nc = _bacc.Bacc("TRN2", target_bir_lowering=False, num_devices=1)
    arrays, t, out = {}, {}, {}
    data = {n: np.ascontiguousarray(inputs[n]) for n in INPUTS}
    data.update(shape_constants())
    for n, a in data.items():
        arrays["in_" + n] = a
        t[n] = nc.dram_tensor("in_" + n, a.shape, mybir.dt.from_np(a.dtype), kind="ExternalInput").ap()
    for n, shape in OUTPUTS:
        out[n] = nc.dram_tensor("out_" + n, shape, F32, kind="ExternalOutput").ap()
    build(nc, t, out)
    r = _run(nc, [arrays], core_ids=[0])
    return tuple(r.results[0]["out_" + n] for n, _ in OUTPUTS)
```

```python
from contextlib import ExitStack
import math

import numpy as np
import concourse.bass as bass
from concourse import mybir

F32 = mybir.dt.float32
F32R = mybir.dt.float32r
BF16 = mybir.dt.bfloat16
I32 = mybir.dt.int32
ALU = mybir.AluOpType
ACT = mybir.ActivationFunctionType
AX = mybir.AxisListType

P = 128
D = 1024
DK = D // P
SEQ, NB, NS = 512, 8, 4
NT = SEQ + NB * NS
HALF = NT // 2
FF = 2816
FK = FF // P
HEADS, HD = 8, 64
IH, ID = 8, 32
TOPK_P, TOPK_S = SEQ // 4, 256
PAST, PAGE = 1024, 128
NPAGE = PAST // PAGE
NKEY = PAST + NB * NS
G, GC, ST = 32, 16, 64
GP = G // 2
CH = 8
NC = SEQ // CH
UC = NC + NB
NBKT = 32
EPS = 1e-6
MASK = -1e30
TAKEN = -3e38
C_U, C_Q, C_K, C_V, C_QI = 0, 512, 1024, 1536, 2048
NQI = IH * ID + ID + IH
C_GS, C_GA = C_QI + NQI, C_QI + NQI + D


def bucket(dist):
    d = np.maximum(dist, 0)
    nf = np.maximum(d, 1).astype(np.float32)
    large = 16 + (np.log(nf / np.float32(16)) / np.float32(math.log(8.0)) * np.float32(16) + np.float32(1e-5)).astype(np.int32)
    return np.where(d < 16, d, np.minimum(large, NBKT - 1))


def shape_constants():
    c = {}
    c["ident"] = np.eye(P, dtype=np.float32)
    y = np.arange(640)
    c["oh_prompt"] = (bucket(511 - y)[None, :] == np.arange(NBKT)[:, None]).astype(np.float32)
    s = np.arange(PAST)
    oh = np.zeros((NS, NBKT, NKEY), np.float32)
    for q in range(NS):
        oh[q, bucket(PAST + q - s), s] = 1
        oh[q, bucket(q - np.arange(NB * NS) % NS), PAST + np.arange(NB * NS)] = 1
    c["oh_sample"] = oh.reshape(P, NKEY)
    q_of = np.arange(P) % NS
    c["same_step"] = (np.repeat(np.arange(NS), NBKT)[:, None] == q_of[None, :]).astype(np.float32)
    row_b, row_h = np.arange(P) // 32, np.arange(P) // NS % HEADS
    tok = np.arange(NB * NS)
    for g in range(2):
        c[f"row_tok{g}"] = ((row_b + 4 * g)[:, None] * NS + q_of[:, None] == tok[None, :]).astype(np.float32)
        c[f"tok_row{g}"] = np.ascontiguousarray(c[f"row_tok{g}"].T)
    c["row_head"] = (row_h[:, None] == np.arange(HEADS)[None, :]).astype(np.float32)
    c["head_row"] = np.ascontiguousarray(c["row_head"].T)
    c["causal"] = np.where(np.arange(P)[None, :] <= np.arange(P)[:, None], 0, MASK).astype(np.float32)
    ok = (tok[:, None] // NS == tok[None, :] // NS) & (tok[None, :] <= tok[:, None])
    c["new_mask"] = np.where(ok, 0, MASK).astype(np.float32)
    return c


def build(nc, t, out):
    ctx = ExitStack()
    with ctx:
        def sb(name, shape, dt=F32):
            return ctx.enter_context(nc.sbuf_tensor(name, shape, dt))

        def sem(name):
            return ctx.enter_context(nc.semaphore(name))

        def one(ap3, i):
            return ap3[:, bass.ds(i, 1), :].rearrange("p a n -> p (a n)")

        hT = sb("hT", [P, DK, NT])
        biasmem = sb("biasmem", [P, HEADS * SEQ + NKEY])
        kvtok = sb("kvtok", [P, 2, 5, 512])
        qkT = sb("qkT", [P, 2, 4, NT])
        qiT = sb("qiT", [P, 2, SEQ])
        kiT = sb("kiT", [P, NT])
        sg = sb("sg", [P, 2, NT])
        rstd = sb("rstd", [P, NT])
        ki4 = sb("ki4", [P, 5, 4, ID])
        qis = sb("qis", [P, NB, IH, NS])
        qbd = sb("qbd", [P, 4, NB, HEADS * NS])
        ident = sb("ident_sb", [P, P])
        identb = sb("identb", [P, P], BF16)
        causb = sb("causb", [P, P], BF16)
        caus = sb("caus", [P, P])
        ones = sb("ones", [P, P])
        gains = sb("gains", [P, 4, DK])
        epsc = sb("epsc", [P, 1])
        wtok = sb("wtok", [P, 4, IH])
        s0 = sb("s0", [P, 2, NB, GP])
        apow = sb("apow", [P, 9, 2, GP])
        cpow = sb("cpow", [P, 9, 2, GP])
        tiny = sb("tiny", [P, 64])
        pt_sb = sb("pt_sb", [1, NB * NPAGE], I32)
        ps = ctx.enter_context(nc.psum_tensor("ps", [P, 8, 512], F32))

        with ExitStack() as ends:
            ends.enter_context(nc.sbuf_tensor("below_ends", [P, 2 * DK * NT], F32))
            xmem = ends.enter_context(nc.sbuf_tensor("xmem", [P, 8064], F32))
        with ExitStack() as ffn:
            def fb(name, shape, dt=F32R):
                return ffn.enter_context(nc.sbuf_tensor(name, shape, dt))
            hnh, hnl = fb("hn_high", [P, DK, NT]), fb("hn_low", [P, DK, NT])
            acth, actl = fb("act_high", [P, 8, NT]), fb("act_low", [P, 8, NT])
            wraw = fb("wraw", [P, 4, DK, P], F32)
            wh, wl = fb("w_high", [P, 2, DK, P]), fb("w_low", [P, 2, DK, P])
        with ExitStack() as norm_mem:
            norm_mem.enter_context(nc.sbuf_tensor("below_norm", [P, DK * NT], F32))
            nrm = norm_mem.enter_context(nc.sbuf_tensor("nrm", [P, DK, NT], F32))
        hn = sb("hn", [P, DK, NT])
        wslot = sb("wslot", [P, 2, DK * NQI])
        big = sb("big", [P, 10496])
        uv = sb("uv", [P, 2, G * UC])
        idxm = sb("idxm", [P, 2160])

        tb = biasmem[:, 0:HEADS * SEQ].rearrange("p (h n) -> p h n", h=HEADS)
        bs = biasmem[:, HEADS * SEQ:]
        ktok, vtok = kvtok[:, 0], kvtok[:, 1]
        qT, kT = qkT[:, 0], qkT[:, 1]
        xtok = xmem[:, 0:5 * D].rearrange("p (t d) -> p t d", t=5)
        yre = biasmem[:, 0:2304].rearrange("p (g k i) -> p g k i", g=GP, k=9)
        yim = biasmem[:, 2304:4608].rearrange("p (g k i) -> p g k i", g=GP, k=9)
        wb = kvtok[:, :, :, :].rearrange("p a b c -> p (a b c)")[:, 0:4096].rearrange(
            "p (c g t j) -> p c g t j", c=2, g=GP, t=CH)
        toep = big[:, 0:4096].rearrange("p (g n) -> p g n", g=G)
        gb = big[:, 4096:8192].rearrange("p (c g n) -> p c g n", c=2, g=GP)
        ych = big[:, 8192:8192 + G * UC].rearrange("p (g c) -> p g c", g=G)
        kbuf = big[:, 8192:10240].rearrange("p (b g n) -> p b g n", b=2, g=8)
        uch = uv[:, 0].rearrange("p (g c) -> p g c", g=G)
        vst = uv[:, 1].rearrange("p (c g n) -> p c g n", c=2, g=GP)
        uT = uv[:, 1, 0:4 * NT].rearrange("p (t n) -> p t n", t=4)
        yT = uv[:, 1, 0:4 * NT].rearrange("p (t n) -> p t n", t=4)
        gT = uv[:, 0, 0:4 * NT].rearrange("p (t n) -> p t n", t=4)
        early = qkT[:, :, :, :].rearrange("p a b c -> p (a b c)")
        lam = early[:, 0:32].rearrange("p (c g) -> p c g", c=2)
        ldt = early[:, 32:48]
        s5v = early[:, 48:48 + 16 * 20].rearrange("p (k g) -> p k g", k=20)
        bmat = early[:, 512:1024].rearrange("p (c g j) -> p c g j", c=2, g=GP)
        bbar = early[:, 1024:1536].rearrange("p (c g j) -> p c g j", c=2, g=GP)
        craw = early[:, 1536:2560].rearrange("p (c t n) -> p c t n", c=2, t=4)
        cT = early[:, 2560:3072].rearrange("p (c g i) -> p c g i", c=2, g=GP)
        s0raw = early[:, 3072:3328].rearrange("p (c n) -> p c n", c=2)
        dd = early[0:GC, 3328:3840].rearrange("p (g i) -> p g i", g=G)
        s5q = early[:, 3840:4096].rearrange("p (k m g) -> p k m g", k=4, m=4)
        pt1, pt2, pt3, pt4 = (kvtok[:, :, :, :].rearrange("p a b c -> p (a b c)")[:, 4096 + 256 * k:4352 + 256 * k]
                              .rearrange("p (g j) -> p g j", g=GP) for k in range(4))
        sgf = sg[:, :, :].rearrange("p a n -> p (a n)")
        fin_s = sgf[:, 0:256].rearrange("p (c b g) -> p c b g", c=2, b=NB)
        fin_p = sgf[:, 256:288].rearrange("p (c g) -> p c g", c=2)
        prodmem = sgf[:, 288:800]
        fin_t = ki4[:, :, :, :].rearrange("p a b c -> p (a b c)")[:, 0:512]
        ohp = xmem[:, 5120:5760]
        relb = tiny[0:NBKT, 0:HEADS]
        relrep = xmem[:, 5760:6784].rearrange("p (h n) -> p h n", h=HEADS)
        shrow = xmem[:, 6784:6784 + 1280].rearrange("p (b n) -> p b n", b=2)
        nmx = tiny[:, 8:10]
        rsum = tiny[:, 16:32].rearrange("p (a h) -> p a h", a=2)
        rinv = tiny[:, 32:48].rearrange("p (a h) -> p a h", a=2)
        top8 = tiny[:, 48:56]
        topwait = tiny[:, 56:57]

        def v(k):
            return s5v[:, k, :]

        mixed = big[:, 0:DK * NT].rearrange("p (m n) -> p m n", m=DK)
        base = DK * NT
        sc = idxm[:, 0:512]
        rl = idxm[:, 512:1536].rearrange("p (b n) -> p b n", b=2)
        selq = [None] + [idxm[:, 1584 + a // 2:1584 + (a + w) // 2].bitcast(BF16) for a, w in ((0, 256), (256, 384), (640, 512))]
        smx = big[:, base:base + 1024].rearrange("p (b n) -> p b n", b=2)
        pexp = big[:, base + 1024:base + 2048].rearrange("p (b n) -> p b n", b=2)
        pT = big[:, base + 2048:base + 3072].rearrange("p (b n) -> p b n", b=2)
        ao = big[:, base + 3072:base + 4096].rearrange("p (b n) -> p b n", b=2)
        attT = kvtok[:, 0, :, :].rearrange("p a b -> p (a b)")[:, 0:4 * NT].rearrange("p (j n) -> p j n", j=4)
        kring = big[:, 8448:10496].rearrange("p (r n) -> p r n", r=4)
        kidx = big[:, 4352:6400].rearrange("p (n d) -> p n d", d=ID)
        kxT = big[:, 6400:6912].rearrange("p (b n) -> p b n", b=2)
        rls = big[:, 6912:6912 + NKEY]
        scs = idxm[0:32, 0:NKEY]
        sels = idxm[0:32, 1056:1056 + NKEY // 2].bitcast(BF16)
        ohs = uv[:, 1, 1024:1024 + NKEY]
        pgT = uv[:, 1, 0:1024].rearrange("p (b n) -> p b n", b=2)
        sms = big[:, base:base + NKEY]
        pes = big[:, base + 1056:base + 1056 + NKEY]
        ptS = big[:, base + 2112:base + 2112 + 9 * P].rearrange("p (k n) -> p k n", k=9)
        osel = sg[:, :, 0:512]
        qis4 = sg[0:32, :, :].rearrange("p a b -> p (a b)")[:, 0:IH * 4 * ID].rearrange("p (h r d) -> p h r d", h=IH, r=4)
        row_tok = rstd[:, 0:64].rearrange("p (g n) -> p g n", g=2)
        row_head = rstd[:, 64:72]
        head_row = rstd[0:8, 72:200]
        wT8 = rstd[0:8, 512:544]
        wsel = rstd[:, 232:296].rearrange("p (g n) -> p g n", g=2)
        new_mask = rstd[0:32, 296:328]
        tok_row = rstd[0:32, 328:456].bitcast(BF16).rearrange("p (g n) -> p g n", g=2)
        rb4 = rstd[:, 456:464]
        hmr = rstd[:, 464:480].rearrange("p (g h) -> p g h", g=2)
        same_step = wslot[:, 0, 2048:2176]
        rbexp = wslot[:, 0, 2176:2304]
        tok_row_f = wslot[0:32, 1, 2048:2304].rearrange("p (g n) -> p g n", g=2)
        ytok = xmem[:, 0:5 * D].rearrange("p (t d) -> p t d", t=5)

        scr_shift = nc.dram_tensor("scr_shift", [HEADS, P, 640], F32, kind="Internal").ap()
        scr_u = nc.dram_tensor("scr_u", [CH, 4, P, NC], F32, kind="Internal").ap()
        scr_us = nc.dram_tensor("scr_us", [NS, 4, P, NB], F32, kind="Internal").ap()
        scr_y = nc.dram_tensor("scr_y", [G, GC, CH, NC], F32, kind="Internal").ap()
        scr_ys = nc.dram_tensor("scr_ys", [G, GC, NS, NB], F32, kind="Internal").ap()

        s = {n: sem(n) for n in (
            "x_in", "const_in", "par_in", "x_turned", "oh_in", "shift_mm", "relrep",
            "pool_const", "early_pe", "shift_ev", "kidx_out", "kv_out", "early_act", "dt_done", "ang_done", "trig_done", "pow_done", "mm_done", "evac",
            "gate_done", "sq_done", "ssum_done", "sqrt_done", "norm_done", "dve_step", "pool_step", "bf_done",
            "prep_done", "gbt", "gb_ev", "km", "k_ev", "tz_zero", "u_zero", "u_out", "u_in", "ud_done", "kt_t", "kt_ev",
            "vmm", "v_ev", "unit_done", "hi_done", "lo_done", "ffn_ev", "silu_done", "mul_done", "acth_done", "act_ready", "nrm_done", "hnh_done", "vcopy_done", "pool_gated", "scan_done", "ymm", "y_ev", "y_out", "y_in", "fin_ready", "fin_mm", "fin_ev", "gelu_done",
            "bias_in", "res_out", "ix_mm", "ix_relu", "ix_acc", "topk", "sx_got", "bs_ev", "ktk_t", "ktk_ev", "sel_done", "at_s", "at_sm", "at_exp", "at_t",
            "at_tc", "at_pv", "at_o", "at_ot", "at_otc", "sc_in", "ohs_in", "bs_mm", "sm_prep", "sm_pe", "sm_b", "kidx_in", "sx_t", "sx_tc",
            "sx_mm", "sx_relu", "sx_w", "sx_sel", "kv_used", "kp_t", "kp_tc", "kp_s", "ss_mm", "ss_sm", "ss_exp", "sp_t",
            "sp_tc", "sv_mm", "sv_o", "so_mm", "so_ev", "att_gated", "yt_t", "yt_ev")}
        s["shift_out"] = [sem(f"shift_out{i}") for i in range(2)]
        s["toep_in"] = [sem(f"toep_in{i}") for i in range(2)]
        raw_in = [sem(f"raw_in{i}") for i in range(4)]
        w_ready = [sem(f"w_ready{i}") for i in range(2)]
        kv_in = [sem(f"kv_in{i}") for i in range(4)]

        LAYERS = [("idx", 1, 1), ("uq", 8, 1), ("kv", 4, 1), ("glu", 8, 2), ("gs", 8, 1), ("ga_att", 8, 2), ("out", 8, 1)]
        first_tile, slot_base, n_, sl_ = {}, {}, 0, [0, 0]
        for name, cnt, d_ in LAYERS:
            first_tile[name], slot_base[name] = n_, list(sl_)
            for k_ in range(cnt):
                sl_[(n_ + k_) % 2] += 16 * d_
            n_ += cnt
        EV0 = DK

        GROUPS = [(0, 8), (8, 8), (16, 6)]
        FFN_UNITS = sum(2 * m + DK for _, m in GROUPS)
        FFN_TILES = sum(m + DK for _, m in GROUPS)
        assert sum(m for _, m in GROUPS) == FK and all(2 * m % 4 == 0 for _, m in GROUPS)
        FE0 = 4

        def ffn_plan(which):
            u, tl, g_ = FFN_UNITS * which, FFN_TILES * which, 0
            for f0, m in GROUPS:
                yield "in", f0, m, u, tl, FK * which + g_
                u, tl, g_ = u + 2 * m, tl + m, g_ + m
                yield "out", f0, m, u, tl, FK * which + g_
                u, tl = u + DK, tl + DK

        def tiles(eng, name, body):
            n0, (_, cnt, d) = first_tile[name], next(l for l in LAYERS if l[0] == name)
            def step(i2, j, i):
                slot = (n0 + j) % 2
                body(i, slot, i + n0, slot_base[name][slot] + (i2 + 1) * (16 * d))
            if cnt > 2:
                with eng.Fori(0, cnt // 2) as r:
                    for j in range(2):
                        step(r, j, r * 2 + j)
            else:
                for i in range(cnt):
                    step(i // 2, i % 2, i)

        def slot_half(layer, slot):
            return slot

        ctx.enter_context(nc.allow_non_contiguous_dma(reason="small parameters"))
        def free_at_norm(k):
            return [(s["evac"], EV0), (s["ffn_ev"], FE0 + FFN_TILES), (s["evac"], EV0 + ALLT), (s["ffn_ev"], FE0 + 2 * FFN_TILES)][k]

        block = ctx.enter_context(nc.Block())


        MM0 = DK
        ALLT = n_

        @block.sync
        def _(sp):
            sp.dma_start(ohp[0:NBKT, :], t["oh_prompt"]).then_inc(s["oh_in"], 16)
            sp.dma_start(relb, t["rel_bias"]).then_inc(s["oh_in"], 16)
            sp.dma_start(xtok[:, 0:4, :], t["x_prompt"][0].rearrange("(t p) d -> p t d", p=P)).then_inc(s["x_in"], 16)
            sp.dma_start(xtok[0:32, 4, :], t["x_sample"].rearrange("b s d -> (b s) d")).then_inc(s["x_in"], 16)
            sp.dma_start(ident[:], t["ident"]).then_inc(s["const_in"], 16)
            sp.dma_start(caus[:], t["causal"]).then_inc(s["const_in"], 16)
            for k, n in enumerate(("g_ffn1", "g_mix", "g_ffn2", "g_final")):
                src = t[n] if n == "g_final" else t[n][0]
                sp.dma_start(gains[:, k, :], src.rearrange("(k p) -> p k", p=P)).then_inc(s["const_in"], 16)
            sp.dma_start(pt_sb[:], t["page_table"].rearrange("b (o n) -> o (b n)", o=1)).then_inc(s["const_in"], 16)
            for c, n in enumerate(("s5_lam_re", "s5_lam_im")):
                sp.dma_start(lam[:, c, :], t[n][0].rearrange("(g s) p -> (s p) g", s=2)).then_inc(s["par_in"], 16)
            for h in range(2):
                sp.dma_start(ldt[64 * h:64 * h + 64, :], t["s5_log_dt"][0].rearrange("(g s) -> s g", s=2)[h:h + 1, :]
                             .broadcast_to([64, GP])).then_inc(s["par_in"], 16)
            for c, n in enumerate(("s5_b_re", "s5_b_im")):
                sp.dma_start(bmat[:, c, :, :], t[n][0].rearrange("(g s) p j -> (s p) g j", s=2)).then_inc(s["par_in"], 16)
            for c, n in enumerate(("s5_c_re", "s5_c_im")):
                for h in range(2):
                    sp.dma_start(craw[:, c, :, 64 * h:64 * h + 64],
                                 t[n][0].rearrange("g i p -> (g i) p").rearrange("(t q) p -> q t p", q=P)).then_inc(s["par_in"], 16)
            for c, n in enumerate(("state_s5_re", "state_s5_im")):
                sp.dma_start(s0raw[:, c, :], t[n][0].rearrange("b (g s) p -> (b g) (s p)", s=2)).then_inc(s["par_in"], 16)
            sp.dma_start(dd.rearrange("p g i -> p (g i)"), t["s5_d"].broadcast_to([GC, G * GC])).then_inc(s["par_in"], 16)

            def load(layer, *parts):
                def body(i, slot, n, ready):
                    sp.wait_ge(s["mm_done"], n + (MM0 - 1))
                    for at, w, c0, width in parts:
                        kb = w.shape[1]
                        dst = wslot[:, slot, at * P:at * P + kb * width].rearrange("p (k n) -> p k n", k=kb)
                        sp.dma_start(dst, w[:, :, bass.ds(i * width + c0, width)]).then_inc(w_ready[slot], 16)
                tiles(sp, layer, body)

            def load_ffn(which, w_in, w_out):
                for kind, f0, m, u0, t0, a0 in ffn_plan(which):
                    steps = m // 2 if kind == "in" else 2
                    with sp.Fori(0, steps) as i:
                        for j in range(4):
                            sp.wait_ge(s["lo_done"], i * 4 + (u0 + j + FE0 - 3))
                            if kind == "in":
                                c0 = P * (f0 + j // 2) + FF * (j % 2)
                                sp.dma_start(wraw[:, j, :, :], w_in[:, :, bass.ds(i * (2 * P) + c0, P)]).then_inc(raw_in[j], 16)
                            else:
                                sp.dma_start(wraw[:, j, 0:m, :], w_out[:, f0:f0 + m, bass.ds(i * (4 * P) + j * P, P)]).then_inc(raw_in[j], 16)

            rows = lambda n: t[n][0].rearrange("(k p) n -> p k n", p=P)
            for h in range(HEADS):
                sp.wait_ge(s["shift_ev"], h + 1)
                sp.dma_start(scr_shift[h], shrow[:, h % 2, :]).then_inc(s["shift_out"][h % 2], 16)
            load_ffn(0, rows("w_ffn1_in"), rows("w_ffn1_out"))
            sp.wait_ge(s["tz_zero"], 1)
            for r in range(4):
                sp.wait_ge(s["k_ev"], r + 1)
                for k in range(CH):
                    sp.dma_start(toep[16 * k:16 * k + 16, 8 * r:8 * r + 8, 16 * k:P],
                                 kbuf[0:16, r % 2, :, 0:P - 16 * k]).then_inc(s["toep_in"][r % 2], 16)
            sp.wait_ge(s["unit_done"], FFN_UNITS)
            load("idx", (0, rows("w_in"), C_QI, NQI))
            load("uq", (0, rows("w_in"), C_U, P))
            load("kv", (0, rows("w_in"), C_K, 256))
            sp.wait_ge(s["evac"], EV0 + first_tile["uq"])
            sp.dma_start(out["kidx_prompt"][0, 0].rearrange("(t p) d -> p t d", p=P), ki4[:, 0:4, 0, :]).then_inc(s["kidx_out"], 16)
            sp.dma_start(out["kidx_sample"][0].rearrange("b s d -> (b s) d"), ki4[0:32, 4, 0, :]).then_inc(s["kidx_out"], 16)
            for g in range(2):
                sp.dma_start(row_tok[:, g, :], t[f"row_tok{g}"]).then_inc(s["sc_in"], 16)
                sp.dma_start(tok_row_f[:, g, :], t[f"tok_row{g}"]).then_inc(s["sc_in"], 16)
            sp.dma_start(row_head, t["row_head"]).then_inc(s["sc_in"], 16)
            sp.dma_start(head_row, t["head_row"]).then_inc(s["sc_in"], 16)
            sp.dma_start(new_mask, t["new_mask"]).then_inc(s["sc_in"], 16)
            sp.dma_start(same_step, t["same_step"]).then_inc(s["sc_in"], 16)
            for q in range(NS):
                sp.dma_start(rb4[32 * q:32 * q + 32, :], t["rel_bias"]).then_inc(s["sc_in"], 16)
            sp.wait_ge(s["vmm"], 4)
            sp.wait_ge(s["const_in"], 16 * 7)
            with sp.Fori(0, NB * NPAGE) as i:
                pg = sp.value_load(pt_sb[0:1, bass.ds(i, 1)], min_val=0, max_val=t["cache_kidx"].shape[1] - 1)
                sp.dma_start(one(kidx, i), t["cache_kidx"][0][bass.ds(pg, 1), :, :].rearrange("a p d -> p (a d)")).then_inc(s["kidx_in"], 16)
            sp.wait_ge(s["evac"], EV0 + first_tile["kv"] + 4)
            for a, n in ((ktok, "k"), (vtok, "v")):
                sp.dma_start(out[n + "_prompt"][0, 0].rearrange("(t p) h d -> p t (h d)", p=P), a[:, 0:4, :]).then_inc(s["kv_out"], 16)
                sp.dma_start(out[n + "_sample"][0].rearrange("b s h d -> (b s) (h d)"), a[0:32, 4, :]).then_inc(s["kv_out"], 16)
            sp.wait_ge(s["y_ev"], 8)
            for k in range(CH):
                sp.dma_start(scr_y[:, :, k, :].rearrange("g i n -> i g n"), ych[16 * k:16 * k + 16, :, 0:NC]).then_inc(s["y_out"], 16)
            for k in range(NS):
                sp.dma_start(scr_ys[:, :, k, :].rearrange("g i n -> i g n"), ych[64 + 16 * k:80 + 16 * k, :, NC:UC]).then_inc(s["y_out"], 16)
            sp.wait_ge(s["y_out"], 16 * 12)
            sp.dma_start(yT[:, :, 0:SEQ], scr_y.rearrange("g i k n -> (g i) (k n)").rearrange("(t q) n -> q t n", q=P)).then_inc(s["y_in"], 16)
            sp.dma_start(yT[:, :, SEQ:NT], scr_ys.rearrange("g i k n -> (g i) (k n)").rearrange("(t q) n -> q t n", q=P)).then_inc(s["y_in"], 16)
            load("glu", (0, rows("w_s5_glu"), 0, P), (4, rows("w_s5_glu"), D, P))
            sp.wait_ge(s["fin_ev"], 1)
            for c, n in enumerate(("s5_re", "s5_im")):
                sp.dma_start(out[n + "_sample"][0].rearrange("b (g s) p -> (b g) (s p)", s=2), fin_t[:, P * c:P * c + P]).then_inc(s["res_out"], 16)
                sp.dma_start(out[n + "_prompt"][0, 0].rearrange("(g s) p -> g (s p)", s=2),
                             fin_t[0:GP, 256 + P * c:384 + P * c]).then_inc(s["res_out"], 16)
            for k in range(2):
                sp.wait_ge(s["shift_out"][k], 16 * HEADS // 2)
            for h in range(HEADS):
                row = scr_shift[h].rearrange("p n -> (p n)")[127:127 + 639 * P].rearrange("(p n) -> p n", n=639)[:, 0:SEQ]
                sp.dma_start(tb[:, h, :], row).then_inc(s["bias_in"], 16)
            load("gs", (0, rows("w_in"), C_GS, P))
            sp.wait_ge(s["gelu_done"], 2)
            sp.dma_start(ohs, t["oh_sample"]).then_inc(s["ohs_in"], 16)
            for g in range(2):
                for c, n in enumerate(("cache_k", "cache_v")):
                    src = t[n][0].rearrange("n p h d -> n p (h d)")
                    with sp.Fori(0, 8) as i:
                        for r in range(4):
                            sp.wait_ge(s["kv_used"], i * 4 + (64 * g + 32 * c + r + 1))
                            pg = sp.value_load(pt_sb[0:1, bass.ds(i * 4 + (32 * g + r), 1)], min_val=0, max_val=src.shape[0] - 1)
                            sp.dma_start(kring[:, r, :], src[bass.ds(pg, 1), :, :].rearrange("a p d -> p (a d)")).then_inc(kv_in[r], 16)
            load("ga_att", (0, rows("w_in"), C_GA, P), (DK, rows("w_att_proj"), 0, P))
            load("out", (0, rows("w_out"), 0, P))
            sp.wait_ge(s["evac"], EV0 + first_tile["out"])
            load_ffn(1, rows("w_ffn2_in"), rows("w_ffn2_out"))
            for k in range(5):
                sp.wait_ge(s["yt_ev"], k + 1)
                if k < 4:
                    sp.dma_start(out["y_prompt"][0, P * k:P * k + P, :], ytok[:, k, :]).then_inc(s["res_out"], 16)
                else:
                    sp.dma_start(out["y_sample"].rearrange("b s d -> (b s) d"), ytok[0:32, 4, :]).then_inc(s["res_out"], 16)
            for done, count in (("kidx_out", 2), ("kv_out", 4), ("res_out", 4 + 5)):
                sp.wait_ge(s[done], 16 * count)

        @block.tensor
        def _(pe):
            def acc(dst, pairs, last_sem=None, **kw):
                for k, (a, b) in enumerate(pairs):
                    ins = pe.matmul(dst, a, b, start=(k == 0), stop=(k == len(pairs) - 1), **kw)
                return ins

            def slot_block(slot, k, m=P):
                return wslot[:, slot, k * P:k * P + m]

            def norm_sum(k):
                pe.wait_ge(*free_at_norm(k))
                src = hn if k == 1 else nrm
                for j in range(DK):
                    pe.wait_ge(s["sq_done"], DK * k + j + 1)
                    for h in range(2):
                        ins = pe.matmul(ps[:, h, 0:HALF], ones[:], src[:, j, h * HALF:(h + 1) * HALF],
                                        start=(j == 0), stop=(j == DK - 1), skip_group_check=True)
                ins.then_inc(s["ssum_done"], 1)

            def linear(layer, outs):
                def body(i, slot, n, ready):
                    half = slot_half(layer, slot)
                    pe.wait_ge(w_ready[slot], ready)
                    pe.wait_ge(s["evac"], n + (EV0 - 1))
                    for o, (k0, kb, x) in enumerate(outs):
                        for h in range(2):
                            ins = acc(ps[:, half * 4 + 2 * o + h, 0:HALF],
                                      [(slot_block(slot, k0 + k), x[:, k, h * HALF:(h + 1) * HALF]) for k in range(kb)])
                    ins.then_inc(s["mm_done"], 1)
                tiles(pe, layer, body)

            def ffn(which):
                def unit(j, w_at, x_hi, x_lo, kb, bank, first_wait=None):
                    for k in range(kb):
                        if first_wait is not None and k == kb - 1:
                            pe.wait_ge(*first_wait)
                        for a, x in ((wh, x_hi), (wh, x_lo), (wl, x_hi)):
                            for h in range(2):
                                ins = pe.matmul(ps[:, bank + h, 0:HALF], a[:, w_at, k, :], x[:, k, h * HALF:(h + 1) * HALF],
                                                start=(k == 0 and a is wh and x is x_hi), stop=(k == kb - 1 and a is wl),
                                                skip_group_check=True)
                    ins.then_inc(s["unit_done"], 1)

                for kind, f0, m, u0, t0, a0 in ffn_plan(which):
                    if kind == "in":
                        with pe.Fori(0, m // 2) as i:
                            for j in range(4):
                                pe.wait_ge(s["lo_done"], i * 4 + (u0 + j + FE0 + 1))
                                if j % 2 == 0:
                                    pe.wait_ge(s["ffn_ev"], i * 2 + (t0 + j // 2 + FE0 - 1))
                                unit(j, j % 2, hnh, hnl, DK, 4 * (j // 2) + 2 * (j % 2))
                    else:
                        pe.wait_ge(s["act_ready"], FE0 + a0 - 1)
                        with pe.Fori(0, 2) as i:
                            for j in range(4):
                                pe.wait_ge(s["lo_done"], i * 4 + (u0 + j + FE0 + 1))
                                pe.wait_ge(s["ffn_ev"], i * 4 + (t0 + j + FE0 - 1))
                                unit(j, j % 2, acth, actl, m, 4 * ((t0 + j) % 2), (s["act_ready"], FE0 + a0) if j == 0 else None)

            pe.wait_ge(s["relrep"], 1)
            pe.wait_ge(s["oh_in"], 32)
            for h in range(HEADS):
                if h:
                    pe.wait_ge(s["shift_ev"], h)
                for k in range(2):
                    ins = pe.matmul(ps[:, 6 + k, 0:320], relrep[0:NBKT, h, :], ohp[0:NBKT, 320 * k:320 * k + 320], start=True, stop=True)
                ins.then_inc(s["shift_mm"], 1)
            pe.wait_ge(s["x_in"], 32)
            pe.wait_ge(s["const_in"], 16 * 7)
            for k in range(DK):
                if k >= 2:
                    pe.wait_ge(s["evac"], k - 1)
                b = 4 * (k % 2)
                for j in range(4):
                    pe.transpose(ps[:, b, P * j:P * j + P], xtok[:, j, P * k:P * k + P], ident[:])
                pe.transpose(ps[:, b + 1, 0:32], xtok[0:32, 4, P * k:P * k + P], ident[0:32, 0:32]).then_inc(s["mm_done"], 1)
            pe.wait_ge(s["pool_const"], 1)
            norm_sum(0)
            pe.wait_ge(s["par_in"], 16 * 13)
            for c in range(2):
                for k in range(4):
                    pe.transpose(ps[:, 2 + c, P * k:P * k + P], craw[:, c, k, :], ident[:])
            for c in range(2):
                ins = pe.transpose(ps[:, 4, P * c:P * c + P], s0raw[:, c, :], ident[:])
            ins.then_inc(s["early_pe"], 1)
            pe.wait_ge(s["early_act"], 2)
            pe.wait_ge(s["norm_done"], DK)
            ffn(0)
            pe.wait_ge(s["ffn_ev"], FE0 + FFN_TILES)
            pe.wait_ge(s["prep_done"], 1)
            for r in range(8):
                c, g4 = r // 4, r % 4
                for q in range(4):
                    ins = pe.transpose(ps[:, r, P * q:P * q + P], wb[:, c, 4 * g4 + q, :, :].rearrange("p t j -> p (t j)"), ident[:])
                ins.then_inc(s["gbt"], 1)
            for r in range(4):
                pe.wait_ge(s["gb_ev"], 2 * (r % 2) + 2)
                if r >= 2:
                    pe.wait_ge(s["k_ev"], r - 1)
                for q in range(4):
                    gp = 4 * r + q
                    for h in range(2):
                        sl = slice(64 * h, 64 * h + 64)
                        ins = acc(ps[0:16, 2 * (r % 2) + h, P * q:P * q + P],
                                  [(bbar[sl, 0, gp, :], yre[sl, gp, 0:CH, :]), (bbar[sl, 1, gp, :], yim[sl, gp, 0:CH, :])])
                ins.then_inc(s["km"], 1)
            pe.wait_ge(s["gb_ev"], 8)
            pe.wait_ge(s["k_ev"], 4)
            norm_sum(1)
            pe.wait_ge(s["norm_done"], 2 * DK)
            def tok_out(tt):
                return slice(P * tt, P * tt + (P if tt < 4 else 32))

            def idx_body(i, slot, n, ready):
                pe.wait_ge(w_ready[slot], ready)
                w = wslot[:, slot, 0:DK * NQI].rearrange("p (k n) -> p k n", k=DK)
                b = 4 * slot
                for m in range(2):
                    acc(ps[:, b + m, :], [(w[:, k, P * m:P * m + P], hn[:, k, 0:SEQ]) for k in range(DK)])
                for tt in range(5):
                    m = P if tt < 4 else 32
                    acc(ps[0:m, b + 2, 40 * tt:40 * tt + 40], [(hn[:, k, tok_out(tt)], w[:, k, 256:296]) for k in range(DK)])
                acc(ps[0:32, b + 3, 0:256], [(hn[:, k, SEQ:NT], w[:, k, 0:256]) for k in range(DK)])
                acc(ps[0:8, b + 3, 256:288], [(w[:, k, 288:296], hn[:, k, SEQ:NT]) for k in range(DK)]).then_inc(s["mm_done"], 1)
            tiles(pe, "idx", idx_body)
            pe.wait_ge(s["evac"], EV0 + first_tile["uq"])

            def turn_tok(b, src):
                for tt in range(5):
                    m = P if tt < 4 else 32
                    dst = ps[:, b, P * tt:P * tt + P] if tt < 4 else ps[:, b + 1, 0:32]
                    ins = pe.transpose(dst, src(tt, m), ident[0:m, 0:m])
                return ins
            turn_tok(4, lambda tt, m: ki4[0:m, tt, :, :].rearrange("p r d -> p (r d)")).then_inc(s["kt_t"], 1)
            for h in range(IH):
                ins = pe.transpose(ps[:, 6, 32 * h:32 * h + 32], qis4[:, h, :, :].rearrange("p r d -> p (r d)"), ident[0:32, 0:32])
            ins.then_inc(s["kt_t"], 1)
            pe.wait_ge(s["kt_ev"], 2)
            for x in range(24):
                qb, h = 1 + x // 8, x % 8
                w = P * (qb + 1)
                r = slice(32 * (h % 4), 32 * (h % 4) + 32)
                if x >= 4:
                    pe.wait_ge(s["ix_relu"], x - 3)
                pe.matmul(ps[:, h % 4, 0:w], qiT[r, h // 4, P * qb:P * qb + P], kiT[r, 0:w], start=True, stop=True).then_inc(s["ix_mm"], 1)
            pe.wait_ge(s["ix_relu"], 24)
            linear("uq", [(0, DK, hn)])
            pe.wait_ge(s["evac"], EV0 + first_tile["kv"])

            pe.wait_ge(s["u_in"], 16 * (CH + NS))
            for q in range(4):
                for g4 in range(4):
                    gp = 4 * q + g4
                    for h in range(2):
                        for c in range(2):
                            ins = pe.matmul(ps[64 * h:64 * h + 64, 2 * q + c, UC * g4:UC * g4 + UC], gb[:, c, gp, 64 * h:64 * h + 64],
                                            uch[:, 2 * gp + h, :], start=True, stop=True)
                ins.then_inc(s["vmm"], 1)
            pe.wait_ge(s["v_ev"], 4)

            def kv_body(i, slot, n, ready):
                pe.wait_ge(w_ready[slot], ready)
                pe.wait_ge(s["evac"], n + (EV0 - 1))
                w = wslot[:, slot, 0:2048].rearrange("p (k n) -> p k n", k=DK)
                for tt in range(5):
                    m = P if tt < 4 else 32
                    ins = acc(ps[0:m, 4 * slot + tt // 2, 256 * (tt % 2):256 * (tt % 2) + 256],
                              [(hn[:, k, tok_out(tt)], w[:, k, :]) for k in range(DK)])
                ins.then_inc(s["mm_done"], 1)
            tiles(pe, "kv", kv_body)
            pe.wait_ge(s["evac"], EV0 + first_tile["glu"])
            for j in range(4):
                if j >= 2:
                    pe.wait_ge(s["ktk_ev"], j - 1)
                turn_tok(2 * (j % 2), lambda tt, m: ktok[0:m, tt, P * j:P * j + P]).then_inc(s["ktk_t"], 1)

            pe.wait_ge(s["toep_in"][0], 16 * 16)
            pe.wait_ge(s["toep_in"][1], 16 * 16)
            pe.wait_ge(s["ktk_ev"], 4)
            pe.wait_ge(s["scan_done"], 1)
            for q4 in range(4):
                for g8 in range(8):
                    g = 8 * q4 + g8
                    q, gp, sl, c0 = q4 + 4 * (g % 2), g // 2, slice(64 * (g % 2), 64 * (g % 2) + 64), UC * (g8 // 2)
                    pe.matmul(ps[:, q, c0:c0 + UC], toep[:, g, :], uch[:, g, :], start=True, stop=False, skip_group_check=True)
                    for c, y in enumerate((yre, yim)):
                        pe.matmul(ps[:, q, c0 + 1:c0 + NC], y[sl, gp, 1:9, :].rearrange("p k i -> p (k i)"), vst[sl, c, gp, 0:NC - 1],
                                  start=False, stop=False, skip_group_check=True)
                    for c, y in enumerate((yre, yim)):
                        ins = pe.matmul(ps[64:128, q, c0 + NC:c0 + UC], y[sl, gp, 1:5, :].rearrange("p k i -> p (k i)"), s0[sl, c, :, gp],
                                        start=False, stop=(c == 1), skip_group_check=True)
                ins.then_inc(s["ymm"], 1)
            pe.wait_ge(s["y_ev"], 2)
            for c in range(2):
                pe.transpose(ps[:, 0, P * c:P * c + P], fin_s[:, c, :, :].rearrange("p b g -> p (b g)"), ident[:])
                ins = pe.transpose(ps[0:GP, 0, 256 + P * c:384 + P * c], fin_p[:, c, :], ident[:])
            ins.then_inc(s["fin_mm"], 1)

            cols = [(0, 512), (512, 1024), (1024, NKEY)]
            pe.wait_ge(s["fin_ev"], 1)
            pe.wait_ge(s["y_ev"], 8)
            pe.wait_ge(s["sm_prep"], 1)
            pe.matmul(ps[:, 3, 0:32], head_row, wT8, start=True, stop=True).then_inc(s["sm_pe"], 1)
            pe.wait_ge(s["sm_b"], 1)
            pe.wait_ge(s["kidx_in"], 16 * NB * NPAGE)
            for b in range(NB):
                if b:
                    pe.wait_ge(s["sx_tc"], b)
                for k in range(2):
                    ins = pe.transpose(ps[:, 4, P * k:P * k + P], kidx[:, 8 * b + 4 * k:8 * b + 4 * k + 4, :].rearrange("p n d -> p (n d)"), ident[:])
                ins.then_inc(s["sx_t"], 1)
                pe.wait_ge(s["sx_tc"], b + 1)
                if b == 4:
                    pe.wait_ge(s["sx_relu"], 1)
                q = slice(32 * (b % 4), 32 * (b % 4) + 32)
                for k in range(NPAGE):
                    r = slice(32 * (k % 4), 32 * (k % 4) + 32)
                    ins = pe.matmul(ps[q, k % 4, P * (k // 4):P * (k // 4) + P], qis[r, b, :, :].rearrange("p h q -> p (h q)"),
                              kxT[r, b % 2, P * (k // 4):P * (k // 4) + P], start=True, stop=True, tile_position=(32 * (k % 4), 32 * (b % 4)))
                if b >= 4:
                    ins.then_inc(s["kv_used"], 1)
                pe.matmul(ps[q, 0, 256:288], qis[0:32, b, :, :].rearrange("p h q -> p (h q)"), kiT[0:32, SEQ:NT],
                          start=True, stop=True, tile_position=(0, 32 * (b % 4))).then_inc(s["sx_mm"], 1)
                if b % 4 == 3:
                    g = b // 4
                    pe.wait_ge(s["sx_relu"], g + 1)
                    for k, (c0, c1) in enumerate(cols):
                        ins = pe.matmul(ps[0:32, 5 + k, 0:c1 - c0], wsel[:, g, :], rls[:, c0:c1], start=(g == 0), stop=(g == 1))
                    ins.then_inc(s["sx_w"], 1)
            pe.wait_ge(s["gelu_done"], 2)
            pe.wait_ge(s["sx_got"], 1)
            linear("glu", [(0, 4, gT), (4, 4, gT)])
            linear("gs", [(0, DK, hn)])
            pe.wait_ge(s["evac"], EV0 + first_tile["ga_att"])
            pe.wait_ge(s["bf_done"], 2)
            def p_scores(x):
                qb, h = x // 8, x % 8
                w = P * (qb + 1)
                r = slice(64 * (h % 2), 64 * (h % 2) + 64)
                if x >= 2:
                    pe.wait_ge(s["at_sm"], x - 1)
                if h == 0 and qb:
                    pe.wait_ge(s["sel_done"], qb)
                pe.matmul(ps[:, x % 2, 0:w], identb[:], causb[:] if qb == 0 else selq[qb], start=True, stop=False)
                pe.matmul(ps[:, x % 2, 0:w], qT[r, h // 2, P * qb:P * qb + P], kT[r, h // 2, 0:w], start=False, stop=True).then_inc(s["at_s"], 1)

            def p_turn(x):
                qb = x // 8
                pe.wait_ge(s["at_exp"], x + 1)
                if x >= 2:
                    pe.wait_ge(s["at_tc"], x - 1)
                for k in range(qb + 1):
                    ins = pe.transpose(ps[:, 2 + x % 2, P * k:P * k + P], pexp[:, x % 2, P * k:P * k + P], ident[:])
                ins.then_inc(s["at_t"], 1)

            def p_values(x):
                qb, h = x // 8, x % 8
                pe.wait_ge(s["at_tc"], x + 1)
                if h == 0 and qb >= 2:
                    pe.wait_ge(s["at_o"], qb - 1)
                acc(ps[:, 4 + qb % 2, HD * h:HD * h + HD],
                    [(pT[:, x % 2, P * k:P * k + P], vtok[:, k, HD * h:HD * h + HD]) for k in range(qb + 1)]).then_inc(s["at_pv"], 1)

            def p_turn_out(qb):
                pe.wait_ge(s["at_o"], qb + 1)
                if qb >= 2:
                    pe.wait_ge(s["at_otc"], qb - 1)
                for j in range(4):
                    ins = pe.transpose(ps[:, 6 + qb % 2, P * j:P * j + P], ao[:, qb % 2, P * j:P * j + P], ident[:])
                ins.then_inc(s["at_ot"], 1)

            for x in range(34):
                if x < 32:
                    p_scores(x)
                if 1 <= x < 33:
                    p_turn(x - 1)
                if x >= 2:
                    p_values(x - 2)
                if x >= 2 and (x - 2) % 8 == 7:
                    p_turn_out((x - 2) // 8)

            pe.wait_ge(s["at_otc"], 4)
            pe.wait_ge(s["ohs_in"], 16)
            for b, (c0, c1) in enumerate(cols):
                ins = pe.matmul(ps[:, b, 0:c1 - c0], rbexp, ohs[:, c0:c1], start=True, stop=True)
            ins.then_inc(s["bs_mm"], 1)
            pe.wait_ge(s["bs_ev"], 1)
            pe.wait_ge(s["sx_sel"], 1)
            for g in range(2):
                if g:
                    pe.wait_ge(s["ss_sm"], g)
                for k, (c0, c1) in enumerate(cols):
                    pe.matmul(ps[:, k, 0:c1 - c0], tok_row[:, g, :], sels[:, c0:c1], start=True, stop=False, skip_group_check=True)
                for bl in range(4):
                    b = 4 * g + bl
                    q = slice(32 * bl, 32 * bl + 32)

                    for k in range(NPAGE):
                        n = 32 * g + 8 * bl + k
                        r = k % 4
                        pe.wait_ge(kv_in[r], 16 * (16 * g + (8 * bl + k) // 4 + 1))
                        if n >= 2:
                            pe.wait_ge(s["kp_tc"], n - 1)
                        for j in range(4):
                            ins = pe.transpose(ps[:, 3 + k % 2, P * j:P * j + P], kring[:, r, P * j:P * j + P], ident[:])
                        ins.then_inc(s["kp_t"], 1)
                        pe.wait_ge(s["kp_tc"], n + 1)
                        for j in range(4):
                            ins = pe.matmul(ps[q, k // 4, P * (k % 4):P * (k % 4) + P], qbd[:, j, b, :], pgT[:, k % 2, P * j:P * j + P],
                                            start=False, stop=False, skip_group_check=True)
                        ins.then_inc(s["kv_used"], 1)
                    for j in range(4):
                        ins = pe.matmul(ps[q, 2, 0:32], qbd[:, j, b, :], kT[:, j, SEQ:NT], start=False, stop=(j == 3), skip_group_check=True)
                    if bl == 3:
                        ins.then_inc(s["ss_mm"], 1)
                pe.wait_ge(s["ss_exp"], g + 1)
                if g:
                    pe.wait_ge(s["sp_tc"], g)
                    pe.wait_ge(s["sv_o"], g)
                for k in range(NPAGE):
                    pe.transpose(ps[:, 6 + k // 4, P * (k % 4):P * (k % 4) + P], pes[:, P * k:P * k + P], ident[:])
                pe.transpose(ps[0:32, 5, 0:P], pes[:, PAST:NKEY], ident[:]).then_inc(s["sp_t"], 1)
                pe.wait_ge(s["sp_tc"], g + 1)
                for bl in range(4):
                    q = slice(32 * bl, 32 * bl + 32)
                    for k in range(NPAGE):
                        r = k % 4
                        pe.wait_ge(kv_in[r], 16 * (16 * g + 8 + (8 * bl + k) // 4 + 1))
                        pe.matmul(ps[q, 5, :], ptS[:, k, q], kring[:, r, :], start=(k == 0), stop=False, skip_group_check=True).then_inc(s["kv_used"], 1)
                    ins = pe.matmul(ps[q, 5, :], ptS[0:32, 8, q], vtok[0:32, 4, :], start=False, stop=True, skip_group_check=True)
                ins.then_inc(s["sv_mm"], 1)
            pe.wait_ge(s["sv_o"], 2)
            for j in range(4):
                ins = acc(ps[:, 6, 32 * j:32 * j + 32], [(osel[:, g, P * j:P * j + P], row_tok[:, g, :]) for g in range(2)])
            ins.then_inc(s["so_mm"], 1)
            pe.wait_ge(s["so_ev"], 1)

            linear("ga_att", [(0, DK, hn), (DK, 4, attT)])
            pe.wait_ge(s["evac"], EV0 + first_tile["out"])
            linear("out", [(0, DK, mixed)])
            norm_sum(2)
            pe.wait_ge(s["norm_done"], 3 * DK)
            ffn(1)
            norm_sum(3)
            pe.wait_ge(s["norm_done"], 4 * DK)
            for k in range(5):
                m = P if k < 4 else 32
                if k >= 2:
                    pe.wait_ge(s["yt_ev"], k - 1)
                for j in range(DK):
                    ins = pe.transpose(ps[0:m, 2 + 2 * (k % 2) + j // 4, P * (j % 4):P * (j % 4) + P], nrm[:, j, P * k:P * k + m], ident[:])
                ins.then_inc(s["yt_t"], 1)

        @block.scalar
        def _(act_e):
            def squares(k):
                dst = hn if k == 1 else nrm
                if k:
                    act_e.wait_ge(*free_at_norm(k))
                for j in range(DK):
                    if k == 0:
                        act_e.wait_ge(s["evac"], j + 1)
                    act_e.activation(dst[:, j, :], hT[:, j, :], ACT.Square).then_inc(s["sq_done"], 1)

            def root(k):
                act_e.wait_ge(s["ssum_done"], k + 1)
                act_e.activation(rstd[:].rearrange("p (h n) -> p h n", h=2), ps[:, 0:2, 0:HALF], ACT.Sqrt, bias=epsc[:, 0:1],
                                 scale=1.0 / D).then_inc(s["sqrt_done"], 1)

            def two(ap):
                return ap.rearrange("p (h n) -> p h n", h=2)

            def pair(half, o):
                return ps[:, 4 * half + 2 * o:4 * half + 2 * o + 2, 0:HALF]

            def high(u, i, j):
                act_e.wait_ge(raw_in[j], i * 16 + 16 * (u // 4 + 1))
                if not (isinstance(i, int) and u + 4 * i < 2):
                    act_e.wait_ge(s["unit_done"], i * 4 + (u - 1))
                act_e.activation(wh[:, j % 2, :, :], wraw[:, j, :, :], ACT.Copy).then_inc(s["hi_done"], 1)

            def norm_high(which):
                for j in range(DK):
                    act_e.wait_ge(s["nrm_done"], DK * which + j + 1)
                    act_e.activation(hnh[:, j, :], nrm[:, j, :], ACT.Copy).then_inc(s["hnh_done"], 1)

            def ffn(which):
                end = FFN_UNITS * (which + 1)
                for j in range(2):
                    high(FFN_UNITS * which + j, 0, j)
                for kind, f0, m, u0, t0, a0 in ffn_plan(which):
                    if kind == "in":
                        with act_e.Fori(0, m // 2) as i:
                            for j in range(2):
                                high(u0 + 2 * j + 2, i, (2 * j + 2) % 4)
                                act_e.wait_ge(s["act_ready"], i * 2 + (a0 + j + FE0 - 1))
                                act_e.activation(two(sg[:, j, :]), pair(j, 0), ACT.Silu).then_inc(s["silu_done"], 1)
                                high(u0 + 2 * j + 3, i, (2 * j + 3) % 4)
                                act_e.wait_ge(s["ffn_ev"], i * 2 + (t0 + j + FE0 + 1))
                                act_e.activation(one(acth, i * 2 + j), sg[:, j, :], ACT.Copy).then_inc(s["acth_done"], 1)
                    elif u0 + DK < end:
                        with act_e.Fori(0, 2) as i:
                            for j in range(4):
                                high(u0 + j + 2, i, (j + 2) % 4)
                    else:
                        for j in range(DK - 2):
                            high(u0 + j + 2, 0, (j + 2) % 4)

            for h in range(HEADS):
                act_e.wait_ge(s["shift_mm"], h + 1)
                if h >= 2:
                    act_e.wait_ge(s["shift_out"][h % 2], 16 * (h // 2))
                act_e.activation(shrow[:, h % 2, :].rearrange("p (b n) -> p b n", b=2), ps[:, 6:8, 0:320], ACT.Copy).then_inc(s["shift_ev"], 1)
            act_e.wait_ge(s["pool_const"], 1)
            squares(0)
            act_e.wait_ge(s["par_in"], 16 * 13)
            act_e.activation(ldt, ldt, ACT.Exp).then_inc(s["dt_done"], 1)
            root(0)
            norm_high(0)
            act_e.wait_ge(s["early_pe"], 1)
            for c in range(2):
                for h in range(2):
                    src = ps[64 * h:64 * h + 64, 2 + c, :].rearrange("p (g s i) -> p g s i", s=2, i=GC)[:, :, h, :]
                    ins = act_e.activation(cT[64 * h:64 * h + 64, c, :, :], src, ACT.Copy, scale=1.0 if c == 0 else -1.0)
            ins.then_inc(s["early_act"], 1)
            act_e.activation(s0[:].rearrange("p c b g -> p (c b g)"), ps[:, 4, 0:256], ACT.Copy).then_inc(s["early_act"], 1)
            act_e.wait_ge(s["ang_done"], 1)
            act_e.activation(v(7), v(2), ACT.Sin).then_inc(s["trig_done"], 1)
            act_e.activation(v(8), v(2), ACT.Sin, scale=0.5).then_inc(s["trig_done"], 1)
            act_e.activation(v(4), v(1), ACT.Exp).then_inc(s["trig_done"], 1)
            ffn(0)
            for r in range(8):
                act_e.wait_ge(s["gbt"], r + 1)
                act_e.activation(gb[:, r // 4, 4 * (r % 4):4 * (r % 4) + 4, :].rearrange("p g n -> p (g n)"), ps[:, r, :], ACT.Copy).then_inc(s["gb_ev"], 1)
            squares(1)
            root(1)
            for x in range(24):
                w = P * (2 + x // 8)
                act_e.wait_ge(s["ix_mm"], x + 1)
                if x >= 2:
                    act_e.wait_ge(s["ix_acc"], x - 1)
                act_e.activation(rl[:, x % 2, 0:w], ps[:, x % 4, 0:w], ACT.Relu).then_inc(s["ix_relu"], 1)

            for i in range(4):
                n = first_tile["uq"] + i
                half = n % 2
                act_e.wait_ge(s["mm_done"], MM0 + n + 1)
                o = uT[:, i, 0:SEQ].rearrange("p (t n) -> p n t", t=CH)
                c = HALF // CH
                act_e.activation(o[:, 0:c, :], ps[:, 4 * half, 0:HALF].rearrange("p (n t) -> p n t", t=CH), ACT.Copy)
                act_e.activation(o[:, c:NC, :], ps[:, 4 * half + 1, 0:SEQ - HALF].rearrange("p (n t) -> p n t", t=CH), ACT.Copy)
                act_e.activation(uT[:, i, SEQ:NT].rearrange("p (t n) -> p n t", t=NS),
                                 ps[:, 4 * half + 1, SEQ - HALF:HALF].rearrange("p (n t) -> p n t", t=NS), ACT.Copy).then_inc(s["evac"], 1)
            act_e.wait_ge(s["evac"], EV0 + first_tile["uq"] + 4)
            for k in range(4):
                act_e.dma_start(scr_u[:, k].rearrange("t p n -> p t n"), uT[:, k, 0:SEQ].rearrange("p (t n) -> p t n", t=CH)).then_inc(s["u_out"], 16)
                act_e.dma_start(scr_us[:, k].rearrange("t p n -> p t n"), uT[:, k, SEQ:NT].rearrange("p (t n) -> p t n", t=NS)).then_inc(s["u_out"], 16)
            for i in range(4):
                n = first_tile["uq"] + 4 + i
                act_e.wait_ge(s["mm_done"], MM0 + n + 1)
                act_e.activation(two(qT[:, i, :]), pair(n % 2, 0), ACT.Copy, scale=HD ** -0.5).then_inc(s["evac"], 1)
                if i == 1:
                    act_e.wait_ge(s["u_out"], 16 * 8)
                    act_e.wait_ge(s["u_zero"], 1)
                    for k in range(CH):
                        act_e.dma_start(uch[16 * k:16 * k + 16, :, 0:NC], scr_u[k].rearrange("q (g c) n -> c (q g) n", c=GC)).then_inc(s["u_in"], 16)
                    for k in range(NS):
                        act_e.dma_start(uch[64 + 16 * k:80 + 16 * k, :, NC:UC], scr_us[k].rearrange("q (g c) n -> c (q g) n", c=GC)).then_inc(s["u_in"], 16)
            for q in range(4):
                act_e.wait_ge(s["vmm"], q + 1)
                for c in range(2):
                    ins = act_e.activation(vst[:, c, 4 * q:4 * q + 4, :].rearrange("p g n -> p (g n)"), ps[:, 2 * q + c, 0:4 * UC], ACT.Copy)
                ins.then_inc(s["v_ev"], 1)
            for i in range(4):
                n = first_tile["kv"] + i
                half, c0 = n % 2, 256 * (i % 2)
                dst = (ktok, vtok)[i // 2]
                act_e.wait_ge(s["mm_done"], MM0 + n + 1)
                act_e.activation(dst[:, 0:4, c0:c0 + 256].rearrange("p (a b) n -> p a b n", a=2),
                                 ps[:, 4 * half:4 * half + 2, :].rearrange("p a (b n) -> p a b n", b=2), ACT.Copy)
                act_e.activation(dst[0:32, 4, c0:c0 + 256], ps[0:32, 4 * half + 2, 0:256], ACT.Copy).then_inc(s["evac"], 1)
            for j in range(4):
                act_e.wait_ge(s["ktk_t"], j + 1)
                act_e.activation(kT[:, j, 0:SEQ], ps[:, 2 * (j % 2), :], ACT.Copy)
                act_e.activation(kT[:, j, SEQ:NT], ps[:, 2 * (j % 2) + 1, 0:32], ACT.Copy).then_inc(s["ktk_ev"], 1)
            for q in range(8):
                act_e.wait_ge(s["ymm"], q // 2 + 1)
                act_e.activation(ych[:, 8 * (q // 2) + q % 2:8 * (q // 2) + 8:2, :],
                                 ps[:, q // 2 + 4 * (q % 2), 0:4 * UC].rearrange("p (g n) -> p g n", g=4), ACT.Copy).then_inc(s["y_ev"], 1)
            act_e.wait_ge(s["fin_mm"], 1)
            act_e.wait_ge(s["kidx_out"], 32)
            act_e.activation(fin_t[:, 0:256], ps[:, 0, 0:256], ACT.Copy)
            act_e.activation(fin_t[0:GP, 256:512], ps[0:GP, 0, 256:512], ACT.Copy).then_inc(s["fin_ev"], 1)
            for g in range(2):
                act_e.wait_ge(s["sx_mm"], 4 * g + 4)
                if g:
                    act_e.wait_ge(s["sx_w"], g)
                for k in range(4):
                    act_e.activation(rls[:, 0:PAST].rearrange("p (j r n) -> p r j n", j=2, r=4)[:, k],
                                     ps[:, k, 0:256].rearrange("p (j n) -> p j n", j=2), ACT.Relu)
                act_e.activation(rls[:, PAST:NKEY], ps[:, 0, 256:288], ACT.Relu).then_inc(s["sx_relu"], 1)
                if g == 0:
                    act_e.wait_ge(s["y_in"], 32)
                    act_e.activation(gT[:, :, 0:SEQ].rearrange("p k (n t) -> p k n t", t=CH),
                                     yT[:, :, 0:SEQ].rearrange("p k (t n) -> p k n t", t=CH), ACT.Gelu_apprx_tanh).then_inc(s["gelu_done"], 1)
                    act_e.activation(gT[:, :, SEQ:NT].rearrange("p k (n t) -> p k n t", t=NS),
                                     yT[:, :, SEQ:NT].rearrange("p k (t n) -> p k n t", t=NS), ACT.Gelu_apprx_tanh).then_inc(s["gelu_done"], 1)

            def glu(i, slot, n, ready):
                act_e.wait_ge(s["mm_done"], n + (MM0 + 1))
                act_e.wait_ge(s["pool_gated"], i + 1)
                act_e.activation(two(sg[:, slot, :]), pair(slot, 1), ACT.Sigmoid)
                act_e.activation(two(one(mixed, i)), pair(slot, 0), ACT.Copy).then_inc(s["evac"], 1)
            tiles(act_e, "glu", glu)

            def gs(i, slot, n, ready):
                act_e.wait_ge(s["mm_done"], n + (MM0 + 1))
                act_e.wait_ge(s["pool_gated"], i + (8 + 1))
                act_e.activation(two(sg[:, slot, :]), pair(slot, 0), ACT.Sigmoid).then_inc(s["evac"], 1)
            tiles(act_e, "gs", gs)
            for x in range(33):
                if x < 32:
                    w = P * (1 + x // 8)
                    act_e.wait_ge(s["at_sm"], x + 1)
                    if x >= 2:
                        act_e.wait_ge(s["at_t"], x - 1)
                    if x % 8 == 0 and x >= 16:
                        act_e.wait_ge(s["at_o"], x // 8 - 1)
                    act_e.activation(pexp[:, x % 2, 0:w], smx[:, x % 2, 0:w], ACT.Exp, scale=-1.0, bias=nmx[:, x % 2:x % 2 + 1],
                                     accum_out=rsum[:, x // 8 % 2, x % 8:x % 8 + 1]).then_inc(s["at_exp"], 1)
                if x >= 1:
                    w = P * (1 + (x - 1) // 8)
                    act_e.wait_ge(s["at_t"], x)
                    if x >= 3:
                        act_e.wait_ge(s["at_pv"], x - 2)
                    act_e.activation(pT[:, (x - 1) % 2, 0:w], ps[:, 2 + (x - 1) % 2, 0:w], ACT.Copy).then_inc(s["at_tc"], 1)
            for g in range(2):
                with act_e.Fori(0, 16) as i:
                    for k in range(2):
                        act_e.wait_ge(s["kp_t"], i * 2 + (32 * g + k + 1))
                        act_e.wait_ge(s["kv_used"], i * 2 + (64 * g + k + 3))
                        act_e.activation(pgT[:, k, :], ps[:, 3 + k, :], ACT.Copy).then_inc(s["kp_tc"], 1)
                act_e.wait_ge(s["ss_sm"], g + 1)
                act_e.activation(pes, sms, ACT.Exp, scale=-1.0, bias=nmx[:, g:g + 1], accum_out=rsum[:, 0, g:g + 1]).then_inc(s["ss_exp"], 1)
                act_e.wait_ge(s["sp_t"], g + 1)
                if g:
                    act_e.wait_ge(s["sv_mm"], g)
                act_e.activation(ptS[:, 0:8, :].rearrange("p (b k) n -> p b (k n)", b=2), ps[:, 6:8, :], ACT.Copy)
                act_e.activation(ptS[0:32, 8, :], ps[0:32, 5, 0:P], ACT.Copy).then_inc(s["sp_tc"], 1)
            act_e.wait_ge(s["so_mm"], 1)
            act_e.wait_ge(s["pool_gated"], 2 + 16)

            def ga(i, slot, n, ready):
                act_e.wait_ge(s["mm_done"], n + (MM0 + 1))
                act_e.wait_ge(s["evac"], n + (EV0 - 1))
                act_e.activation(two(sg[:, slot, :]), pair(slot, 0), ACT.Sigmoid).then_inc(s["gate_done"], 1)
            tiles(act_e, "ga_att", ga)
            squares(2)
            root(2)
            norm_high(1)
            ffn(1)
            squares(3)
            root(3)

        @block.gpsimd
        def _(pool):
            pool.memset(ones[:], 1.0)
            pool.memset(epsc[:], EPS).then_inc(s["pool_const"], 1)
            pool.sem_inc(s["pool_gated"], 2)
            pool.wait_ge(s["oh_in"], 32)
            for h in range(HEADS):
                ins = pool.tensor_copy(relrep[0:NBKT, h, :], relb[:, h:h + 1].broadcast_to([NBKT, P]))
            ins.then_inc(s["relrep"], 1)
            pool.wait_ge(s["pow_done"], 1)
            pool.wait_ge(s["early_act"], 1)

            def product(n0, i, ar, ai, xr, xi, o_re, o_im, sub_re, sub_im):
                for o, a, b in ((pt1, xr, ar), (pt2, xi, ai), (pt3, xi, ar), (pt4, xr, ai)):
                    ins = pool.tensor_tensor(o, a, b, ALU.mult)
                    ins.then_inc(s["pool_step"], 1)
                pool.wait_ge(s["pool_step"], i * 6 + (n0 + 4))
                pool.tensor_tensor(o_re, pt1, pt2, sub_re).then_inc(s["pool_step"], 1)
                pool.tensor_tensor(o_im, pt3, pt4, sub_im).then_inc(s["pool_step"], 1)
                pool.wait_ge(s["pool_step"], i * 6 + (n0 + 6))

            def power(k, c):
                return apow[:, bass.ds(k, 1), c, :].rearrange("p a g -> p (a g)").unsqueeze(2).broadcast_to([P, GP, GC])

            def at_lag(a, k):
                return a[:, :, bass.ds(k, 1), :].rearrange("p g a i -> p g (a i)")
            with pool.Fori(0, 9) as k:
                product(0, k, power(k, 0), power(k, 1), cT[:, 0], cT[:, 1], at_lag(yre, k), at_lag(yim, k), ALU.add, ALU.subtract)
            with pool.Fori(0, CH) as k:
                product(54, k, power(k * -1 + 7, 0), power(k * -1 + 7, 1), bbar[:, 0], bbar[:, 1],
                        at_lag(wb[:, 0], k), at_lag(wb[:, 1], k), ALU.subtract, ALU.add)
            pool.sem_inc(s["prep_done"], 1)
            pool.wait_ge(s["unit_done"], FFN_UNITS)
            pool.memset(toep[:].rearrange("p g n -> p (g n)"), 0.0).then_inc(s["tz_zero"], 1)
            pool.memset(uch[0:64, :, NC:UC], 0.0).then_inc(s["u_zero"], 1)

            steps = [6 * (9 + CH)]

            def link(*ops):
                for ins in ops:
                    steps[0] += 1
                    ins.then_inc(s["pool_step"], 1)
                pool.wait_ge(s["pool_step"], steps[0])

            def advance(dst, src, a, shape):
                w = int(np.prod(shape))
                tm = [prodmem[:, w * k:w * (k + 1)] for k in range(4)]
                if len(shape) == 2:
                    tm = [x.rearrange("p (a b) -> p a b", a=shape[0]) for x in tm]
                tt = pool.tensor_tensor
                link(tt(tm[0], src[0], a[0], ALU.mult), tt(tm[1], src[1], a[1], ALU.mult),
                     tt(tm[2], src[0], a[1], ALU.mult), tt(tm[3], src[1], a[0], ALU.mult))
                link(tt(tm[0], tm[0], tm[1], ALU.subtract), tt(tm[2], tm[2], tm[3], ALU.add))
                link(tt(dst[0], dst[0], tm[0], ALU.add), tt(dst[1], dst[1], tm[2], ALU.add))

            pool.wait_ge(s["v_ev"], 4)
            pool.wait_ge(s["kt_ev"], 2)
            vb = vst[:, :, :, 0:NC].rearrange("p c g (b j) -> p c g b j", j=8)
            for j in range(1, 8):
                advance([vb[:, c, :, :, j] for c in range(2)], [vb[:, c, :, :, j - 1] for c in range(2)],
                        [cpow[:, 1, c, :].unsqueeze(2).broadcast_to([P, GP, 8]) for c in range(2)], (GP, 8))
            for b_ in range(1, 8):
                advance([vb[:, c, :, b_, 7] for c in range(2)], [vb[:, c, :, b_ - 1, 7] for c in range(2)],
                        [cpow[:, 8, c, :] for c in range(2)], (GP,))
            for j in range(7):
                advance([vb[:, c, :, 1:8, j] for c in range(2)], [vb[:, c, :, 0:7, 7] for c in range(2)],
                        [cpow[:, j + 1, c, :].unsqueeze(2).broadcast_to([P, GP, 7]) for c in range(2)], (GP, 7))
            link(*[pool.tensor_copy(fin_s[:, c, :, :], vst[:, c, :, NC:UC].rearrange("p g b -> p b g")) for c in range(2)],
                 *[pool.tensor_copy(fin_p[:, c, :], vst[:, c, :, NC - 1]) for c in range(2)])
            advance([fin_s[:, c] for c in range(2)], [s0[:, c] for c in range(2)],
                    [apow[:, 4, c, :].unsqueeze(1).broadcast_to([P, NB, GP]) for c in range(2)], (NB, GP))
            pool.sem_inc(s["scan_done"], 1)

            def gated(i, slot, n, ready):
                pool.wait_ge(s["evac"], n + (EV0 + 1))
                pool.tensor_tensor(one(mixed, i), one(mixed, i), sg[:, slot, :], ALU.mult).then_inc(s["pool_gated"], 1)
            tiles(pool, "glu", gated)
            pool.wait_ge(s["pool_gated"], 2 + 8)
            tiles(pool, "gs", gated)

        @block.vector
        def _(dve):
            count = [0]

            def link(*steps):
                for ins in steps:
                    count[0] += 1
                    ins.then_inc(s["dve_step"], 1)
                dve.wait_ge(s["dve_step"], count[0])

            def tt(o, a, b, op):
                return dve.tensor_tensor(o, a, b, op)

            def norm(k):
                dve.wait_ge(s["sqrt_done"], k + 1)
                link(dve.reciprocal(rstd[:], rstd[:]))
                for j in range(DK):
                    if k % 2 == 0:
                        dve.scalar_tensor_tensor(out=nrm[:, j, :], in0=hT[:, j, :], scalar=gains[:, k, j:j + 1], in1=rstd[:],
                                                 op0=ALU.mult, op1=ALU.mult).then_inc(s["nrm_done"], 1)
                    else:
                        dst = hn if k == 1 else nrm
                        dve.scalar_tensor_tensor(out=dst[:, j, :], in0=hT[:, j, :], scalar=gains[:, k, j:j + 1], in1=rstd[:],
                                                 op0=ALU.mult, op1=ALU.mult).then_inc(s["norm_done"], 1)
                if k % 2 == 0:
                    for j in range(DK):
                        dve.wait_ge(s["hnh_done"], DK * (k // 2) + j + 1)
                        tt(hnl[:, j, :], nrm[:, j, :], hnh[:, j, :].bitcast(F32), ALU.subtract).then_inc(s["norm_done"], 1)

            def low(u, i, j):
                dve.wait_ge(s["hi_done"], i * 4 + (u + 1))
                tt(wl[:, j % 2, :, :], wraw[:, j, :, :], wh[:, j % 2, :, :].bitcast(F32), ALU.subtract).then_inc(s["lo_done"], 1)

            def ffn(which):
                end = FFN_UNITS * (which + 1)
                for j in range(2):
                    low(FFN_UNITS * which + j, 0, j)

                def in_tile(i, j, u0, t0, a0):
                    for k in range(2):
                        low(u0 + 2 * j + k + 2, i, (2 * j + k + 2) % 4)
                    dve.wait_ge(s["silu_done"], i * 2 + (a0 + j + 1))
                    dve.wait_ge(s["unit_done"], i * 4 + (u0 + 2 * j + 2))
                    tt(two(sg[:, j, :]), two(sg[:, j, :]), pair(j, 1), ALU.mult).then_inc(s["ffn_ev"], 1)
                    dve.wait_ge(s["acth_done"], i * 2 + (a0 + j + 1))
                    tt(one(actl, i * 2 + j), sg[:, j, :], one(acth, i * 2 + j).bitcast(F32), ALU.subtract).then_inc(s["act_ready"], 1)

                def out_tile(i, j, u0, split):
                    if split:
                        low(u0 + j + 2, i, (j + 2) % 4)
                    dve.wait_ge(s["unit_done"], i * 4 + (u0 + j + 1))
                    h = two(one(hT, i * 4 + j))
                    dve.scalar_tensor_tensor(out=h, in0=pair(j % 2, 0), scalar=0.5, in1=h, op0=ALU.mult, op1=ALU.add).then_inc(s["ffn_ev"], 1)

                for kind, f0, m, u0, t0, a0 in ffn_plan(which):
                    if kind == "in":
                        with dve.Fori(0, m // 2) as i:
                            for j in range(2):
                                in_tile(i, j, u0, t0, a0)
                    elif u0 + DK < end:
                        dve.wait_ge(s["ffn_ev"], FE0 + t0)
                        with dve.Fori(0, 2) as i:
                            for j in range(4):
                                out_tile(i, j, u0, True)
                    else:
                        dve.wait_ge(s["ffn_ev"], FE0 + t0)
                        for k in range(DK):
                            out_tile(k // 4, k % 4, u0, k < DK - 2)

            def evac(layer, fn, wait_gate=None):
                def body(i, slot, n, ready):
                    dve.wait_ge(s["mm_done"], n + (MM0 + 1))
                    if wait_gate is not None:
                        dve.wait_ge(s["gate_done"], i + (wait_gate + 1))
                    fn(i, slot_half(layer, slot)).then_inc(s["evac"], 1)
                tiles(dve, layer, body)

            def pair(half, o):
                return ps[:, 4 * half + 2 * o:4 * half + 2 * o + 2, 0:HALF]

            def two(ap):
                return ap.rearrange("p (h n) -> p h n", h=2)

            dve.sem_inc(s["lo_done"], FE0)
            dve.sem_inc(s["ffn_ev"], FE0)
            dve.sem_inc(s["act_ready"], FE0)
            for k in range(DK):
                dve.wait_ge(s["mm_done"], k + 1)
                dve.tensor_copy(hT[:, k, 0:SEQ], ps[:, 4 * (k % 2), :])
                dve.tensor_copy(hT[:, k, SEQ:NT], ps[:, 4 * (k % 2) + 1, 0:32]).then_inc(s["evac"], 1)
            dve.tensor_copy(identb[:], ident[:]).then_inc(s["bf_done"], 1)
            dve.tensor_copy(causb[:], caus[:]).then_inc(s["bf_done"], 1)
            norm(0)
            dve.wait_ge(s["dt_done"], 1)
            dve.wait_ge(s["par_in"], 16 * 13)
            lr, li = lam[:, 0, :], lam[:, 1, :]
            TWO_PI_HI = 6.28125
            TWO_PI_LO = 2 * math.pi - TWO_PI_HI
            ROUND = 12582912.0
            link(tt(v(1), lr, ldt, ALU.mult), tt(v(2), li, ldt, ALU.mult))
            link(dve.tensor_scalar(v(5), v(2), 1 / (2 * math.pi), ROUND, ALU.mult, ALU.add))
            link(dve.tensor_scalar(v(5), v(5), -ROUND, None, ALU.add))
            link(dve.scalar_tensor_tensor(out=v(2), in0=v(5), scalar=-TWO_PI_HI, in1=v(2), op0=ALU.mult, op1=ALU.add))
            link(dve.scalar_tensor_tensor(out=v(2), in0=v(5), scalar=-TWO_PI_LO, in1=v(2), op0=ALU.mult, op1=ALU.add))
            link(dve.tensor_scalar(v(2), v(2), 3.1415925, -3.1415925, ALU.min, ALU.max))
            dve.sem_inc(s["ang_done"], 1)
            link(tt(v(9), lr, lr, ALU.mult), tt(v(10), li, li, ALU.mult))
            link(tt(v(9), v(9), v(10), ALU.add))
            link(dve.reciprocal(v(9), v(9)))
            dve.wait_ge(s["trig_done"], 3)
            link(tt(v(8), v(8), v(8), ALU.mult))
            link(dve.tensor_scalar(v(8), v(8), -2.0, 1.0, ALU.mult, ALU.add))
            link(dve.memset(apow[:, 0, 0, :], 1.0), dve.memset(apow[:, 0, 1, :], 0.0),
                 tt(apow[:, 1, 0, :], v(4), v(8), ALU.mult), tt(apow[:, 1, 1, :], v(4), v(7), ALU.mult))
            ar, ai = apow[:, 1, 0, :], apow[:, 1, 1, :]
            link(dve.tensor_scalar(v(10), ar, -1.0, None, ALU.add))
            link(tt(v(11), v(10), lr, ALU.mult), tt(v(12), ai, li, ALU.mult), tt(v(13), ai, lr, ALU.mult), tt(v(14), v(10), li, ALU.mult))
            link(tt(v(11), v(11), v(12), ALU.add), tt(v(13), v(13), v(14), ALU.subtract))
            link(tt(v(11), v(11), v(9), ALU.mult), tt(v(13), v(13), v(9), ALU.mult))

            def powers(arr):
                for m in (1, 2, 4):
                    def bc(c):
                        return arr[:, m, c, :].unsqueeze(1).broadcast_to([P, m, GP])
                    lo = [arr[:, 1:m + 1, c, :] for c in range(2)]
                    hi = [arr[:, m + 1:2 * m + 1, c, :] for c in range(2)]
                    p4 = [s5q[:, k, 0:m, :] for k in range(4)]
                    link(tt(p4[0], lo[0], bc(0), ALU.mult), tt(p4[1], lo[1], bc(1), ALU.mult),
                         tt(p4[2], lo[0], bc(1), ALU.mult), tt(p4[3], lo[1], bc(0), ALU.mult))
                    link(tt(hi[0], p4[0], p4[1], ALU.subtract), tt(hi[1], p4[2], p4[3], ALU.add))
            powers(apow)
            link(dve.tensor_copy(cpow[:, 1], apow[:, 8]))
            powers(cpow)

            def zb(k):
                return v(k).unsqueeze(2).broadcast_to([P, GP, GC])
            link(tt(pt1, bmat[:, 0], zb(11), ALU.mult), tt(pt2, bmat[:, 1], zb(13), ALU.mult),
                 tt(pt3, bmat[:, 1], zb(11), ALU.mult), tt(pt4, bmat[:, 0], zb(13), ALU.mult))
            link(tt(bbar[:, 0], pt1, pt2, ALU.subtract), tt(bbar[:, 1], pt3, pt4, ALU.add))
            dve.sem_inc(s["pow_done"], 1)

            link(tt(dd, dd, ident[0:GC, 0:GC].unsqueeze(1).broadcast_to([GC, G, GC]), ALU.mult))
            ffn(0)
            for r in range(4):
                dve.wait_ge(s["km"], r + 1)
                if r >= 2:
                    dve.wait_ge(s["toep_in"][r % 2], 16 * 8)
                for h in range(2):
                    ins = dve.tensor_copy(kbuf[0:16, r % 2, :, :].rearrange("p (g s) n -> p g s n", s=2)[:, :, h, :],
                                          ps[0:16, 2 * (r % 2) + h, :].rearrange("p (g n) -> p g n", g=4))
                link(ins)
                dve.tensor_tensor(kbuf[0:16, r % 2, :, 0:GC], kbuf[0:16, r % 2, :, 0:GC], dd[:, 8 * r:8 * r + 8, :], ALU.add).then_inc(s["k_ev"], 1)
            norm(1)
            n = first_tile["idx"]
            b = 4 * (n % 2)
            dve.wait_ge(s["mm_done"], MM0 + n + 1)
            dve.tensor_copy(qiT[:, 0:2, :], ps[:, b:b + 2, :])
            W_SCALE = ID ** -0.5 * IH ** -0.5
            for tt_ in range(5):
                m = P if tt_ < 4 else 32
                c0 = 40 * tt_
                dve.tensor_copy(ki4[0:m, tt_, :, :], ps[0:m, b + 2, c0:c0 + ID].unsqueeze(1).broadcast_to([m, 4, ID]))
                if tt_ < 4:
                    dve.tensor_scalar(wtok[:, tt_, :], ps[:, b + 2, c0 + ID:c0 + ID + IH], W_SCALE, None, ALU.mult)
            dve.tensor_copy(qis4, ps[0:32, b + 3, 0:256].rearrange("p (h d) -> p h d", h=IH).unsqueeze(2).broadcast_to([32, IH, 4, ID]))
            dve.tensor_scalar(wT8, ps[0:8, b + 3, 256:288], W_SCALE, None, ALU.mult).then_inc(s["evac"], 1)
            dve.wait_ge(s["kt_t"], 1)
            dve.tensor_copy(kiT[:, 0:SEQ], ps[:, 4, :])
            dve.tensor_copy(kiT[:, SEQ:NT], ps[:, 5, 0:32]).then_inc(s["kt_ev"], 1)
            dve.wait_ge(s["kt_t"], 2)
            dve.tensor_copy(qis[:].rearrange("p b h q -> p h b q"), ps[:, 6, 0:256].rearrange("p (h b q) -> p h b q", h=IH, b=NB)).then_inc(s["kt_ev"], 1)

            topk_n = [0]

            def top(scores, rounds):
                n0 = topk_n[0]
                with dve.Fori(0, rounds) as i:
                    dve.max(out=top8[0:scores.shape[0], :], in_=scores).then_inc(s["topk"], 1)
                    dve.wait_ge(s["topk"], i * 2 + (n0 + 1))
                    dve.tensor_copy(topwait, top8[:, 0:1])
                    dve.match_replace(out=scores, in_to_replace=top8[0:scores.shape[0], :], in_values=scores, imm_value=TAKEN).then_inc(s["topk"], 1)
                    dve.wait_ge(s["topk"], i * 2 + (n0 + 2))
                topk_n[0] += 2 * rounds
            for x in range(24):
                qb, h = 1 + x // 8, x % 8
                w = P * (qb + 1)
                dve.wait_ge(s["ix_relu"], x + 1)
                if h == 0:
                    dve.tensor_scalar(sc[:, 0:w], rl[:, x % 2, 0:w], wtok[:, qb, 0:1], None, ALU.mult).then_inc(s["ix_acc"], 1)
                else:
                    dve.wait_ge(s["ix_acc"], x)
                    dve.scalar_tensor_tensor(out=sc[:, 0:w], in0=rl[:, x % 2, 0:w], scalar=wtok[:, qb, h:h + 1], in1=sc[:, 0:w],
                                             op0=ALU.mult, op1=ALU.add).then_inc(s["ix_acc"], 1)
                if h == 7:
                    dve.wait_ge(s["ix_acc"], x + 1)
                    link(tt(sc[:, w - P:w], sc[:, w - P:w], caus[:], ALU.add))
                    top(sc[:, 0:w], TOPK_P // 8)
                    dve.tensor_scalar(selq[qb], sc[:, 0:w], 0.5 * TAKEN, MASK, ALU.is_ge, ALU.mult).then_inc(s["sel_done"], 1)
                    dve.wait_ge(s["sel_done"], qb)

            dve.wait_ge(s["evac"], EV0 + first_tile["kv"])
            link(dve.memset(qbd[:].rearrange("p j b r -> p (j b r)"), 0.0))
            for j in range(4):
                for h in range(2):
                    sl = slice(64 * h, 64 * h + 64)
                    hh = 2 * j + h
                    ins = dve.tensor_copy(qbd[sl, j, :, NS * hh:NS * hh + NS], qT[sl, j, SEQ:NT].rearrange("p (b q) -> p b q", b=NB))
            link(ins)
            dve.wait_ge(s["sc_in"], 16 * 12)
            tt(rbexp.rearrange("p (b h q) -> p b h q", b=4, h=HEADS), same_step.rearrange("p (b h q) -> p b h q", b=4, h=HEADS),
               rb4.unsqueeze(1).unsqueeze(3).broadcast_to([P, 4, HEADS, NS]), ALU.mult)
            link(dve.tensor_copy(tok_row, tok_row_f))
            dve.sem_inc(s["sm_prep"], 1)
            dve.wait_ge(s["sm_pe"], 1)
            for g in range(2):
                ins = tt(wsel[:, g, :], ps[:, 3, 0:32], row_tok[:, g, :], ALU.mult)
            link(ins)
            dve.sem_inc(s["sm_b"], 1)
            for b_ in range(NB):
                dve.wait_ge(s["sx_t"], b_ + 1)
                if b_ >= 2:
                    dve.wait_ge(s["sx_mm"], b_ - 1)
                dve.tensor_copy(kxT[:, b_ % 2, :], ps[:, 4, 0:256]).then_inc(s["sx_tc"], 1)
            dve.wait_ge(s["sx_w"], 2)
            link(dve.tensor_copy(scs[:, 0:PAST].rearrange("p (b n) -> p b n", b=2), ps[0:32, 5:7, :]),
                 tt(scs[:, PAST:NKEY], ps[0:32, 7, 0:32], new_mask, ALU.add))
            dve.sem_inc(s["sx_got"], 1)
            top(scs, TOPK_S // 8)
            dve.tensor_scalar(sels, scs, 0.5 * TAKEN, MASK, ALU.is_ge, ALU.mult).then_inc(s["sx_sel"], 1)
            dve.wait_ge(s["sx_sel"], 1)
            dve.wait_ge(s["bias_in"], 16 * HEADS)
            for x in range(34):
                if x < 32:
                    qb, h = x // 8, x % 8
                    w = P * (qb + 1)
                    dve.wait_ge(s["at_s"], x + 1)
                    if x >= 2:
                        dve.wait_ge(s["at_exp"], x - 1)
                    dve.tensor_tensor_reduce(smx[:, x % 2, 0:w], ps[:, x % 2, 0:w], tb[:, h, SEQ - w:SEQ], -1.0, 3e38,
                                             ALU.add, ALU.min, nmx[:, x % 2:x % 2 + 1]).then_inc(s["at_sm"], 1)
                if x >= 2 and (x - 2) % 8 == 7:
                    qb = (x - 2) // 8
                    dve.wait_ge(s["at_pv"], x - 1)
                    dve.wait_ge(s["at_exp"], 8 * qb + 8)
                    link(dve.reciprocal(rinv[:, qb % 2, :], rsum[:, qb % 2, :]))
                    if qb >= 2:
                        dve.wait_ge(s["at_ot"], qb - 1)
                    tt(ao[:, qb % 2, :].rearrange("p (h d) -> p h d", h=HEADS), ps[:, 4 + qb % 2, :].rearrange("p (h d) -> p h d", h=HEADS),
                       rinv[:, qb % 2, :].unsqueeze(2).broadcast_to([P, HEADS, HD]), ALU.mult).then_inc(s["at_o"], 1)
                    dve.wait_ge(s["at_ot"], qb + 1)
                    if qb == 0:
                        dve.wait_ge(s["kv_out"], 16 * 4)
                    dve.tensor_copy(attT[:, :, P * qb:P * qb + P], ps[:, 6 + qb % 2, :].rearrange("p (j n) -> p j n", j=4)).then_inc(s["at_otc"], 1)

            dve.wait_ge(s["bs_mm"], 1)
            dve.tensor_copy(bs[:, 0:PAST].rearrange("p (b n) -> p b n", b=2), ps[:, 0:2, :])
            dve.tensor_copy(bs[:, PAST:NKEY], ps[:, 2, 0:32]).then_inc(s["bs_ev"], 1)
            dve.wait_ge(s["pool_gated"], 2 + 16)
            for g in range(2):
                dve.wait_ge(s["ss_mm"], g + 1)
                if g:
                    dve.wait_ge(s["ss_exp"], g)
                dve.tensor_tensor_reduce(sms, ps[:, 0:3, :].rearrange("p b n -> p (b n)")[:, 0:NKEY], bs, -1.0, 3e38,
                                         ALU.add, ALU.min, nmx[:, g:g + 1]).then_inc(s["ss_sm"], 1)
                dve.wait_ge(s["ss_exp"], g + 1)
                link(dve.reciprocal(rinv[:, 0, g:g + 1], rsum[:, 0, g:g + 1]))
                link(dve.tensor_scalar(hmr[:, g, :], row_head, rinv[:, 0, g:g + 1], None, ALU.mult))
                dve.wait_ge(s["sv_mm"], g + 1)
                tt(osel[:, g, :].rearrange("p (h d) -> p h d", h=HEADS), ps[:, 5, :].rearrange("p (h d) -> p h d", h=HEADS),
                   hmr[:, g, :].unsqueeze(2).broadcast_to([P, HEADS, HD]), ALU.mult).then_inc(s["sv_o"], 1)
            dve.wait_ge(s["so_mm"], 1)
            dve.tensor_copy(attT[:, :, SEQ:NT], ps[:, 6, 0:128].rearrange("p (j n) -> p j n", j=4)).then_inc(s["so_ev"], 1)

            def add_att(i, half):
                tt(two(sg[:, half, :]), pair(half, 1), two(sg[:, half, :]), ALU.mult).then_inc(s["att_gated"], 1)
                dve.wait_ge(s["att_gated"], i + 1)
                return tt(one(mixed, i), one(mixed, i), sg[:, half, :], ALU.add)
            evac("ga_att", add_att, 0)
            evac("out", lambda i, half: tt(two(one(hT, i)), pair(half, 0), two(one(hT, i)), ALU.add))
            norm(2)
            ffn(1)
            norm(3)
            for k in range(5):
                m = P if k < 4 else 32
                bk = 2 + 2 * (k % 2)
                dve.wait_ge(s["yt_t"], k + 1)
                dve.tensor_copy(ytok[0:m, k, :].rearrange("p (b n) -> p b n", b=2), ps[0:m, bk:bk + 2, :]).then_inc(s["yt_ev"], 1)


INPUTS = ["x_prompt", "x_sample", "cache_k", "cache_v", "cache_kidx", "state_s5_re", "state_s5_im", "page_table",
          "g_ffn1", "w_ffn1_in", "w_ffn1_out", "g_mix", "w_in", "s5_lam_re", "s5_lam_im", "s5_log_dt",
          "s5_b_re", "s5_b_im", "s5_c_re", "s5_c_im", "s5_d", "w_s5_glu", "w_att_proj", "rel_bias", "w_out",
          "g_ffn2", "w_ffn2_in", "w_ffn2_out", "g_final"]
OUTPUTS = [("y_prompt", (1, SEQ, D)), ("y_sample", (NB, NS, D)),
           ("k_prompt", (1, 1, SEQ, HEADS, HD)), ("v_prompt", (1, 1, SEQ, HEADS, HD)), ("kidx_prompt", (1, 1, SEQ, ID)),
           ("s5_re_prompt", (1, 1, G, ST)), ("s5_im_prompt", (1, 1, G, ST)),
           ("k_sample", (1, NB, NS, HEADS, HD)), ("v_sample", (1, NB, NS, HEADS, HD)), ("kidx_sample", (1, NB, NS, ID)),
           ("s5_re_sample", (1, NB, G, ST)), ("s5_im_sample", (1, NB, G, ST))]


def kernel(**inputs):
    import concourse.bacc as _bacc
    from concourse.bass_utils import run_bass_kernel_spmd as _run

    nc = _bacc.Bacc("TRN2", target_bir_lowering=False, num_devices=1)
    arrays, t, out = {}, {}, {}
    data = {n: np.ascontiguousarray(inputs[n]) for n in INPUTS}
    data.update(shape_constants())
    for n, a in data.items():
        arrays["in_" + n] = a
        t[n] = nc.dram_tensor("in_" + n, a.shape, mybir.dt.from_np(a.dtype), kind="ExternalInput").ap()
    for n, shape in OUTPUTS:
        out[n] = nc.dram_tensor("out_" + n, shape, F32, kind="ExternalOutput").ap()
    build(nc, t, out)
    r = _run(nc, [arrays], core_ids=[0])
    return tuple(r.results[0]["out_" + n] for n, _ in OUTPUTS)
```

```python
from contextlib import ExitStack
import math

import numpy as np
import concourse.bass as bass
from concourse import mybir

F32 = mybir.dt.float32
F32R = mybir.dt.float32r
BF16 = mybir.dt.bfloat16
I32 = mybir.dt.int32
ALU = mybir.AluOpType
ACT = mybir.ActivationFunctionType
AX = mybir.AxisListType

P = 128
D = 1024
DK = D // P
SEQ, NB, NS = 512, 8, 4
NT = SEQ + NB * NS
HALF = NT // 2
FF = 2816
FK = FF // P
HEADS, HD = 8, 64
IH, ID = 8, 32
TOPK_P, TOPK_S = SEQ // 4, 256
PAST, PAGE = 1024, 128
NPAGE = PAST // PAGE
NKEY = PAST + NB * NS
G, GC, ST = 32, 16, 64
GP = G // 2
CH = 8
NC = SEQ // CH
UC = NC + NB
NBKT = 32
EPS = 1e-6
MASK = -1e30
TAKEN = -3e38
C_U, C_Q, C_K, C_V, C_QI = 0, 512, 1024, 1536, 2048
NQI = IH * ID + ID + IH
C_GS, C_GA = C_QI + NQI, C_QI + NQI + D


def bucket(dist):
    d = np.maximum(dist, 0)
    nf = np.maximum(d, 1).astype(np.float32)
    large = 16 + (np.log(nf / np.float32(16)) / np.float32(math.log(8.0)) * np.float32(16) + np.float32(1e-5)).astype(np.int32)
    return np.where(d < 16, d, np.minimum(large, NBKT - 1))


def shape_constants():
    c = {}
    c["ident"] = np.eye(P, dtype=np.float32)
    y = np.arange(640)
    c["oh_prompt"] = (bucket(511 - y)[None, :] == np.arange(NBKT)[:, None]).astype(np.float32)
    s = np.arange(PAST)
    oh = np.zeros((NS, NBKT, NKEY), np.float32)
    for q in range(NS):
        oh[q, bucket(PAST + q - s), s] = 1
        oh[q, bucket(q - np.arange(NB * NS) % NS), PAST + np.arange(NB * NS)] = 1
    c["oh_sample"] = oh.reshape(P, NKEY)
    q_of = np.arange(P) % NS
    c["same_step"] = (np.repeat(np.arange(NS), NBKT)[:, None] == q_of[None, :]).astype(np.float32)
    row_b, row_h = np.arange(P) // 32, np.arange(P) // NS % HEADS
    tok = np.arange(NB * NS)
    for g in range(2):
        c[f"row_tok{g}"] = ((row_b + 4 * g)[:, None] * NS + q_of[:, None] == tok[None, :]).astype(np.float32)
        c[f"tok_row{g}"] = np.ascontiguousarray(c[f"row_tok{g}"].T)
    c["row_head"] = (row_h[:, None] == np.arange(HEADS)[None, :]).astype(np.float32)
    c["head_row"] = np.ascontiguousarray(c["row_head"].T)
    c["causal"] = np.where(np.arange(P)[None, :] <= np.arange(P)[:, None], 0, MASK).astype(np.float32)
    ok = (tok[:, None] // NS == tok[None, :] // NS) & (tok[None, :] <= tok[:, None])
    c["new_mask"] = np.where(ok, 0, MASK).astype(np.float32)
    return c


def build(nc, t, out):
    ctx = ExitStack()
    with ctx:
        def sb(name, shape, dt=F32):
            return ctx.enter_context(nc.sbuf_tensor(name, shape, dt))

        def sem(name):
            return ctx.enter_context(nc.semaphore(name))

        def one(ap3, i):
            return ap3[:, bass.ds(i, 1), :].rearrange("p a n -> p (a n)")

        hT = sb("hT", [P, DK, NT])
        biasmem = sb("biasmem", [P, HEADS * SEQ + NKEY])
        kvtok = sb("kvtok", [P, 2, 5, 512])
        qkT = sb("qkT", [P, 2, 4, NT])
        qiT = sb("qiT", [P, 2, SEQ])
        kiT = sb("kiT", [P, NT])
        sg = sb("sg", [P, 2, NT])
        rstd = sb("rstd", [P, NT])
        ki4 = sb("ki4", [P, 5, 4, ID])
        qis = sb("qis", [P, NB, IH, NS])
        qbd = sb("qbd", [P, 4, NB, HEADS * NS])
        ident = sb("ident_sb", [P, P])
        caus = sb("caus", [P, P])
        ones = sb("ones", [P, P])
        gains = sb("gains", [P, 4, DK])
        epsc = sb("epsc", [P, 1])
        wtok = sb("wtok", [P, 4, IH])
        s0 = sb("s0", [P, 2, NB, GP])
        apow = sb("apow", [P, 9, 2, GP])
        cpow = sb("cpow", [P, 9, 2, GP])
        tiny = sb("tiny", [P, 64])
        pt_sb = sb("pt_sb", [1, NB * NPAGE], I32)
        ps = ctx.enter_context(nc.psum_tensor("ps", [P, 8, 512], F32))

        with ExitStack() as ends:
            ends.enter_context(nc.sbuf_tensor("below_ends", [P, 2 * DK * NT], F32))
            xmem = ends.enter_context(nc.sbuf_tensor("xmem", [P, 8064], F32))
        with ExitStack() as ffn:
            def fb(name, shape, dt=F32R):
                return ffn.enter_context(nc.sbuf_tensor(name, shape, dt))
            hnh, hnl = fb("hn_high", [P, DK, NT]), fb("hn_low", [P, DK, NT])
            acth, actl = fb("act_high", [P, 8, NT]), fb("act_low", [P, 8, NT])
            wraw = fb("wraw", [P, 4, DK, P], F32)
            wh, wl = fb("w_high", [P, 2, DK, P]), fb("w_low", [P, 2, DK, P])
        with ExitStack() as norm_mem:
            norm_mem.enter_context(nc.sbuf_tensor("below_norm", [P, DK * NT], F32))
            nrm = norm_mem.enter_context(nc.sbuf_tensor("nrm", [P, DK, NT], F32))
        hn = sb("hn", [P, DK, NT])
        wslot = sb("wslot", [P, 2, DK * NQI])
        big = sb("big", [P, 10496])
        uv = sb("uv", [P, 2, G * (UC + 1)])
        idxm = sb("idxm", [P, 2160])

        tb = biasmem[:, 0:HEADS * SEQ].rearrange("p (h n) -> p h n", h=HEADS)
        bs = biasmem[:, HEADS * SEQ:]
        ktok, vtok = kvtok[:, 0], kvtok[:, 1]
        qT, kT = qkT[:, 0], qkT[:, 1]
        xtok = xmem[:, 0:5 * D].rearrange("p (t d) -> p t d", t=5)
        yre = biasmem[:, 0:2304].rearrange("p (g k i) -> p g k i", g=GP, k=9)
        yim = biasmem[:, 2304:4608].rearrange("p (g k i) -> p g k i", g=GP, k=9)
        wb = kvtok[:, :, :, :].rearrange("p a b c -> p (a b c)")[:, 0:4096].rearrange(
            "p (c g t j) -> p c g t j", c=2, g=GP, t=CH)
        toep = big[:, 0:4096].rearrange("p (g n) -> p g n", g=G)
        gb = big[:, 4096:8192].rearrange("p (c g n) -> p c g n", c=2, g=GP)
        ybuf = big[0:UC, 8320:8320 + 2 * CH * P].rearrange("p (b k g i) -> p b k g i", b=2, k=CH, g=8)
        kbuf = [m.rearrange("p (g n) -> p g n", g=8) for m in (big[0:GC, 8192:9216], big[0:GC, 9216:10240], uv[0:GC, 0, 0:1024], uv[0:GC, 0, 1024:2048])]
        uch = uv[:, 0, 0:G * UC].rearrange("p (g c) -> p g c", g=G)
        vst = uv[:, 1].rearrange("p (c g n) -> p c g n", c=2, g=GP)
        uT = uv[:, 1, 0:4 * NT].rearrange("p (t n) -> p t n", t=4)
        yT = big[:, 6144:6144 + 4 * NT].rearrange("p (t n) -> p t n", t=4)
        gT = uv[:, 0, 0:4 * NT].rearrange("p (t n) -> p t n", t=4)
        early = qkT[:, :, :, :].rearrange("p a b c -> p (a b c)")
        lam = early[:, 0:32].rearrange("p (c g) -> p c g", c=2)
        ldt = early[:, 32:48]
        s5v = early[:, 48:48 + 16 * 20].rearrange("p (k g) -> p k g", k=20)
        bmat = early[:, 512:1024].rearrange("p (c g j) -> p c g j", c=2, g=GP)
        bbar = early[:, 1024:1536].rearrange("p (c g j) -> p c g j", c=2, g=GP)
        craw = early[:, 1536:2560].rearrange("p (c t n) -> p c t n", c=2, t=4)
        cT = early[:, 2560:3072].rearrange("p (c g i) -> p c g i", c=2, g=GP)
        s0raw = early[:, 3072:3328].rearrange("p (c n) -> p c n", c=2)
        dd = early[0:GC, 3328:3840].rearrange("p (g i) -> p g i", g=G)
        s5q = early[:, 3840:4096].rearrange("p (k m g) -> p k m g", k=4, m=4)
        pt1, pt2, pt3, pt4 = (kvtok[:, :, :, :].rearrange("p a b c -> p (a b c)")[:, 4096 + 256 * k:4352 + 256 * k]
                              .rearrange("p (g j) -> p g j", g=GP) for k in range(4))
        sgf = sg[:, :, :].rearrange("p a n -> p (a n)")
        fin_s = sgf[:, 0:256].rearrange("p (c b g) -> p c b g", c=2, b=NB)
        fin_p = sgf[:, 256:288].rearrange("p (c g) -> p c g", c=2)
        prodmem = sgf[:, 288:800]
        fin_t = ki4[:, :, :, :].rearrange("p a b c -> p (a b c)")[:, 0:512]
        ohp = xmem[:, 5120:5760]
        relb = tiny[0:NBKT, 0:HEADS]
        shrow = xmem[0:HEADS, 5760:6400]
        nmx = tiny[:, 8:10]
        rsum = tiny[:, 16:32].rearrange("p (a h) -> p a h", a=2)
        rinv = tiny[:, 32:48].rearrange("p (a h) -> p a h", a=2)
        top8 = tiny[:, 48:56]
        topwait = tiny[:, 56:57]
        rootwarm = tiny[:, 57:58]

        def v(k):
            return s5v[:, k, :]

        mixed = big[:, 0:DK * NT].rearrange("p (m n) -> p m n", m=DK)
        base = DK * NT
        sc = idxm[:, 0:512]
        rl = idxm[:, 512:1536].rearrange("p (b n) -> p b n", b=2)
        selq = [None] + [idxm[:, 1584 + a // 2:1584 + (a + w) // 2].bitcast(BF16) for a, w in ((0, 256), (256, 384), (640, 512))]
        smx = big[:, base:base + 1024].rearrange("p (b n) -> p b n", b=2)
        pexp = big[:, base + 1024:base + 2048].rearrange("p (b n) -> p b n", b=2)
        pT = big[:, base + 2048:base + 3072].rearrange("p (b n) -> p b n", b=2)
        ao = big[:, base + 3072:base + 4096].rearrange("p (b n) -> p b n", b=2)
        attT = kvtok[:, 0, :, :].rearrange("p a b -> p (a b)")[:, 0:4 * NT].rearrange("p (j n) -> p j n", j=4)
        val = uv[:, 1, 0:2 * NT].rearrange("p (b n) -> p b n", b=2)
        wflat = wslot[:, :, :].rearrange("p s n -> p (s n)")
        kring = [m.rearrange("p (r n) -> p r n", r=4) for m in (wflat[:, 0:2048], wflat[:, 2048:4096], biasmem[:, 0:2048], biasmem[:, 2048:4096])]
        kidx = big[:, 4096:6144].rearrange("p (n d) -> p n d", d=ID)
        kxT = wflat[:, 3392:4416].rearrange("p (b n) -> p b n", b=2)
        rls = big[:, 0:NKEY]
        scs = idxm[0:32, 0:NKEY]
        tbm = uv[:, 1, 2 * NT:2 * NT + 1024].rearrange("p (b n) -> p b n", b=2)
        sels = idxm[0:32, 1056:1056 + NKEY // 2].bitcast(BF16)
        ohs = big[:, 8448:8448 + NKEY]
        pgT = uv[:, :, :].rearrange("p a n -> p (a n)")[:, 0:4096].rearrange("p (b j n) -> p b j n", b=2, j=4)
        sms = big[:, base:base + NKEY]
        pes = big[:, base + 1056:base + 1056 + NKEY]
        ptS = big[:, base + 2112:base + 2112 + 9 * P].rearrange("p (k n) -> p k n", k=9)
        osel = sg[:, :, 0:512]
        qis4 = sg[0:32, :, :].rearrange("p a b -> p (a b)")[:, 0:IH * 4 * ID].rearrange("p (h r d) -> p h r d", h=IH, r=4)
        row_tok = rstd[:, 0:64].rearrange("p (g n) -> p g n", g=2)
        row_head = rstd[:, 64:72]
        head_row = rstd[0:8, 72:200]
        wT8 = rstd[0:8, 512:544]
        wsel = rstd[:, 232:296].rearrange("p (g n) -> p g n", g=2)
        new_mask = rstd[0:32, 296:328]
        tok_row = rstd[0:32, 328:456].bitcast(BF16).rearrange("p (g n) -> p g n", g=2)
        rb4 = rstd[:, 456:464]
        hmr = rstd[:, 464:480].rearrange("p (g h) -> p g h", g=2)
        same_step = wflat[:, 4544:4672]
        rbexp = wflat[:, 4416:4544]
        tok_row_f = wslot[0:32, 0, 2048:2304].rearrange("p (g n) -> p g n", g=2)
        gaw = big[:, 8448:8448 + 2 * DK * P].rearrange("p (b k n) -> p b k n", b=2, k=DK)
        v_rows = vtok.rearrange("p a n -> p (a n)")
        ga_s = [qT[:, i, :] for i in range(4)] + [v_rows[:, NT * i:NT * i + NT] for i in range(3)] + [idxm[:, 1584:1584 + NT]]
        attw = wflat[:, 0:4 * D].rearrange("p (k n) -> p k n", k=4)
        fin_mix = biasmem[:, 0:2 * NT].rearrange("p (b n) -> p b n", b=2)
        ytok = xmem[:, 0:5 * D].rearrange("p (t d) -> p t d", t=5)

        scr_shift = nc.dram_tensor("scr_shift", [HEADS, P, 640], F32, kind="Internal").ap()
        scr_u = nc.dram_tensor("scr_u", [CH, 4, P, NC], F32, kind="Internal").ap()
        scr_us = nc.dram_tensor("scr_us", [NS, 4, P, NB], F32, kind="Internal").ap()

        s = {n: sem(n) for n in (
            "x_in", "x_rest", "oh_in", "caus_in", "const_in", "par_in", "pt_in", "sample_const_in", "sample_onehot_in",
            "kidx_in", "bias_in", "att_w_in", "shift_out", "toep_in", "u_out", "u_in", "kidx_out", "kv_out", "res_out",
            "mm_done", "evac",
            "unit_done", "hi_done", "lo_done", "ffn_ev", "silu_done", "acth_done", "act_ready",
            "sq_done", "sum_done", "ssum_done", "sqrt_done", "scaled", "norm_done", "nrm_done", "hnh_done",
            "norm_even", "norm_odd",
            "dve_step", "pool_step", "topk_step",
            "pool_const", "early_pe", "early_act", "shift_mm", "shift_ev", "dt_done", "ang_done", "trig_done",
            "pow_done", "prep_done", "input_mats_turned", "input_mats_out", "lag_kernels", "lag_kernels_out",
            "toep_zero", "u_zero",
            "chunk_inputs", "chunk_inputs_out", "scan_done", "chunk_outputs", "chunk_outputs_out", "y_turn",
            "y_turned", "gelu_done", "fin_mm", "fin_ev", "val_gated", "pool_gated",
            "index_keys_turned", "index_keys_out", "keys_turned", "keys_out", "logits_ready", "relu_done",
            "index_added", "prompt_selected",
            "tbm_done", "scores_ready", "scores_biased", "probs_ready", "probs_turned", "probs_out", "values_ready",
            "att_scaled", "att_turned", "att_out",
            "sample_prep", "head_weights", "head_weights_out", "pages_turned", "pages_out", "sample_logits",
            "sample_relu", "sample_index", "sample_index_out", "sample_selected", "sample_bias", "sample_bias_out",
            "kv_used", "k_turned", "k_out_act", "k_out_dve", "k_scored", "sample_scores", "sample_biased",
            "sample_exp", "sample_probs_turned", "sample_probs_out", "sample_values", "sample_values_out",
            "sample_att_turned", "sample_att_out",
            "ga_mm", "ga_ev", "att_mm", "att_ev", "mix_done", "mixh_done", "mix_ready",
            "final_turned", "final_out")}
        raw_in = [sem(f"raw_in{i}") for i in range(4)]
        ga_in = [sem(f"ga_in{i}") for i in range(2)]
        w_ready = [sem(f"w_ready{i}") for i in range(2)]
        kv_in = [[sem(f"kv_in{i}_{q}") for i in range(4)] for q in ("first", "last")]

        LAYERS = [("idx", 1, 1), ("u", 4, 1), ("q", 4, 1), ("kv", 4, 1), ("gs", 8, 1), ("glu", 8, 2)]
        first_tile, slot_base, n_, sl_ = {}, {}, 0, [0, 0]
        for name, cnt, d_ in LAYERS:
            first_tile[name], slot_base[name] = n_, list(sl_)
            for k_ in range(cnt):
                sl_[(n_ + k_) % 2] += 16 * d_
            n_ += cnt
        EV0 = DK

        GROUPS = [(0, 8), (8, 8), (16, 6)]
        FFN_UNITS = sum(2 * m + DK for _, m in GROUPS)
        FFN_TILES = sum(m + DK for _, m in GROUPS)
        FIRST_UNIT, FIRST_FTILE = (0, FFN_UNITS + DK), (0, FFN_TILES + DK)
        assert sum(m for _, m in GROUPS) == FK and all(2 * m % 4 == 0 for _, m in GROUPS)
        FE0 = 4

        def ffn_plan(which):
            u, tl, g_ = FIRST_UNIT[which], FIRST_FTILE[which], 0
            for f0, m in GROUPS:
                yield "in", f0, m, u, tl, FK * which + g_
                u, tl, g_ = u + 2 * m, tl + m, g_ + m
                yield "out", f0, m, u, tl, FK * which + g_
                u, tl = u + DK, tl + DK

        def tiles(eng, name, body):
            n0, (_, cnt, d) = first_tile[name], next(l for l in LAYERS if l[0] == name)
            def step(i2, j, i):
                slot = (n0 + j) % 2
                body(i, slot, i + n0, slot_base[name][slot] + (i2 + 1) * (16 * d))
            if cnt > 2:
                with eng.Fori(0, cnt // 2) as r:
                    for j in range(2):
                        step(r, j, r * 2 + j)
            else:
                for i in range(cnt):
                    step(i // 2, i % 2, i)

        ctx.enter_context(nc.allow_non_contiguous_dma(reason="small parameters"))
        def h_ready(k, j):
            return [(s["evac"], EV0 - DK + j + 1), (s["ffn_ev"], FE0 + FFN_TILES - DK + j + 1),
                    (s["ffn_ev"], FE0 + FFN_TILES + j + 1), (s["ffn_ev"], FE0 + 2 * FFN_TILES + j + 1)][k]

        block = ctx.enter_context(nc.Block())

        GA_AFTER_K, GA_AFTER_V = (2, 3, 5, 6), (4, 5)

        def mix_low_at(k):
            return (k + 1) % DK

        LOGIT_BANK = (2, 3, 6, 7)
        MM0 = DK
        ALLT = n_

        ACT_PAGES = 6

        def kidx_page(eng, i):
            pg = eng.value_load(pt_sb[0:1, bass.ds(i, 1)], min_val=0, max_val=t["cache_kidx"].shape[1] - 1)
            eng.dma_start(one(kidx, i), t["cache_kidx"][0][bass.ds(pg, 1), :, :].rearrange("a p d -> p (a d)")).then_inc(s["kidx_in"], 16)

        def page_loads(eng, first):
            for g in range(2):
                for c, n in enumerate(("cache_k", "cache_v")):
                    src = t[n][0].rearrange("n p h d -> n p (h d)")
                    with eng.Fori(0, 2) as i:
                        for r in range(4):
                            eng.wait_ge(s["kv_used"], i * 4 + (16 * g + 8 * c + r + 1))
                            if r == 2:
                                eng.wait_ge(s["scores_biased"], 32)
                            for k in range(first, first + 2):
                                pg = eng.value_load(pt_sb[0:1, bass.ds(i * 16 + (32 * g + 4 * r + k), 1)], min_val=0, max_val=src.shape[0] - 1)
                                eng.dma_start(kring[r][:, k, :], src[bass.ds(pg, 1), :, :].rearrange("a p d -> p (a d)")).then_inc(kv_in[first // 2][r], 16)

        @block.sync
        def _(sp):
            sp.dma_start(xtok[:, 0:4, 0:P], t["x_prompt"][0].rearrange("(t p) d -> p t d", p=P)[:, :, 0:P]).then_inc(s["x_in"], 16)
            sp.dma_start(xtok[0:32, 4, :], t["x_sample"].rearrange("b s d -> (b s) d")).then_inc(s["x_in"], 16)
            sp.dma_start(ident[:], t["ident"]).then_inc(s["x_in"], 16)
            sp.dma_start(xtok[:, 0:4, P:D], t["x_prompt"][0].rearrange("(t p) d -> p t d", p=P)[:, :, P:D]).then_inc(s["x_rest"], 16)

            def load(layer, *parts):
                def body(i, slot, n, ready):
                    sp.wait_ge(s["mm_done"], n + (MM0 - 1))
                    for at, w, c0, width in parts:
                        kb = w.shape[1]
                        dst = wslot[:, slot, at * P:at * P + kb * width].rearrange("p (k n) -> p k n", k=kb)
                        sp.dma_start(dst, w[:, :, bass.ds(i * width + c0, width)]).then_inc(w_ready[slot], 16)
                tiles(sp, layer, body)

            def load_ffn(which, w_in, w_out):
                for kind, f0, m, u0, t0, a0 in ffn_plan(which):
                    steps = m // 2 if kind == "in" else 2
                    with sp.Fori(0, steps) as i:
                        for j in range(4):
                            sp.wait_ge(s["lo_done"], i * 4 + (u0 + j + FE0 - 3))
                            if kind == "in":
                                c0 = P * (f0 + j // 2) + FF * (j % 2)
                                sp.dma_start(wraw[:, j, :, :], w_in[:, :, bass.ds(i * (2 * P) + c0, P)]).then_inc(raw_in[j], 16)
                            else:
                                sp.dma_start(wraw[:, j, 0:m, :], w_out[:, f0:f0 + m, bass.ds(i * (4 * P) + j * P, P)]).then_inc(raw_in[j], 16)

            rows = lambda n: t[n][0].rearrange("(k p) n -> p k n", p=P)
            load_ffn(0, rows("w_ffn1_in"), rows("w_ffn1_out"))
            sp.wait_ge(s["unit_done"], FFN_UNITS)
            load("idx", (0, rows("w_in"), C_QI, NQI))
            load("u", (0, rows("w_in"), C_U, P))
            load("q", (0, rows("w_in"), C_Q, P))
            load("kv", (0, rows("w_in"), C_K, 256))
            sp.wait_ge(s["evac"], EV0 + first_tile["u"])
            sp.dma_start(out["kidx_prompt"][0, 0].rearrange("(t p) d -> p t d", p=P), ki4[:, 0:4, 0, :]).then_inc(s["kidx_out"], 16)
            sp.dma_start(out["kidx_sample"][0].rearrange("b s d -> (b s) d"), ki4[0:32, 4, 0, :]).then_inc(s["kidx_out"], 16)
            for g in range(2):
                sp.dma_start(row_tok[:, g, :], t[f"row_tok{g}"]).then_inc(s["sample_const_in"], 16)
                sp.dma_start(tok_row_f[:, g, :], t[f"tok_row{g}"]).then_inc(s["sample_const_in"], 16)
            sp.dma_start(row_head, t["row_head"]).then_inc(s["sample_const_in"], 16)
            sp.dma_start(head_row, t["head_row"]).then_inc(s["sample_const_in"], 16)
            sp.dma_start(new_mask, t["new_mask"]).then_inc(s["sample_const_in"], 16)
            sp.dma_start(same_step, t["same_step"]).then_inc(s["sample_const_in"], 16)
            for q in range(NS):
                sp.dma_start(rb4[32 * q:32 * q + 32, :], t["rel_bias"]).then_inc(s["sample_const_in"], 16)
            sp.wait_ge(s["chunk_inputs"], 4)
            sp.wait_ge(s["pt_in"], 16)
            with sp.Fori(0, (NB * NPAGE - 4 * ACT_PAGES) // 4) as i:
                for k in range(4):
                    kidx_page(sp, i * 4 + k)
            sp.wait_ge(s["evac"], EV0 + first_tile["gs"])
            for a, n in ((ktok, "k"), (vtok, "v")):
                sp.dma_start(out[n + "_prompt"][0, 0].rearrange("(t p) h d -> p t (h d)", p=P), a[:, 0:4, :]).then_inc(s["kv_out"], 16)
                sp.dma_start(out[n + "_sample"][0].rearrange("b s h d -> (b s) (h d)"), a[0:32, 4, :]).then_inc(s["kv_out"], 16)
            sp.wait_ge(s["fin_ev"], 1)
            for c, n in enumerate(("s5_re", "s5_im")):
                sp.dma_start(out[n + "_sample"][0].rearrange("b (g s) p -> (b g) (s p)", s=2), fin_t[:, P * c:P * c + P]).then_inc(s["res_out"], 16)
                sp.dma_start(out[n + "_prompt"][0, 0].rearrange("(g s) p -> g (s p)", s=2),
                             fin_t[0:GP, 256 + P * c:384 + P * c]).then_inc(s["res_out"], 16)
            load("gs", (0, rows("w_in"), C_GS, P))
            load("glu", (0, rows("w_s5_glu"), 0, P), (4, rows("w_s5_glu"), D, P))
            sp.wait_ge(s["mm_done"], MM0 + ALLT)
            page_loads(sp, 0)
            sp.wait_ge(s["kv_used"], 4 + 30)
            sp.dma_start(attw, rows("w_att_proj")).then_inc(s["att_w_in"], 16)
            sp.wait_ge(s["kv_used"], 4 + 32)
            sp.wait_ge(s["ga_mm"], 16)
            w_out = rows("w_out")
            with sp.Fori(0, 2) as i:
                for j in range(4):
                    sp.wait_ge(s["lo_done"], i * 4 + (FFN_UNITS + j + FE0 - 3))
                    sp.dma_start(wraw[:, j, :, :], w_out[:, :, bass.ds(i * (4 * P) + j * P, P)]).then_inc(raw_in[j], 16)
            load_ffn(1, rows("w_ffn2_in"), rows("w_ffn2_out"))
            for k in range(5):
                sp.wait_ge(s["final_out"], k + 1)
                if k < 4:
                    sp.dma_start(out["y_prompt"][0, P * k:P * k + P, :], ytok[:, k, :]).then_inc(s["res_out"], 16)
                else:
                    sp.dma_start(out["y_sample"].rearrange("b s d -> (b s) d"), ytok[0:32, 4, :]).then_inc(s["res_out"], 16)
            for done, count in (("kidx_out", 2), ("kv_out", 4), ("res_out", 4 + 5)):
                sp.wait_ge(s[done], 16 * count)

        @block.tensor
        def _(pe):
            def acc(dst, pairs, **kw):
                for k, (a, b) in enumerate(pairs):
                    ins = pe.matmul(dst, a, b, start=(k == 0), stop=(k == len(pairs) - 1), **kw)
                return ins

            def slot_block(slot, k, m=P):
                return wslot[:, slot, k * P:k * P + m]

            def norm_sum(k):
                pe.wait_ge(s["sum_done"], (DK - 1) * (k + 1))
                for h in range(2):
                    ins = pe.matmul(ps[:, h, 0:HALF], ones[:], rstd[:, h * HALF:(h + 1) * HALF], start=True, stop=True)
                ins.then_inc(s["ssum_done"], 1)

            def linear(layer, outs):
                def body(i, slot, n, ready):
                    half = slot
                    pe.wait_ge(w_ready[slot], ready)
                    pe.wait_ge(s["evac"], n + (EV0 - 1))
                    for o, (k0, kb, x) in enumerate(outs):
                        for h in range(2):
                            ins = acc(ps[:, half * 4 + 2 * o + h, 0:HALF],
                                      [(slot_block(slot, k0 + k), x[:, k, h * HALF:(h + 1) * HALF]) for k in range(kb)])
                    ins.then_inc(s["mm_done"], 1)
                tiles(pe, layer, body)

            def unit(w_at, x_hi, x_lo, kb, bank, block_wait=None, lo_at=lambda k: k):
                for k in range(kb):
                    if block_wait is not None:
                        block_wait(k)
                    for a, x in ((wh, x_hi), (wh, x_lo), (wl, x_hi)):
                        for h in range(2):
                            ins = pe.matmul(ps[:, bank + h, 0:HALF], a[:, w_at, k, :], x[:, lo_at(k) if x is x_lo else k, h * HALF:(h + 1) * HALF],
                                            start=(k == 0 and a is wh and x is x_hi), stop=(k == kb - 1 and a is wl),
                                            skip_group_check=True)
                ins.then_inc(s["unit_done"], 1)

            def ffn(which):
                def norm_block(k):
                    pe.wait_ge((s["norm_even"], s["norm_odd"])[k % 2], DK // 2 * which + k // 2 + 1)

                def last_hidden(m, count):
                    def body(k):
                        if k == m - 1:
                            pe.wait_ge(s["act_ready"], count)
                    return body

                for kind, f0, m, u0, t0, a0 in ffn_plan(which):
                    if kind == "in":
                        with pe.Fori(0, m // 2) as i:
                            for j in range(4):
                                pe.wait_ge(s["lo_done"], i * 4 + (u0 + j + FE0 + 1))
                                if u0 == 0 and j in (1, 2):
                                    pe.wait_ge(*((s["shift_ev"], 1), (s["early_act"], 2))[j - 1])
                                if j % 2 == 0:
                                    pe.wait_ge(s["ffn_ev"], i * 2 + (t0 + j // 2 + FE0 - 1))
                                unit(j % 2, hnh, hnl, DK, 4 * (j // 2) + 2 * (j % 2), norm_block if f0 == 0 and j == 0 else None)
                    else:
                        pe.wait_ge(s["act_ready"], FE0 + a0 - 1)
                        with pe.Fori(0, 2) as i:
                            for j in range(4):
                                pe.wait_ge(s["lo_done"], i * 4 + (u0 + j + FE0 + 1))
                                pe.wait_ge(s["ffn_ev"], i * 4 + (t0 + j + FE0 - 1))
                                unit(j % 2, acth, actl, m, 4 * ((t0 + j) % 2), last_hidden(m, FE0 + a0) if j == 0 else None)

            pe.wait_ge(s["x_in"], 48)
            for k in range(DK):
                if k == 1:
                    pe.wait_ge(s["x_rest"], 16)
                if k >= 2:
                    pe.wait_ge(s["evac"], k - 1)
                b = 4 * (k % 2)
                for j in range(4):
                    pe.transpose(ps[:, b, P * j:P * j + P], xtok[:, j, P * k:P * k + P], ident[:])
                pe.transpose(ps[:, b + 1, 0:32], xtok[0:32, 4, P * k:P * k + P], ident[0:32, 0:32]).then_inc(s["mm_done"], 1)
            pe.wait_ge(s["pool_const"], 1)
            norm_sum(0)
            pe.wait_ge(s["oh_in"], 32)
            for k in range(2):
                ins = pe.matmul(ps[0:HEADS, 2 + k, 0:320], relb, ohp[0:NBKT, 320 * k:320 * k + 320], start=True, stop=True)
            ins.then_inc(s["shift_mm"], 1)
            pe.wait_ge(s["par_in"], 16 * 13)
            for c in range(2):
                for k in range(4):
                    pe.transpose(ps[:, 4 + c, P * k:P * k + P], craw[:, c, k, :], ident[:])
            for c in range(2):
                ins = pe.transpose(ps[:, 6, P * c:P * c + P], s0raw[:, c, :], ident[:])
            ins.then_inc(s["early_pe"], 1)
            ffn(0)
            norm_sum(1)
            pe.wait_ge(s["prep_done"], 1)
            for r in range(8):
                c, g4 = r // 4, r % 4
                if r == 6:
                    pe.wait_ge(s["sqrt_done"], 2)
                for q in range(4):
                    ins = pe.transpose(ps[:, (r + 2) % 8, P * q:P * q + P], wb[:, c, 4 * g4 + q, :, :].rearrange("p t j -> p (t j)"), ident[:])
                ins.then_inc(s["input_mats_turned"], 1)
            pe.wait_ge(s["input_mats_out"], 8)
            def tok_out(tt):
                return slice(P * tt, P * tt + (P if tt < 4 else 32))

            def idx_body(i, slot, n, ready):
                pe.wait_ge(w_ready[slot], ready)
                w = wslot[:, slot, 0:DK * NQI].rearrange("p (k n) -> p k n", k=DK)
                b = 4 * slot
                for m in range(2):
                    for k in range(DK):
                        if m == 0:
                            pe.wait_ge(s["norm_done"], k + 1)
                        pe.matmul(ps[:, b + m, :], w[:, k, P * m:P * m + P], hn[:, k, 0:SEQ], start=(k == 0), stop=(k == DK - 1))
                for tt in range(5):
                    m = P if tt < 4 else 32
                    acc(ps[0:m, b + 2, 40 * tt:40 * tt + 40], [(hn[:, k, tok_out(tt)], w[:, k, 256:296]) for k in range(DK)])
                acc(ps[0:32, b + 3, 0:256], [(hn[:, k, SEQ:NT], w[:, k, 0:256]) for k in range(DK)])
                acc(ps[0:8, b + 3, 256:288], [(w[:, k, 288:296], hn[:, k, SEQ:NT]) for k in range(DK)]).then_inc(s["mm_done"], 1)
            tiles(pe, "idx", idx_body)
            for r in range(4):
                if r >= 2:
                    pe.wait_ge(s["lag_kernels_out"], r - 1)
                for q in range(4):
                    gp = 4 * r + q
                    for h in range(2):
                        sl = slice(64 * h, 64 * h + 64)
                        ins = acc(ps[0:16, 4 + 2 * (r % 2) + h, P * q:P * q + P],
                                  [(bbar[sl, 0, gp, :], yre[sl, gp, 0:CH, :]), (bbar[sl, 1, gp, :], yim[sl, gp, 0:CH, :])])
                ins.then_inc(s["lag_kernels"], 1)
            pe.wait_ge(s["lag_kernels_out"], 4)
            pe.wait_ge(s["evac"], EV0 + first_tile["u"])

            def turn_tok(b, src):
                for tt in range(5):
                    m = P if tt < 4 else 32
                    dst = ps[:, b, P * tt:P * tt + P] if tt < 4 else ps[:, b + 1, 0:32]
                    ins = pe.transpose(dst, src(tt, m), ident[0:m, 0:m])
                return ins
            turn_tok(4, lambda tt, m: ki4[0:m, tt, :, :].rearrange("p r d -> p (r d)")).then_inc(s["index_keys_turned"], 1)
            for h in range(IH):
                ins = pe.transpose(ps[:, 6, 32 * h:32 * h + 32], qis4[:, h, :, :].rearrange("p r d -> p (r d)"), ident[0:32, 0:32])
            ins.then_inc(s["index_keys_turned"], 1)
            pe.wait_ge(s["index_keys_out"], 2)

            def logits(qb):
                w = P * (qb + 1)
                for h in range(IH):
                    x = 8 * (qb - 1) + h
                    r = slice(32 * (h % 4), 32 * (h % 4) + 32)
                    if x >= 4:
                        pe.wait_ge(s["relu_done"], x - 3)
                    pe.matmul(ps[:, LOGIT_BANK[h % 4], 0:w], qiT[r, h // 4, P * qb:P * qb + P], kiT[r, 0:w],
                              start=True, stop=True).then_inc(s["logits_ready"], 1)
            logits(1)
            linear("u", [(0, DK, hn)])
            logits(2)
            linear("q", [(0, DK, hn)])
            logits(3)
            pe.wait_ge(s["relu_done"], 24)
            pe.wait_ge(s["evac"], EV0 + first_tile["kv"])

            pe.wait_ge(s["u_in"], 16 * (CH + NS))
            for q in range(4):
                for g4 in range(4):
                    gp = 4 * q + g4
                    for h in range(2):
                        for c in range(2):
                            ins = pe.matmul(ps[64 * h:64 * h + 64, 2 * q + c, UC * g4:UC * g4 + UC], gb[:, c, gp, 64 * h:64 * h + 64],
                                            uch[:, 2 * gp + h, :], start=True, stop=True)
                ins.then_inc(s["chunk_inputs"], 1)
            pe.wait_ge(s["chunk_inputs_out"], 4)

            def kv_body(i, slot, n, ready):
                pe.wait_ge(w_ready[slot], ready)
                pe.wait_ge(s["evac"], n + (EV0 - 1))
                w = wslot[:, slot, 0:2048].rearrange("p (k n) -> p k n", k=DK)
                for tt in range(5):
                    m = P if tt < 4 else 32
                    ins = acc(ps[0:m, 4 * slot + tt // 2, 256 * (tt % 2):256 * (tt % 2) + 256],
                              [(hn[:, k, tok_out(tt)], w[:, k, :]) for k in range(DK)])
                ins.then_inc(s["mm_done"], 1)
            tiles(pe, "kv", kv_body)
            pe.wait_ge(s["evac"], EV0 + first_tile["gs"])
            for j in range(4):
                if j >= 2:
                    pe.wait_ge(s["keys_out"], j - 1)
                turn_tok(2 * (j % 2), lambda tt, m: ktok[0:m, tt, P * j:P * j + P]).then_inc(s["keys_turned"], 1)

            pe.wait_ge(s["toep_in"], 16 * 4 * CH)
            pe.wait_ge(s["keys_out"], 4)
            pe.wait_ge(s["scan_done"], 1)
            def outputs(q4):
                for g8 in range(8):
                    g = 8 * q4 + g8
                    q, gp, sl, c0 = 2 * q4 + g % 2, g // 2, slice(64 * (g % 2), 64 * (g % 2) + 64), P * (g8 // 2)
                    pe.matmul(ps[0:UC, q, c0:c0 + P], uch[:, g, :], toep[:, g, :], start=True, stop=False, skip_group_check=True)
                    for c, y in enumerate((yre, yim)):
                        pe.matmul(ps[0:NC, q, c0:c0 + P], vst[sl, c, gp, 0:NC], y[sl, gp, 1:9, :].rearrange("p k i -> p (k i)"),
                                  start=False, stop=False, skip_group_check=True)
                    for c, y in enumerate((yre, yim)):
                        ins = pe.matmul(ps[NC:UC, q, c0 + 64:c0 + P], s0[sl, c, :, gp], y[sl, gp, 1:5, :].rearrange("p k i -> p (k i)"),
                                        start=False, stop=(c == 1), skip_group_check=True)
                ins.then_inc(s["chunk_outputs"], 1)

            def turn_outputs(j):
                pe.wait_ge(s["chunk_outputs_out"], 2 * j + 2)
                for k in range(CH):
                    ins = pe.transpose(ps[:, 2 * j + k // 4, UC * (k % 4):UC * (k % 4) + UC],
                                       ybuf[:, j % 2, k, :, :].rearrange("p g i -> p (g i)"), ident[0:UC, 0:UC])
                ins.then_inc(s["y_turn"], 1)
            for q4 in range(4):
                outputs(q4)
                if q4:
                    turn_outputs(q4 - 1)
            turn_outputs(3)
            pe.wait_ge(s["y_turned"], 1)
            for c in range(2):
                pe.transpose(ps[:, 0, P * c:P * c + P], fin_s[:, c, :, :].rearrange("p b g -> p (b g)"), ident[:])
                ins = pe.transpose(ps[0:GP, 0, 256 + P * c:384 + P * c], fin_p[:, c, :], ident[:])
            ins.then_inc(s["fin_mm"], 1)

            cols = [(0, 512), (512, 1024), (1024, NKEY)]
            pe.wait_ge(s["fin_ev"], 1)
            pe.wait_ge(s["y_turned"], 4)
            pe.wait_ge(s["sample_prep"], 1)
            pe.matmul(ps[:, 3, 0:32], head_row, wT8, start=True, stop=True).then_inc(s["head_weights"], 1)
            pe.wait_ge(s["head_weights_out"], 1)
            pe.wait_ge(s["kidx_in"], 16 * NB * NPAGE)

            def turn_pages(both):
                if both:
                    pe.wait_ge(s["pages_out"], both)
                for k in range(4):
                    ins = pe.transpose(ps[:, 4, P * k:P * k + P], kidx[:, 16 * both + 4 * k:16 * both + 4 * k + 4, :].rearrange("p n d -> p (n d)"), ident[:])
                ins.then_inc(s["pages_turned"], 1)

            def sample_logits(b):
                q = slice(32 * (b % 4), 32 * (b % 4) + 32)
                for k in range(NPAGE):
                    r = slice(32 * (k % 4), 32 * (k % 4) + 32)
                    c0 = 256 * (b % 2) + P * (k // 4)
                    pe.matmul(ps[q, k % 4, P * (k // 4):P * (k // 4) + P], qis[r, b, :, :].rearrange("p h q -> p (h q)"),
                              kxT[r, b // 2 % 2, c0:c0 + P], start=True, stop=True, tile_position=(32 * (k % 4), 32 * (b % 4)))
                pe.matmul(ps[q, 0, 256:288], qis[0:32, b, :, :].rearrange("p h q -> p (h q)"), kiT[0:32, SEQ:NT],
                          start=True, stop=True, tile_position=(0, 32 * (b % 4))).then_inc(s["sample_logits"], 1)
            turn_pages(0)
            for both in range(NB // 2):
                if both + 1 < NB // 2:
                    turn_pages(both + 1)
                pe.wait_ge(s["pages_out"], both + 1)
                if both == 2:
                    pe.wait_ge(s["sample_relu"], 1)
                sample_logits(2 * both)
                sample_logits(2 * both + 1)
                if both % 2:
                    g = both // 2
                    pe.wait_ge(s["sample_relu"], g + 1)
                    for k, (c0, c1) in enumerate(cols):
                        ins = pe.matmul(ps[0:32, 5 + k, 0:c1 - c0], wsel[:, g, :], rls[:, c0:c1], start=(g == 0), stop=(g == 1))
                    ins.then_inc(s["sample_index"], 1)
            pe.wait_ge(s["sample_index_out"], 1)
            def tile_half(x, part):
                i = x // 2 % DK
                layer = "gs" if x < 16 else "glu"
                n = first_tile[layer] + i
                slot = n % 2
                if x % 2 == 0 and part == 0:
                    pe.wait_ge(w_ready[slot], slot_base[layer][slot] + (i // 2 + 1) * 16 * (1 if layer == "gs" else 2))
                    if layer == "gs":
                        pe.wait_ge(s["evac"], EV0 + n - 1)
                    else:
                        pe.wait_ge(s["evac"], EV0 + n)
                        if i == 0:
                            pe.wait_ge(s["gelu_done"], 2)
                if layer == "gs":
                    h = x % 2
                    for k in range(4 * part, 4 * part + 4):
                        ins = pe.matmul(ps[:, 4 * slot + h, 0:HALF], slot_block(slot, k), hn[:, k, h * HALF:(h + 1) * HALF],
                                        start=(k == 0), stop=(k == DK - 1), skip_group_check=True)
                else:
                    o = x % 2
                    ins = acc(ps[:, 4 * o + part, 0:HALF], [(slot_block(slot, 4 * o + k), gT[:, k, part * HALF:(part + 1) * HALF]) for k in range(4)])
                if x % 2 and part:
                    ins.then_inc(s["mm_done"], 1)

            def p_scores(x):
                qb, h = x // 8, x % 8
                w = P * (qb + 1)
                r = slice(64 * (h % 2), 64 * (h % 2) + 64)
                if x:
                    pe.wait_ge(s["scores_biased"], x)
                pe.matmul(ps[:, 2, 0:w], qT[r, h // 2, P * qb:P * qb + P], kT[r, h // 2, 0:w], start=True, stop=True).then_inc(s["scores_ready"], 1)

            def p_turn(x):
                qb = x // 8
                pe.wait_ge(s["probs_ready"], x + 1)
                if x:
                    pe.wait_ge(s["probs_out"], x)
                for k in range(qb + 1):
                    ins = pe.transpose(ps[:, 3, P * k:P * k + P], pexp[:, x % 2, P * k:P * k + P], ident[:])
                ins.then_inc(s["probs_turned"], 1)

            def p_values(x):
                qb, h = x // 8, x % 8
                pe.wait_ge(s["probs_out"], x + 1)
                if h == 0 and qb:
                    pe.wait_ge(s["att_scaled"], qb)
                acc(ps[:, 6, HD * h:HD * h + HD],
                    [(pT[:, x % 2, P * k:P * k + P], vtok[:, k, HD * h:HD * h + HD]) for k in range(qb + 1)]).then_inc(s["values_ready"], 1)

            def p_turn_out(qb):
                pe.wait_ge(s["att_scaled"], qb + 1)
                if qb:
                    pe.wait_ge(s["att_out"], qb)
                for j in range(4):
                    ins = pe.transpose(ps[:, 7, P * j:P * j + P], ao[:, qb % 2, P * j:P * j + P], ident[:])
                ins.then_inc(s["att_turned"], 1)

            for x in range(34):
                if x < 32:
                    p_scores(x)
                    tile_half(x, 0)
                if 1 <= x < 33:
                    p_turn(x - 1)
                if x < 32:
                    tile_half(x, 1)
                if x >= 2:
                    p_values(x - 2)
                if x >= 2 and (x - 2) % 8 == 7:
                    p_turn_out((x - 2) // 8)
            pe.wait_ge(s["evac"], EV0 + ALLT)
            pe.wait_ge(s["sample_onehot_in"], 16)
            for b, (c0, c1) in enumerate(cols):
                ins = pe.matmul(ps[:, b, 0:c1 - c0], rbexp, ohs[:, c0:c1], start=True, stop=True)
            ins.then_inc(s["sample_bias"], 1)
            pe.wait_ge(s["sample_bias_out"], 1)
            pe.wait_ge(s["att_out"], 4)
            pe.wait_ge(s["sample_selected"], 1)

            def k_turn(g, i):
                n = 8 * g + i
                for half in range(2):
                    pe.wait_ge(kv_in[half][i % 4], 32 * (4 * g + i // 4 + 1))
                if i:
                    pe.wait_ge(s["k_out_act"], n)
                    pe.wait_ge(s["k_out_dve"], n)
                for j in range(4):
                    for k in range(4):
                        ins = pe.transpose(ps[:, 3 + j, P * k:P * k + P], kring[i % 4][:, k, P * j:P * j + P], ident[:])
                    ins.then_inc(s["k_turned"], 1)

            def k_score(g, i):
                n = 8 * g + i
                b, q = 4 * g + i // 2, slice(32 * (i // 2), 32 * (i // 2) + 32)
                pe.wait_ge(s["k_out_act"], n + 1)
                pe.wait_ge(s["k_out_dve"], n + 1)
                for j in range(4):
                    ins = pe.matmul(ps[q, i % 2, :], qbd[:, j, b, :], pgT[:, n % 2, j, :], start=False, stop=(j == 3), skip_group_check=True)
                ins.then_inc(s["k_scored"], 1)
                if i % 2:
                    for j in range(4):
                        ins = pe.matmul(ps[q, 2, 0:32], qbd[:, j, b, :], kT[:, j, SEQ:NT], start=False, stop=(j == 3), skip_group_check=True)
                    if i == 7:
                        ins.then_inc(s["sample_scores"], 1)

            def ga_half(m):
                i, h = m // 2, m % 2
                if h == 0:
                    pe.wait_ge(ga_in[i % 2], 16 * (i // 2 + 1))
                if m:
                    pe.wait_ge(s["ga_ev"], m)
                acc(ps[:, 7, 0:HALF], [(gaw[:, i % 2, k, :], hn[:, k, h * HALF:(h + 1) * HALF]) for k in range(DK)]).then_inc(s["ga_mm"], 1)

            for g in range(2):
                if g:
                    pe.wait_ge(s["sample_biased"], g)
                    pe.wait_ge(s["sample_probs_out"], g)
                    pe.wait_ge(s["sample_values_out"], g)
                for k, (c0, c1) in enumerate(cols):
                    pe.matmul(ps[:, k, 0:c1 - c0], tok_row[:, g, :], sels[:, c0:c1], start=True, stop=False, skip_group_check=True)
                for i in range(8):
                    k_turn(g, i)
                    if i:
                        k_score(g, i - 1)
                    if i in GA_AFTER_K:
                        ga_half(8 * g + GA_AFTER_K.index(i))
                k_score(g, 7)
                ga_half(8 * g + 4)
                ga_half(8 * g + 5)
                pe.wait_ge(s["ga_ev"], 8 * g + 6)
                pe.wait_ge(s["sample_exp"], g + 1)
                for k in range(NPAGE):
                    pe.transpose(ps[:, 6 + k // 4, P * (k % 4):P * (k % 4) + P], pes[:, P * k:P * k + P], ident[:])
                pe.transpose(ps[0:32, 5, 0:P], pes[:, PAST:NKEY], ident[:]).then_inc(s["sample_probs_turned"], 1)
                pe.wait_ge(s["sample_probs_out"], g + 1)
                for i in range(8):
                    q = slice(32 * (i // 2), 32 * (i // 2) + 32)
                    for half in range(2):
                        pe.wait_ge(kv_in[half][i % 4], 32 * (4 * g + 2 + i // 4 + 1))
                    for k in range(4):
                        ins = pe.matmul(ps[q, 5, :], ptS[:, 4 * (i % 2) + k, q], kring[i % 4][:, k, :], start=(i % 2 == 0 and k == 0),
                                        stop=False, skip_group_check=True)
                    ins.then_inc(s["kv_used"], 1)
                    if i % 2:
                        ins = pe.matmul(ps[q, 5, :], ptS[0:32, 8, q], vtok[0:32, 4, :], start=False, stop=True, skip_group_check=True)
                        if i == 7:
                            ins.then_inc(s["sample_values"], 1)
                    if i in GA_AFTER_V:
                        ga_half(8 * g + 6 + GA_AFTER_V.index(i))
            pe.wait_ge(s["sample_values_out"], 2)
            for j in range(4):
                ins = acc(ps[:, 6, 32 * j:32 * j + 32], [(osel[:, g, P * j:P * j + P], row_tok[:, g, :]) for g in range(2)])
            ins.then_inc(s["sample_att_turned"], 1)
            pe.wait_ge(s["sample_att_out"], 1)

            pe.wait_ge(s["att_w_in"], 16)
            for i in range(DK):
                if i >= 2:
                    pe.wait_ge(s["att_ev"], i - 1)
                for h in range(2):
                    ins = acc(ps[:, 4 * (i % 2) + h, 0:HALF], [(attw[:, k, P * i:P * i + P], attT[:, k, h * HALF:(h + 1) * HALF]) for k in range(4)])
                ins.then_inc(s["att_mm"], 1)
            def mix_ready(k):
                pe.wait_ge(s["mix_ready"], k + 1)
            pe.wait_ge(s["att_ev"], DK)
            with pe.Fori(0, 2) as i:
                for j in range(4):
                    pe.wait_ge(s["lo_done"], i * 4 + (FFN_UNITS + j + FE0 + 1))
                    pe.wait_ge(s["ffn_ev"], i * 4 + (FFN_TILES + j + FE0 - 1))
                    unit(j % 2, acth, actl, DK, 4 * (j % 2), mix_ready if j == 0 else None, mix_low_at)
            norm_sum(2)
            ffn(1)
            norm_sum(3)
            for k in range(5):
                m = P if k < 4 else 32
                if k >= 2:
                    pe.wait_ge(s["final_out"], k - 1)
                for j in range(DK):
                    if k == 0:
                        pe.wait_ge(s["norm_done"], DK + j + 1)
                    ins = pe.transpose(ps[0:m, 2 + 2 * (k % 2) + j // 4, P * (j % 4):P * (j % 4) + P], hn[:, j, P * k:P * k + m], ident[:])
                ins.then_inc(s["final_turned"], 1)

        @block.scalar
        def _(act_e):
            def square(k, j):
                act_e.wait_ge(*h_ready(k, j))
                act_e.activation(hn[:, j, :], hT[:, j, :], ACT.Square).then_inc(s["sq_done"], 1)

            def root(k):
                act_e.activation(rootwarm, epsc[:, 0:1], ACT.Sqrt)
                act_e.wait_ge(s["ssum_done"], k + 1)
                act_e.activation(rstd[:].rearrange("p (h n) -> p h n", h=2), ps[:, 0:2, 0:HALF], ACT.Sqrt, bias=epsc[:, 0:1],
                                 scale=1.0 / D).then_inc(s["sqrt_done"], 1)

            def two(ap):
                return ap.rearrange("p (h n) -> p h n", h=2)

            def pair(half, o):
                return ps[:, 4 * half + 2 * o:4 * half + 2 * o + 2, 0:HALF]

            def high(u, i, j):
                act_e.wait_ge(raw_in[j], i * 16 + 16 * (u // 4 + 1))
                if not (isinstance(i, int) and u + 4 * i < 2):
                    act_e.wait_ge(s["unit_done"], i * 4 + (u - 1))
                act_e.activation(wh[:, j % 2, :, :], wraw[:, j, :, :], ACT.Copy).then_inc(s["hi_done"], 1)

            def gain(k, j):
                act_e.wait_ge(s["scaled"], DK * (k // 2) + j + 1)
                act_e.activation(hn[:, j, :], hn[:, j, :], ACT.Copy, scale=gains[:, k, j:j + 1]).then_inc(s["norm_done"], 1)

            def norm_high(which):
                for j in range(DK):
                    act_e.wait_ge(s["nrm_done"], DK * which + j + 1)
                    act_e.activation(hnh[:, j, :], nrm[:, j, :], ACT.Copy).then_inc(s["hnh_done"], 1)

            def first_units(which):
                for j in range(2):
                    high(FIRST_UNIT[which] + j, 0, j)

            def ffn(which):
                end = FIRST_UNIT[which] + FFN_UNITS
                for kind, f0, m, u0, t0, a0 in ffn_plan(which):
                    if kind == "in":
                        with act_e.Fori(0, m // 2) as i:
                            for j in range(2):
                                high(u0 + 2 * j + 2, i, (2 * j + 2) % 4)
                                act_e.wait_ge(s["act_ready"], i * 2 + (a0 + j + FE0 - 1))
                                act_e.activation(two(sg[:, j, :]), pair(j, 0), ACT.Silu).then_inc(s["silu_done"], 1)
                                high(u0 + 2 * j + 3, i, (2 * j + 3) % 4)
                                act_e.wait_ge(s["ffn_ev"], i * 2 + (t0 + j + FE0 + 1))
                                act_e.activation(one(acth, i * 2 + j), sg[:, j, :], ACT.Copy).then_inc(s["acth_done"], 1)
                    elif u0 + DK < end:
                        with act_e.Fori(0, 2) as i:
                            for j in range(4):
                                high(u0 + j + 2, i, (j + 2) % 4)
                    else:
                        for j in range(DK):
                            if j < DK - 2:
                                high(u0 + j + 2, 0, (j + 2) % 4)
                            square(2 * which + 1, j)

            act_e.dma_start(ohp[0:NBKT, :], t["oh_prompt"]).then_inc(s["oh_in"], 16)
            act_e.dma_start(relb, t["rel_bias"]).then_inc(s["oh_in"], 16)
            for k, n in enumerate(("g_ffn1", "g_mix", "g_ffn2", "g_final")):
                src = t[n] if n == "g_final" else t[n][0]
                act_e.dma_start(gains[:, k, :], src.rearrange("(k p) -> p k", p=P)).then_inc(s["const_in"], 16)
            act_e.wait_ge(s["pool_const"], 1)
            for j in range(DK):
                square(0, j)
            first_units(0)
            root(0)
            norm_high(0)
            act_e.wait_ge(s["par_in"], 16 * 13)
            act_e.activation(ldt, ldt, ACT.Exp).then_inc(s["dt_done"], 1)
            act_e.wait_ge(s["shift_mm"], 1)
            act_e.activation(shrow.rearrange("p (b n) -> p b n", b=2), ps[0:HEADS, 2:4, 0:320], ACT.Copy).then_inc(s["shift_ev"], 1)
            act_e.wait_ge(s["shift_ev"], 1)
            act_e.dma_start(scr_shift, shrow.unsqueeze(1).broadcast_to([HEADS, P, 640])).then_inc(s["shift_out"], 16)
            act_e.wait_ge(s["early_pe"], 1)
            for c in range(2):
                for h in range(2):
                    src = ps[64 * h:64 * h + 64, 4 + c, :].rearrange("p (g s i) -> p g s i", s=2, i=GC)[:, :, h, :]
                    ins = act_e.activation(cT[64 * h:64 * h + 64, c, :, :], src, ACT.Copy, scale=1.0 if c == 0 else -1.0)
            ins.then_inc(s["early_act"], 1)
            act_e.activation(s0[:].rearrange("p c b g -> p (c b g)"), ps[:, 6, 0:256], ACT.Copy).then_inc(s["early_act"], 1)
            act_e.wait_ge(s["ang_done"], 1)
            act_e.activation(v(7), v(2), ACT.Sin).then_inc(s["trig_done"], 1)
            act_e.activation(v(8), v(2), ACT.Sin, scale=0.5).then_inc(s["trig_done"], 1)
            act_e.activation(v(4), v(1), ACT.Exp).then_inc(s["trig_done"], 1)
            ffn(0)
            root(1)
            for r in range(8):
                act_e.wait_ge(s["input_mats_turned"], r + 1)
                act_e.activation(gb[:, r // 4, 4 * (r % 4):4 * (r % 4) + 4, :].rearrange("p g n -> p (g n)"), ps[:, (r + 2) % 8, :], ACT.Copy).then_inc(s["input_mats_out"], 1)
                gain(1, r)

            def relus(qb):
                w = P * (qb + 1)
                for h in range(IH):
                    x = 8 * (qb - 1) + h
                    act_e.wait_ge(s["logits_ready"], x + 1)
                    if x >= 2:
                        act_e.wait_ge(s["index_added"], x - 1)
                    act_e.activation(rl[:, x % 2, 0:w], ps[:, LOGIT_BANK[h % 4], 0:w], ACT.Relu).then_inc(s["relu_done"], 1)
            relus(1)
            for i in range(4):
                n = first_tile["u"] + i
                half = n % 2
                act_e.wait_ge(s["mm_done"], MM0 + n + 1)
                o = uT[:, i, 0:SEQ].rearrange("p (t n) -> p n t", t=CH)
                c = HALF // CH
                act_e.activation(o[:, 0:c, :], ps[:, 4 * half, 0:HALF].rearrange("p (n t) -> p n t", t=CH), ACT.Copy)
                act_e.activation(o[:, c:NC, :], ps[:, 4 * half + 1, 0:SEQ - HALF].rearrange("p (n t) -> p n t", t=CH), ACT.Copy)
                act_e.activation(uT[:, i, SEQ:NT].rearrange("p (t n) -> p n t", t=NS),
                                 ps[:, 4 * half + 1, SEQ - HALF:HALF].rearrange("p (n t) -> p n t", t=NS), ACT.Copy).then_inc(s["evac"], 1)
            act_e.wait_ge(s["evac"], EV0 + first_tile["u"] + 4)
            for k in range(4):
                act_e.dma_start(scr_u[:, k].rearrange("t p n -> p t n"), uT[:, k, 0:SEQ].rearrange("p (t n) -> p t n", t=CH)).then_inc(s["u_out"], 16)
                act_e.dma_start(scr_us[:, k].rearrange("t p n -> p t n"), uT[:, k, SEQ:NT].rearrange("p (t n) -> p t n", t=NS)).then_inc(s["u_out"], 16)
            relus(2)
            for i in range(4):
                n = first_tile["q"] + i
                act_e.wait_ge(s["mm_done"], MM0 + n + 1)
                act_e.activation(two(qT[:, i, :]), pair(n % 2, 0), ACT.Copy, scale=HD ** -0.5).then_inc(s["evac"], 1)
                if i == 1:
                    act_e.wait_ge(s["u_out"], 16 * 8)
                    act_e.wait_ge(s["u_zero"], 1)
                    for k in range(CH):
                        act_e.dma_start(uch[16 * k:16 * k + 16, :, 0:NC], scr_u[k].rearrange("q (g c) n -> c (q g) n", c=GC)).then_inc(s["u_in"], 16)
                    for k in range(NS):
                        act_e.dma_start(uch[64 + 16 * k:80 + 16 * k, :, NC:UC], scr_us[k].rearrange("q (g c) n -> c (q g) n", c=GC)).then_inc(s["u_in"], 16)
            relus(3)
            for q in range(4):
                act_e.wait_ge(s["chunk_inputs"], q + 1)
                for c in range(2):
                    ins = act_e.activation(vst[:, c, 4 * q:4 * q + 4, 1:1 + UC], ps[:, 2 * q + c, 0:4 * UC].rearrange("p (g n) -> p g n", g=4), ACT.Copy)
                ins.then_inc(s["chunk_inputs_out"], 1)
            act_e.wait_ge(s["pt_in"], 16)
            for i in range(4):
                n = first_tile["kv"] + i
                half, c0 = n % 2, 256 * (i % 2)
                dst = (ktok, vtok)[i // 2]
                for k in range(ACT_PAGES):
                    kidx_page(act_e, NB * NPAGE - ACT_PAGES * (4 - i) + k)
                act_e.wait_ge(s["mm_done"], MM0 + n + 1)
                act_e.activation(dst[:, 0:4, c0:c0 + 256].rearrange("p (a b) n -> p a b n", a=2),
                                 ps[:, 4 * half:4 * half + 2, :].rearrange("p a (b n) -> p a b n", b=2), ACT.Copy)
                act_e.activation(dst[0:32, 4, c0:c0 + 256], ps[0:32, 4 * half + 2, 0:256], ACT.Copy).then_inc(s["evac"], 1)
            for j in range(4):
                act_e.wait_ge(s["keys_turned"], j + 1)
                act_e.activation(kT[:, j, 0:SEQ], ps[:, 2 * (j % 2), :], ACT.Copy)
                act_e.activation(kT[:, j, SEQ:NT], ps[:, 2 * (j % 2) + 1, 0:32], ACT.Copy).then_inc(s["keys_out"], 1)
            def outputs(q4):
                act_e.wait_ge(s["chunk_outputs"], q4 + 1)
                if q4 >= 2:
                    act_e.wait_ge(s["y_turn"], q4 - 1)
                for h in range(2):
                    act_e.activation(ybuf[:, q4 % 2, :, h::2, :].rearrange("p k g i -> p g k i"),
                                     ps[0:UC, 2 * q4 + h, :].rearrange("p (g k i) -> p g k i", g=4, k=CH), ACT.Copy).then_inc(s["chunk_outputs_out"], 1)

            def turned(j):
                act_e.wait_ge(s["y_turn"], j + 1)
                src = ps[:, 2 * j:2 * j + 2, 0:4 * UC].rearrange("p b (k n) -> p b k n", k=4)
                act_e.activation(yT[:, j, 0:SEQ].rearrange("p (b k n) -> p b k n", b=2, k=4), src[:, :, :, 0:NC], ACT.Copy)
                act_e.activation(yT[:, j, SEQ:NT].rearrange("p (k n) -> p k n", k=NS), src[:, 1, :, NC:UC], ACT.Copy).then_inc(s["y_turned"], 1)
            for q4 in range(4):
                outputs(q4)
                if q4:
                    turned(q4 - 1)
            turned(3)
            act_e.wait_ge(s["y_turned"], 4)
            act_e.activation(gT[:, :, 0:SEQ].rearrange("p k (n t) -> p k n t", t=CH),
                             yT[:, :, 0:SEQ].rearrange("p k (t n) -> p k n t", t=CH), ACT.Gelu_apprx_tanh).then_inc(s["gelu_done"], 1)
            act_e.activation(gT[:, :, SEQ:NT].rearrange("p k (n t) -> p k n t", t=NS),
                             yT[:, :, SEQ:NT].rearrange("p k (t n) -> p k n t", t=NS), ACT.Gelu_apprx_tanh).then_inc(s["gelu_done"], 1)
            act_e.wait_ge(s["fin_mm"], 1)
            act_e.wait_ge(s["kidx_out"], 32)
            act_e.activation(fin_t[:, 0:256], ps[:, 0, 0:256], ACT.Copy)
            act_e.activation(fin_t[0:GP, 256:512], ps[0:GP, 0, 256:512], ACT.Copy).then_inc(s["fin_ev"], 1)
            act_e.wait_ge(s["gelu_done"], 2)
            act_e.dma_start(ohs, t["oh_sample"]).then_inc(s["sample_onehot_in"], 16)
            act_e.wait_ge(s["shift_out"], 16)
            for h in range(HEADS):
                row = scr_shift[h].rearrange("p n -> (p n)")[127:127 + 639 * P].rearrange("(p n) -> p n", n=639)[:, 0:SEQ]
                act_e.dma_start(tb[:, h, :], row).then_inc(s["bias_in"], 16)
            for g in range(2):
                act_e.wait_ge(s["sample_logits"], 4 * g + 4)
                if g:
                    act_e.wait_ge(s["sample_index"], g)
                for k in range(4):
                    act_e.activation(rls[:, 0:PAST].rearrange("p (j r n) -> p r j n", j=2, r=4)[:, k],
                                     ps[:, k, 0:256].rearrange("p (j n) -> p j n", j=2), ACT.Relu)
                act_e.activation(rls[:, PAST:NKEY], ps[:, 0, 256:288], ACT.Relu).then_inc(s["sample_relu"], 1)

            def tile_out(tl):
                i, layer = tl % DK, ("gs", "glu")[tl // DK]
                n = first_tile[layer] + i
                act_e.wait_ge(s["mm_done"], MM0 + n + 1)
                if layer == "gs":
                    act_e.activation(two(mixed[:, i, :]), pair(n % 2, 0), ACT.Sigmoid).then_inc(s["evac"], 1)
                else:
                    act_e.wait_ge(s["pool_gated"], i + 1)
                    act_e.activation(two(val[:, n % 2, :]), pair(0, 0), ACT.Copy)
                    act_e.activation(two(sg[:, n % 2, :]), pair(1, 0), ACT.Sigmoid).then_inc(s["evac"], 1)

            for x in range(33):
                if x and x % 2 == 0:
                    tile_out(x // 2 - 1)
                if x < 32:
                    w = P * (1 + x // 8)
                    act_e.wait_ge(s["scores_biased"], x + 1)
                    if x >= 2:
                        act_e.wait_ge(s["probs_turned"], x - 1)
                    if x % 8 == 0 and x >= 16:
                        act_e.wait_ge(s["att_scaled"], x // 8 - 1)
                    act_e.activation(pexp[:, x % 2, 0:w], smx[:, x % 2, 0:w], ACT.Exp, scale=-1.0, bias=nmx[:, x % 2:x % 2 + 1],
                                     accum_out=rsum[:, x // 8 % 2, x % 8:x % 8 + 1]).then_inc(s["probs_ready"], 1)
                if x >= 1:
                    w = P * (1 + (x - 1) // 8)
                    act_e.wait_ge(s["probs_turned"], x)
                    if x >= 3:
                        act_e.wait_ge(s["values_ready"], x - 2)
                    act_e.activation(pT[:, (x - 1) % 2, 0:w], ps[:, 3, 0:w], ACT.Copy).then_inc(s["probs_out"], 1)
            def ga_load(i):
                act_e.dma_start(gaw[:, i % 2, :, :], t["w_in"][0].rearrange("(k p) n -> p k n", p=P)[:, :, C_GA + P * i:C_GA + P * i + P]).then_inc(ga_in[i % 2], 16)

            def ga_out(m):
                act_e.wait_ge(s["ga_mm"], m + 1)
                i, h = m // 2, m % 2
                act_e.activation(ga_s[i][:, h * HALF:(h + 1) * HALF], ps[:, 7, 0:HALF], ACT.Sigmoid).then_inc(s["ga_ev"], 1)
                if h and i + 2 < DK:
                    ga_load(i + 2)
            act_e.wait_ge(s["sample_bias"], 1)
            ga_load(0)
            ga_load(1)
            for g in range(2):
                for i in range(8):
                    n = 8 * g + i
                    act_e.wait_ge(s["k_turned"], 4 * n + 2)
                    if n >= 2:
                        act_e.wait_ge(s["k_scored"], n - 1)
                    act_e.activation(pgT[:, n % 2, 0:2, :], ps[:, 3:5, :], ACT.Copy).then_inc(s["k_out_act"], 1)
                    if i in GA_AFTER_K:
                        ga_out(8 * g + GA_AFTER_K.index(i))
                ga_out(8 * g + 4)
                act_e.wait_ge(s["sample_biased"], g + 1)
                act_e.activation(pes, sms, ACT.Exp, scale=-1.0, bias=nmx[:, g:g + 1], accum_out=rsum[:, 0, g:g + 1]).then_inc(s["sample_exp"], 1)
                ga_out(8 * g + 5)
                act_e.wait_ge(s["sample_probs_turned"], g + 1)
                if g:
                    act_e.wait_ge(s["sample_values"], g)
                act_e.activation(ptS[:, 0:8, :].rearrange("p (b k) n -> p b (k n)", b=2), ps[:, 6:8, :], ACT.Copy)
                act_e.activation(ptS[0:32, 8, :], ps[0:32, 5, 0:P], ACT.Copy).then_inc(s["sample_probs_out"], 1)
                ga_out(8 * g + 6)
                ga_out(8 * g + 7)
            act_e.wait_ge(s["sample_att_turned"], 1)
            act_e.wait_ge(s["pool_gated"], 2 + 8)

            def mix_high(i):
                act_e.wait_ge(s["mix_done"], i + 1)
                act_e.activation(acth[:, i, :], fin_mix[:, i % 2, :], ACT.Copy).then_inc(s["mixh_done"], 1)

            for i in range(DK - 1):
                mix_high(i)
            for j in range(2):
                high(FFN_UNITS + j, 0, j)
            mix_high(DK - 1)
            for j in range(DK - 1):
                high(FFN_UNITS + 2 + j, 0, (j + 2) % 4)
                square(2, j)
            square(2, DK - 1)
            high(FFN_UNITS + 1 + DK, 0, (DK + 1) % 4)
            root(2)
            norm_high(1)
            ffn(1)
            root(3)
            for j in range(DK):
                gain(3, j)

        @block.gpsimd
        def _(pool):
            pool.memset(ones[:], 1.0)
            pool.memset(epsc[:], EPS).then_inc(s["pool_const"], 1)
            for c, n in enumerate(("s5_lam_re", "s5_lam_im")):
                pool.dma_start(lam[:, c, :], t[n][0].rearrange("(g s) p -> (s p) g", s=2)).then_inc(s["par_in"], 16)
            for h in range(2):
                pool.dma_start(ldt[64 * h:64 * h + 64, :], t["s5_log_dt"][0].rearrange("(g s) -> s g", s=2)[h:h + 1, :]
                                .broadcast_to([64, GP])).then_inc(s["par_in"], 16)
            for c, n in enumerate(("s5_b_re", "s5_b_im")):
                pool.dma_start(bmat[:, c, :, :], t[n][0].rearrange("(g s) p j -> (s p) g j", s=2)).then_inc(s["par_in"], 16)
            for c, n in enumerate(("s5_c_re", "s5_c_im")):
                for h in range(2):
                    pool.dma_start(craw[:, c, :, 64 * h:64 * h + 64],
                                    t[n][0].rearrange("g i p -> (g i) p").rearrange("(t q) p -> q t p", q=P)).then_inc(s["par_in"], 16)
            for c, n in enumerate(("state_s5_re", "state_s5_im")):
                pool.dma_start(s0raw[:, c, :], t[n][0].rearrange("b (g s) p -> (b g) (s p)", s=2)).then_inc(s["par_in"], 16)
            pool.dma_start(dd.rearrange("p g i -> p (g i)"), t["s5_d"].broadcast_to([GC, G * GC])).then_inc(s["par_in"], 16)
            pool.dma_start(caus[:], t["causal"]).then_inc(s["caus_in"], 16)
            pool.dma_start(pt_sb[:], t["page_table"].rearrange("b (o n) -> o (b n)", o=1)).then_inc(s["pt_in"], 16)
            pool.sem_inc(s["pool_gated"], 2)

            def norm_low(which):
                for j in range(1, DK, 2):
                    pool.wait_ge(s["hnh_done"], DK * which + j + 1)
                    pool.tensor_tensor(hnl[:, j, :], nrm[:, j, :], hnh[:, j, :].bitcast(F32), ALU.subtract).then_inc(s["norm_odd"], 1)
            norm_low(0)
            pool.wait_ge(s["pow_done"], 1)
            pool.wait_ge(s["early_act"], 1)

            def product(n0, i, ar, ai, xr, xi, o_re, o_im, sub_re, sub_im):
                for o, a, b in ((pt1, xr, ar), (pt2, xi, ai), (pt3, xi, ar), (pt4, xr, ai)):
                    ins = pool.tensor_tensor(o, a, b, ALU.mult)
                    ins.then_inc(s["pool_step"], 1)
                pool.wait_ge(s["pool_step"], i * 6 + (n0 + 4))
                pool.tensor_tensor(o_re, pt1, pt2, sub_re).then_inc(s["pool_step"], 1)
                pool.tensor_tensor(o_im, pt3, pt4, sub_im).then_inc(s["pool_step"], 1)
                pool.wait_ge(s["pool_step"], i * 6 + (n0 + 6))

            def power(k, c):
                return apow[:, bass.ds(k, 1), c, :].rearrange("p a g -> p (a g)").unsqueeze(2).broadcast_to([P, GP, GC])

            def at_lag(a, k):
                return a[:, :, bass.ds(k, 1), :].rearrange("p g a i -> p g (a i)")
            with pool.Fori(0, 9) as k:
                product(0, k, power(k, 0), power(k, 1), cT[:, 0], cT[:, 1], at_lag(yre, k), at_lag(yim, k), ALU.add, ALU.subtract)
            with pool.Fori(0, CH) as k:
                product(54, k, power(k * -1 + 7, 0), power(k * -1 + 7, 1), bbar[:, 0], bbar[:, 1],
                        at_lag(wb[:, 0], k), at_lag(wb[:, 1], k), ALU.subtract, ALU.add)
            pool.sem_inc(s["prep_done"], 1)
            pool.wait_ge(s["unit_done"], FFN_UNITS)
            pool.memset(toep[:].rearrange("p g n -> p (g n)"), 0.0).then_inc(s["toep_zero"], 1)
            pool.wait_ge(s["toep_zero"], 1)
            for r in range(4):
                pool.wait_ge(s["lag_kernels_out"], r + 1)
                for k in range(CH):
                    pool.dma_start(toep[16 * k:16 * k + 16, 8 * r:8 * r + 8, 16 * k:P],
                                   kbuf[r][:, :, 0:P - 16 * k]).then_inc(s["toep_in"], 16)
            pool.wait_ge(s["toep_in"], 16 * 4 * CH)
            pool.memset(uch[0:64, :, NC:UC], 0.0).then_inc(s["u_zero"], 1)

            steps = [6 * (9 + CH)]

            def link(*ops):
                for ins in ops:
                    steps[0] += 1
                    ins.then_inc(s["pool_step"], 1)
                pool.wait_ge(s["pool_step"], steps[0])

            def advance(dst, src, a, shape):
                w = int(np.prod(shape))
                tm = [prodmem[:, w * k:w * (k + 1)] for k in range(4)]
                if len(shape) == 2:
                    tm = [x.rearrange("p (a b) -> p a b", a=shape[0]) for x in tm]
                tt = pool.tensor_tensor
                link(tt(tm[0], src[0], a[0], ALU.mult), tt(tm[1], src[1], a[1], ALU.mult),
                     tt(tm[2], src[0], a[1], ALU.mult), tt(tm[3], src[1], a[0], ALU.mult))
                link(tt(tm[0], tm[0], tm[1], ALU.subtract), tt(tm[2], tm[2], tm[3], ALU.add))
                link(tt(dst[0], dst[0], tm[0], ALU.add), tt(dst[1], dst[1], tm[2], ALU.add))

            pool.wait_ge(s["chunk_inputs_out"], 4)
            pool.wait_ge(s["index_keys_out"], 2)
            link(pool.memset(vst[:, :, :, 0:1], 0.0))
            vb = vst[:, :, :, 1:1 + NC].rearrange("p c g (b j) -> p c g b j", j=8)
            for j in range(1, 8):
                advance([vb[:, c, :, :, j] for c in range(2)], [vb[:, c, :, :, j - 1] for c in range(2)],
                        [cpow[:, 1, c, :].unsqueeze(2).broadcast_to([P, GP, 8]) for c in range(2)], (GP, 8))
            for b_ in range(1, 8):
                advance([vb[:, c, :, b_, 7] for c in range(2)], [vb[:, c, :, b_ - 1, 7] for c in range(2)],
                        [cpow[:, 8, c, :] for c in range(2)], (GP,))
            for j in range(7):
                advance([vb[:, c, :, 1:8, j] for c in range(2)], [vb[:, c, :, 0:7, 7] for c in range(2)],
                        [cpow[:, j + 1, c, :].unsqueeze(2).broadcast_to([P, GP, 7]) for c in range(2)], (GP, 7))
            link(*[pool.tensor_copy(fin_s[:, c, :, :], vst[:, c, :, 1 + NC:1 + UC].rearrange("p g b -> p b g")) for c in range(2)],
                 *[pool.tensor_copy(fin_p[:, c, :], vst[:, c, :, NC]) for c in range(2)])
            advance([fin_s[:, c] for c in range(2)], [s0[:, c] for c in range(2)],
                    [apow[:, 4, c, :].unsqueeze(1).broadcast_to([P, NB, GP]) for c in range(2)], (NB, GP))
            pool.sem_inc(s["scan_done"], 1)

            pool.wait_ge(s["bias_in"], 16 * HEADS)
            pool.wait_ge(s["caus_in"], 16)
            pool.wait_ge(s["gelu_done"], 2)
            for x in range(33):
                if x < 32:
                    qb, h = x // 8, x % 8
                    w = P * (qb + 1)
                    if x >= 2:
                        pool.wait_ge(s["scores_biased"], x - 1)
                    if x % 8 == 0 and qb:
                        pool.wait_ge(s["prompt_selected"], qb)
                    pool.tensor_tensor(tbm[:, x % 2, 0:w], tb[:, h, SEQ - w:SEQ], caus[:] if qb == 0 else selq[qb], ALU.add).then_inc(s["tbm_done"], 1)
                if x > 16 and x % 2 == 0:
                    i = x // 2 - 1 - DK
                    n = first_tile["glu"] + i
                    pool.wait_ge(s["evac"], EV0 + n + 1)
                    pool.tensor_tensor(mixed[:, i, :], mixed[:, i, :], sg[:, n % 2, :], ALU.mult).then_inc(s["val_gated"], 1)
                    pool.wait_ge(s["val_gated"], i + 1)
                    pool.tensor_tensor(mixed[:, i, :], mixed[:, i, :], val[:, n % 2, :], ALU.mult).then_inc(s["pool_gated"], 1)
            pool.wait_ge(s["mm_done"], MM0 + ALLT)
            page_loads(pool, 2)
            norm_low(1)

        @block.vector
        def _(dve):
            count = [0]

            def link(*steps):
                for ins in steps:
                    count[0] += 1
                    ins.then_inc(s["dve_step"], 1)
                dve.wait_ge(s["dve_step"], count[0])

            def tt(o, a, b, op):
                return dve.tensor_tensor(o, a, b, op)

            def norm(k):
                dve.wait_ge(s["sqrt_done"], k + 1)
                link(dve.reciprocal(rstd[:], rstd[:]))
                for j in range(DK):
                    if k % 2:
                        tt(hn[:, j, :], hT[:, j, :], rstd[:], ALU.mult).then_inc(s["scaled"], 1)
                        continue
                    dve.scalar_tensor_tensor(out=nrm[:, j, :], in0=hT[:, j, :], scalar=gains[:, k, j:j + 1], in1=rstd[:],
                                             op0=ALU.mult, op1=ALU.mult).then_inc(s["nrm_done"], 1)
                    if j % 2:
                        low_part(k // 2, j - 1)

            def low_part(which, j):
                dve.wait_ge(s["hnh_done"], DK * which + j + 1)
                tt(hnl[:, j, :], nrm[:, j, :], hnh[:, j, :].bitcast(F32), ALU.subtract).then_inc(s["norm_even"], 1)

            def add_square(k, j):
                dve.wait_ge(s["sq_done"], DK * k + j + 1)
                if j:
                    if j > 1:
                        dve.wait_ge(s["sum_done"], (DK - 1) * k + j - 1)
                    tt(rstd[:], hn[:, 0, :] if j == 1 else rstd[:], hn[:, j, :], ALU.add).then_inc(s["sum_done"], 1)

            def low(u, i, j):
                dve.wait_ge(s["hi_done"], i * 4 + (u + 1))
                tt(wl[:, j % 2, :, :], wraw[:, j, :, :], wh[:, j % 2, :, :].bitcast(F32), ALU.subtract).then_inc(s["lo_done"], 1)

            def first_units(which):
                for j in range(2):
                    low(FIRST_UNIT[which] + j, 0, j)

            def ffn(which, between=()):
                between = list(between)
                end = FIRST_UNIT[which] + FFN_UNITS

                def in_tile(i, j, u0, t0, a0):
                    for k in range(2):
                        low(u0 + 2 * j + k + 2, i, (2 * j + k + 2) % 4)
                    dve.wait_ge(s["silu_done"], i * 2 + (a0 + j + 1))
                    dve.wait_ge(s["unit_done"], i * 4 + (u0 + 2 * j + 2))
                    tt(two(sg[:, j, :]), two(sg[:, j, :]), pair(j, 1), ALU.mult).then_inc(s["ffn_ev"], 1)
                    dve.wait_ge(s["acth_done"], i * 2 + (a0 + j + 1))
                    tt(one(actl, i * 2 + j), sg[:, j, :], one(acth, i * 2 + j).bitcast(F32), ALU.subtract).then_inc(s["act_ready"], 1)

                def out_tile(i, j, u0, split):
                    dve.wait_ge(s["unit_done"], i * 4 + (u0 + j + 1))
                    h = two(one(hT, i * 4 + j))
                    dve.scalar_tensor_tensor(out=h, in0=pair(j % 2, 0), scalar=0.5, in1=h, op0=ALU.mult, op1=ALU.add).then_inc(s["ffn_ev"], 1)
                    if split:
                        low(u0 + j + 2, i, (j + 2) % 4)

                for kind, f0, m, u0, t0, a0 in ffn_plan(which):
                    if kind == "in":
                        with dve.Fori(0, m // 2) as i:
                            for j in range(2):
                                in_tile(i, j, u0, t0, a0)
                        if between:
                            between.pop(0)()
                    elif u0 + DK < end:
                        dve.wait_ge(s["ffn_ev"], FE0 + t0)
                        with dve.Fori(0, 2) as i:
                            for j in range(4):
                                out_tile(i, j, u0, True)
                        if between:
                            between.pop(0)()
                    else:
                        dve.wait_ge(s["ffn_ev"], FE0 + t0)
                        for k in range(DK):
                            out_tile(k // 4, k % 4, u0, k < DK - 2)
                            if k:
                                add_square(2 * which + 1, k - 1)
                        add_square(2 * which + 1, DK - 1)

            def pair(half, o):
                return ps[:, 4 * half + 2 * o:4 * half + 2 * o + 2, 0:HALF]

            def two(ap):
                return ap.rearrange("p (h n) -> p h n", h=2)

            dve.sem_inc(s["lo_done"], FE0)
            dve.sem_inc(s["ffn_ev"], FE0)
            dve.sem_inc(s["act_ready"], FE0)
            dve.sem_inc(s["kv_used"], 4)
            for k in range(DK):
                dve.wait_ge(s["mm_done"], k + 1)
                dve.tensor_copy(hT[:, k, 0:SEQ], ps[:, 4 * (k % 2), :])
                dve.tensor_copy(hT[:, k, SEQ:NT], ps[:, 4 * (k % 2) + 1, 0:32]).then_inc(s["evac"], 1)
                if k:
                    add_square(0, k - 1)
            add_square(0, DK - 1)
            first_units(0)
            dve.wait_ge(s["const_in"], 16 * 4)
            norm(0)
            dve.wait_ge(s["dt_done"], 1)
            dve.wait_ge(s["par_in"], 16 * 13)
            lr, li = lam[:, 0, :], lam[:, 1, :]
            TWO_PI_HI = 6.28125
            TWO_PI_LO = 2 * math.pi - TWO_PI_HI
            ROUND = 12582912.0
            link(tt(v(1), lr, ldt, ALU.mult), tt(v(2), li, ldt, ALU.mult))
            link(dve.tensor_scalar(v(5), v(2), 1 / (2 * math.pi), ROUND, ALU.mult, ALU.add))
            link(dve.tensor_scalar(v(5), v(5), -ROUND, None, ALU.add))
            link(dve.scalar_tensor_tensor(out=v(2), in0=v(5), scalar=-TWO_PI_HI, in1=v(2), op0=ALU.mult, op1=ALU.add))
            link(dve.scalar_tensor_tensor(out=v(2), in0=v(5), scalar=-TWO_PI_LO, in1=v(2), op0=ALU.mult, op1=ALU.add))
            link(dve.tensor_scalar(v(2), v(2), 3.1415925, -3.1415925, ALU.min, ALU.max))
            dve.sem_inc(s["ang_done"], 1)
            link(tt(v(9), lr, lr, ALU.mult), tt(v(10), li, li, ALU.mult))
            link(tt(v(9), v(9), v(10), ALU.add))
            link(dve.reciprocal(v(9), v(9)))
            dve.wait_ge(s["trig_done"], 3)
            link(tt(v(8), v(8), v(8), ALU.mult))
            link(dve.tensor_scalar(v(8), v(8), -2.0, 1.0, ALU.mult, ALU.add))
            link(dve.memset(apow[:, 0, 0, :], 1.0), dve.memset(apow[:, 0, 1, :], 0.0),
                 tt(apow[:, 1, 0, :], v(4), v(8), ALU.mult), tt(apow[:, 1, 1, :], v(4), v(7), ALU.mult))
            ar, ai = apow[:, 1, 0, :], apow[:, 1, 1, :]
            link(dve.tensor_scalar(v(10), ar, -1.0, None, ALU.add))
            link(tt(v(11), v(10), lr, ALU.mult), tt(v(12), ai, li, ALU.mult), tt(v(13), ai, lr, ALU.mult), tt(v(14), v(10), li, ALU.mult))
            link(tt(v(11), v(11), v(12), ALU.add), tt(v(13), v(13), v(14), ALU.subtract))
            link(tt(v(11), v(11), v(9), ALU.mult), tt(v(13), v(13), v(9), ALU.mult))

            def powers(arr):
                for m in (1, 2, 4):
                    def bc(c):
                        return arr[:, m, c, :].unsqueeze(1).broadcast_to([P, m, GP])
                    lo = [arr[:, 1:m + 1, c, :] for c in range(2)]
                    hi = [arr[:, m + 1:2 * m + 1, c, :] for c in range(2)]
                    p4 = [s5q[:, k, 0:m, :] for k in range(4)]
                    link(tt(p4[0], lo[0], bc(0), ALU.mult), tt(p4[1], lo[1], bc(1), ALU.mult),
                         tt(p4[2], lo[0], bc(1), ALU.mult), tt(p4[3], lo[1], bc(0), ALU.mult))
                    link(tt(hi[0], p4[0], p4[1], ALU.subtract), tt(hi[1], p4[2], p4[3], ALU.add))
            def more_powers():
                link(dve.tensor_copy(cpow[:, 1], apow[:, 8]))
                powers(cpow)

            def scaled_b():
                def zb(k):
                    return v(k).unsqueeze(2).broadcast_to([P, GP, GC])
                link(tt(pt1, bmat[:, 0], zb(11), ALU.mult), tt(pt2, bmat[:, 1], zb(13), ALU.mult),
                     tt(pt3, bmat[:, 1], zb(11), ALU.mult), tt(pt4, bmat[:, 0], zb(13), ALU.mult))
                link(tt(bbar[:, 0], pt1, pt2, ALU.subtract), tt(bbar[:, 1], pt3, pt4, ALU.add))
                dve.sem_inc(s["pow_done"], 1)
                link(tt(dd, dd, ident[0:GC, 0:GC].unsqueeze(1).broadcast_to([GC, G, GC]), ALU.mult))
            dve.wait_ge(s["shift_out"], 16)
            ffn(0, [lambda: powers(apow), more_powers, scaled_b])
            norm(1)
            n = first_tile["idx"]
            b = 4 * (n % 2)
            dve.wait_ge(s["mm_done"], MM0 + n + 1)
            dve.tensor_copy(qiT[:, 0:2, :], ps[:, b:b + 2, :])
            W_SCALE = ID ** -0.5 * IH ** -0.5
            for tt_ in range(5):
                m = P if tt_ < 4 else 32
                c0 = 40 * tt_
                dve.tensor_copy(ki4[0:m, tt_, :, :], ps[0:m, b + 2, c0:c0 + ID].unsqueeze(1).broadcast_to([m, 4, ID]))
                if tt_ < 4:
                    dve.tensor_scalar(wtok[:, tt_, :], ps[:, b + 2, c0 + ID:c0 + ID + IH], W_SCALE, None, ALU.mult)
            dve.tensor_copy(qis4, ps[0:32, b + 3, 0:256].rearrange("p (h d) -> p h d", h=IH).unsqueeze(2).broadcast_to([32, IH, 4, ID]))
            dve.tensor_scalar(wT8, ps[0:8, b + 3, 256:288], W_SCALE, None, ALU.mult).then_inc(s["evac"], 1)
            for r in range(4):
                dve.wait_ge(s["lag_kernels"], r + 1)
                for h in range(2):
                    ins = dve.tensor_copy(kbuf[r].rearrange("p (g s) n -> p g s n", s=2)[:, :, h, :],
                                          ps[0:16, 4 + 2 * (r % 2) + h, :].rearrange("p (g n) -> p g n", g=4))
                link(ins)
                dve.tensor_tensor(kbuf[r][:, :, 0:GC], kbuf[r][:, :, 0:GC], dd[:, 8 * r:8 * r + 8, :], ALU.add).then_inc(s["lag_kernels_out"], 1)
            dve.wait_ge(s["index_keys_turned"], 1)
            dve.tensor_copy(kiT[:, 0:SEQ], ps[:, 4, :])
            dve.tensor_copy(kiT[:, SEQ:NT], ps[:, 5, 0:32]).then_inc(s["index_keys_out"], 1)
            dve.wait_ge(s["index_keys_turned"], 2)
            dve.tensor_copy(qis[:].rearrange("p b h q -> p h b q"), ps[:, 6, 0:256].rearrange("p (h b q) -> p h b q", h=IH, b=NB)).then_inc(s["index_keys_out"], 1)

            topk_n = [0]

            def top(scores, rounds):
                n0 = topk_n[0]
                with dve.Fori(0, rounds) as i:
                    dve.max(out=top8[0:scores.shape[0], :], in_=scores).then_inc(s["topk_step"], 1)
                    dve.wait_ge(s["topk_step"], i * 2 + (n0 + 1))
                    dve.tensor_copy(topwait, top8[:, 0:1])
                    dve.match_replace(out=scores, in_to_replace=top8[0:scores.shape[0], :], in_values=scores, imm_value=TAKEN).then_inc(s["topk_step"], 1)
                    dve.wait_ge(s["topk_step"], i * 2 + (n0 + 2))
                topk_n[0] += 2 * rounds
            dve.wait_ge(s["caus_in"], 16)
            for x in range(24):
                qb, h = 1 + x // 8, x % 8
                w = P * (qb + 1)
                dve.wait_ge(s["relu_done"], x + 1)
                if h == 0:
                    dve.tensor_scalar(sc[:, 0:w], rl[:, x % 2, 0:w], wtok[:, qb, 0:1], None, ALU.mult).then_inc(s["index_added"], 1)
                else:
                    dve.wait_ge(s["index_added"], x)
                    dve.scalar_tensor_tensor(out=sc[:, 0:w], in0=rl[:, x % 2, 0:w], scalar=wtok[:, qb, h:h + 1], in1=sc[:, 0:w],
                                             op0=ALU.mult, op1=ALU.add).then_inc(s["index_added"], 1)
                if h == 7:
                    dve.wait_ge(s["index_added"], x + 1)
                    link(tt(sc[:, w - P:w], sc[:, w - P:w], caus[:], ALU.add))
                    top(sc[:, 0:w], TOPK_P // 8)
                    dve.tensor_scalar(selq[qb], sc[:, 0:w], 0.5 * TAKEN, MASK, ALU.is_ge, ALU.mult).then_inc(s["prompt_selected"], 1)
                    dve.wait_ge(s["prompt_selected"], qb)

            dve.wait_ge(s["evac"], EV0 + first_tile["kv"])
            link(dve.memset(qbd[:].rearrange("p j b r -> p (j b r)"), 0.0))
            for j in range(4):
                for h in range(2):
                    sl = slice(64 * h, 64 * h + 64)
                    hh = 2 * j + h
                    ins = dve.tensor_copy(qbd[sl, j, :, NS * hh:NS * hh + NS], qT[sl, j, SEQ:NT].rearrange("p (b q) -> p b q", b=NB))
            link(ins)
            dve.wait_ge(s["sample_const_in"], 16 * 12)
            tt(rbexp.rearrange("p (b h q) -> p b h q", b=4, h=HEADS), same_step.rearrange("p (b h q) -> p b h q", b=4, h=HEADS),
               rb4.unsqueeze(1).unsqueeze(3).broadcast_to([P, 4, HEADS, NS]), ALU.mult)
            link(dve.tensor_copy(tok_row, tok_row_f))
            dve.sem_inc(s["sample_prep"], 1)
            dve.wait_ge(s["head_weights"], 1)
            for g in range(2):
                ins = tt(wsel[:, g, :], ps[:, 3, 0:32], row_tok[:, g, :], ALU.mult)
            link(ins)
            dve.sem_inc(s["head_weights_out"], 1)
            for both in range(NB // 2):
                dve.wait_ge(s["pages_turned"], both + 1)
                if both >= 2:
                    dve.wait_ge(s["sample_logits"], 2 * both - 2)
                dve.tensor_copy(kxT[:, both % 2, :], ps[:, 4, :]).then_inc(s["pages_out"], 1)
            dve.wait_ge(s["sample_index"], 2)
            link(dve.tensor_copy(scs[:, 0:PAST].rearrange("p (b n) -> p b n", b=2), ps[0:32, 5:7, :]),
                 tt(scs[:, PAST:NKEY], ps[0:32, 7, 0:32], new_mask, ALU.add))
            dve.sem_inc(s["sample_index_out"], 1)
            assert TOPK_S // 8 == 32
            n_top = topk_n[0]
            for x in range(34):
                if x < 32:
                    qb, h = x // 8, x % 8
                    w = P * (qb + 1)
                    dve.wait_ge(s["scores_ready"], x + 1)
                    dve.wait_ge(s["tbm_done"], x + 1)
                    if x >= 2:
                        dve.wait_ge(s["probs_ready"], x - 1)
                    dve.tensor_tensor_reduce(smx[:, x % 2, 0:w], ps[:, 2, 0:w], tbm[:, x % 2, 0:w], -1.0, 3e38,
                                             ALU.add, ALU.min, nmx[:, x % 2:x % 2 + 1]).then_inc(s["scores_biased"], 1)
                    dve.max(out=top8[0:32, :], in_=scs).then_inc(s["topk_step"], 1)
                    dve.wait_ge(s["topk_step"], n_top + 2 * x + 1)
                    dve.match_replace(out=scs, in_to_replace=top8[0:32, :], in_values=scs, imm_value=TAKEN).then_inc(s["topk_step"], 1)
                    dve.wait_ge(s["topk_step"], n_top + 2 * x + 2)
                if x >= 2 and (x - 2) % 8 == 7:
                    qb = (x - 2) // 8
                    dve.wait_ge(s["values_ready"], x - 1)
                    dve.wait_ge(s["probs_ready"], 8 * qb + 8)
                    link(dve.reciprocal(rinv[:, qb % 2, :], rsum[:, qb % 2, :]))
                    if qb >= 2:
                        dve.wait_ge(s["att_turned"], qb - 1)
                    tt(ao[:, qb % 2, :].rearrange("p (h d) -> p h d", h=HEADS), ps[:, 6, :].rearrange("p (h d) -> p h d", h=HEADS),
                       rinv[:, qb % 2, :].unsqueeze(2).broadcast_to([P, HEADS, HD]), ALU.mult).then_inc(s["att_scaled"], 1)
                    dve.wait_ge(s["att_turned"], qb + 1)
                    if qb == 0:
                        dve.wait_ge(s["kv_out"], 16 * 4)
                    dve.tensor_copy(attT[:, :, P * qb:P * qb + P], ps[:, 7, :].rearrange("p (j n) -> p j n", j=4)).then_inc(s["att_out"], 1)
            dve.tensor_scalar(sels, scs, 0.5 * TAKEN, MASK, ALU.is_ge, ALU.mult).then_inc(s["sample_selected"], 1)
            dve.wait_ge(s["sample_bias"], 1)
            dve.tensor_copy(bs[:, 0:PAST].rearrange("p (b n) -> p b n", b=2), ps[:, 0:2, :])
            dve.tensor_copy(bs[:, PAST:NKEY], ps[:, 2, 0:32]).then_inc(s["sample_bias_out"], 1)
            dve.wait_ge(s["pool_gated"], 2 + 8)

            for g in range(2):
                for i in range(8):
                    n = 8 * g + i
                    dve.wait_ge(s["k_turned"], 4 * n + 4)
                    dve.sem_inc(s["kv_used"], 1)
                    if n >= 2:
                        dve.wait_ge(s["k_scored"], n - 1)
                    dve.tensor_copy(pgT[:, n % 2, 2:4, :], ps[:, 5:7, :]).then_inc(s["k_out_dve"], 1)
                dve.wait_ge(s["sample_scores"], g + 1)
                if g:
                    dve.wait_ge(s["sample_exp"], g)
                dve.tensor_tensor_reduce(sms, ps[:, 0:3, :].rearrange("p b n -> p (b n)")[:, 0:NKEY], bs, -1.0, 3e38,
                                         ALU.add, ALU.min, nmx[:, g:g + 1]).then_inc(s["sample_biased"], 1)
                dve.wait_ge(s["sample_exp"], g + 1)
                link(dve.reciprocal(rinv[:, 0, g:g + 1], rsum[:, 0, g:g + 1]))
                link(dve.tensor_scalar(hmr[:, g, :], row_head, rinv[:, 0, g:g + 1], None, ALU.mult))
                dve.wait_ge(s["sample_values"], g + 1)
                tt(osel[:, g, :].rearrange("p (h d) -> p h d", h=HEADS), ps[:, 5, :].rearrange("p (h d) -> p h d", h=HEADS),
                   hmr[:, g, :].unsqueeze(2).broadcast_to([P, HEADS, HD]), ALU.mult).then_inc(s["sample_values_out"], 1)
            dve.wait_ge(s["sample_att_turned"], 1)
            dve.tensor_copy(attT[:, :, SEQ:NT], ps[:, 6, 0:128].rearrange("p (j n) -> p j n", j=4)).then_inc(s["sample_att_out"], 1)

            def mix_low(i):
                dve.wait_ge(s["mixh_done"], i + 1)
                tt(actl[:, mix_low_at(i), :], fin_mix[:, i % 2, :], acth[:, i, :].bitcast(F32), ALU.subtract).then_inc(s["mix_ready"], 1)

            for i in range(DK):
                half = i % 2
                dve.wait_ge(s["att_mm"], i + 1)
                dve.wait_ge(s["ga_ev"], 16)
                tt(two(sg[:, half, :]), pair(half, 0), two(ga_s[i]), ALU.mult).then_inc(s["att_ev"], 1)
                dve.wait_ge(s["att_ev"], i + 1)
                if i >= 2:
                    dve.wait_ge(s["mixh_done"], i - 1)
                tt(fin_mix[:, i % 2, :], mixed[:, i, :], sg[:, half, :], ALU.add).then_inc(s["mix_done"], 1)
                if i:
                    mix_low(i - 1)
            for j in range(2):
                low(FFN_UNITS + j, 0, j)
            mix_low(DK - 1)
            for i in range(DK):
                dve.wait_ge(s["unit_done"], FFN_UNITS + i + 1)
                tt(two(hT[:, i, :]), pair(i % 2, 0), two(hT[:, i, :]), ALU.add).then_inc(s["ffn_ev"], 1)
                low(FFN_UNITS + 2 + i, 0, (i + 2) % 4)
                if i:
                    add_square(2, i - 1)
            add_square(2, DK - 1)
            norm(2)
            ffn(1)
            norm(3)
            for k in range(5):
                m = P if k < 4 else 32
                bk = 2 + 2 * (k % 2)
                dve.wait_ge(s["final_turned"], k + 1)
                dve.tensor_copy(ytok[0:m, k, :].rearrange("p (b n) -> p b n", b=2), ps[0:m, bk:bk + 2, :]).then_inc(s["final_out"], 1)


INPUTS = ["x_prompt", "x_sample", "cache_k", "cache_v", "cache_kidx", "state_s5_re", "state_s5_im", "page_table",
          "g_ffn1", "w_ffn1_in", "w_ffn1_out", "g_mix", "w_in", "s5_lam_re", "s5_lam_im", "s5_log_dt",
          "s5_b_re", "s5_b_im", "s5_c_re", "s5_c_im", "s5_d", "w_s5_glu", "w_att_proj", "rel_bias", "w_out",
          "g_ffn2", "w_ffn2_in", "w_ffn2_out", "g_final"]
OUTPUTS = [("y_prompt", (1, SEQ, D)), ("y_sample", (NB, NS, D)),
           ("k_prompt", (1, 1, SEQ, HEADS, HD)), ("v_prompt", (1, 1, SEQ, HEADS, HD)), ("kidx_prompt", (1, 1, SEQ, ID)),
           ("s5_re_prompt", (1, 1, G, ST)), ("s5_im_prompt", (1, 1, G, ST)),
           ("k_sample", (1, NB, NS, HEADS, HD)), ("v_sample", (1, NB, NS, HEADS, HD)), ("kidx_sample", (1, NB, NS, ID)),
           ("s5_re_sample", (1, NB, G, ST)), ("s5_im_sample", (1, NB, G, ST))]


def kernel(**inputs):
    import concourse.bacc as _bacc
    from concourse.bass_utils import run_bass_kernel_spmd as _run

    nc = _bacc.Bacc("TRN2", target_bir_lowering=False, num_devices=1)
    arrays, t, out = {}, {}, {}
    data = {n: np.ascontiguousarray(inputs[n]) for n in INPUTS}
    data.update(shape_constants())
    for n, a in data.items():
        arrays["in_" + n] = a
        t[n] = nc.dram_tensor("in_" + n, a.shape, mybir.dt.from_np(a.dtype), kind="ExternalInput").ap()
    for n, shape in OUTPUTS:
        out[n] = nc.dram_tensor("out_" + n, shape, F32, kind="ExternalOutput").ap()
    build(nc, t, out)
    r = _run(nc, [arrays], core_ids=[0])
    return tuple(r.results[0]["out_" + n] for n, _ in OUTPUTS)
```
